# Optimizing a Trainium2 kernel written in Bass

```python
import math
import jax, jax.numpy as jnp
from jax import lax
import numpy as np

D_MODEL = 2048
BATCH = 1
SEQ = 256
DEPTH = 2
DEC_BATCH = 8
DEC_SEQ = 1
PAST_LEN = 2048
PAGE_SIZE = 128

MIX_GROUP = D_MODEL // 4
D_FF = 4 * D_MODEL
EPS = 1e-6
CONV_W = 4

GLA_HEADS = 4
GLA_DV = MIX_GROUP // GLA_HEADS
GLA_DK = GLA_DV // 2
GLA_RANK = 16
GLA_GATE_TEMP = 16.0
GLA_CHUNK = 16

LRU_WIDTH = MIX_GROUP
LRU_BLOCKS = 8
LRU_BLOCK = LRU_WIDTH // LRU_BLOCKS
LRU_C = 8.0

RWKV_HEAD = 64
RWKV_HEADS = MIX_GROUP // RWKV_HEAD
RWKV_W_RANK = 64
RWKV_A_RANK = 64
RWKV_G_RANK = 128
RWKV_DECAY_SCALE = math.exp(-0.5)
RWKV_LN_EPS = 64e-5

SSD_HEADDIM = 64
SSD_HEADS = MIX_GROUP // SSD_HEADDIM
SSD_GROUPS = 2
SSD_STATE = 128
SSD_CHUNK = 64
SSD_CONV_DIM = MIX_GROUP + 2 * SSD_GROUPS * SSD_STATE

GLA_COLS = 2 * GLA_HEADS * GLA_DK + 2 * MIX_GROUP + GLA_RANK
LRU_COLS = 2 * LRU_WIDTH
RWKV_COLS = 3 * MIX_GROUP + RWKV_W_RANK + RWKV_A_RANK + RWKV_G_RANK
SSD_COLS = MIX_GROUP + SSD_CONV_DIM + SSD_HEADS
PROJ_COLS = GLA_COLS + LRU_COLS + RWKV_COLS + SSD_COLS
SPLIT_IDX = (GLA_COLS, GLA_COLS + LRU_COLS, GLA_COLS + LRU_COLS + RWKV_COLS)

kernel_name = 'hybrid_gla_hawk_rwkv7_ssd_step'

F32 = jnp.float32

def rmsnorm(x, w):
    xf = x.astype(F32)
    y = xf * lax.rsqrt(jnp.mean(xf * xf, axis=-1, keepdims=True) + EPS)
    return (y * w.astype(F32)).astype(x.dtype)

def causal_conv(x, buf, w, b):
    T = x.shape[1]
    xp = jnp.concatenate([buf.astype(x.dtype), x], axis=1)
    y = b
    for i in range(CONV_W):
        y = y + xp[:, i:i + T] * w[i]
    return y, xp[:, T:]

def gla_chunked(q, k, v, g, s0):
    B, T, H, K = q.shape
    V = v.shape[-1]
    C = math.gcd(T, GLA_CHUNK)
    N = T // C
    q, k, g = (t.reshape(B, N, C, H, K) for t in (q, k, g))
    v = v.reshape(B, N, C, H, V)
    cum = jnp.cumsum(g, axis=2)
    mask = jnp.tril(jnp.ones((C, C), bool))[:, :, None, None]
    diff = cum[:, :, :, None] - cum[:, :, None, :]
    decay = jnp.exp(jnp.where(mask, diff, -jnp.inf))
    scores = jnp.einsum('bnlhk,bnshk,bnlshk->bnhls', q, k, decay)
    y_intra = jnp.einsum('bnhls,bnshv->bnlhv', scores, v)
    last = cum[:, :, -1]
    k_dec = k * jnp.exp(last[:, :, None] - cum)
    chunk_states = jnp.einsum('bnshk,bnshv->bnhkv', k_dec, v)

    def step(s, inp):
        dec, cs = inp
        return s * dec[..., None] + cs, s

    s_final, s_prev = lax.scan(step, s0.astype(F32),
                               (jnp.moveaxis(jnp.exp(last), 1, 0), jnp.moveaxis(chunk_states, 1, 0)))
    s_prev = jnp.moveaxis(s_prev, 0, 1)
    y_inter = jnp.einsum('bnlhk,bnhkv->bnlhv', q * jnp.exp(cum), s_prev)
    return (y_intra + y_inter).reshape(B, T, H, V), s_final

def rg_lru(x, gate_a, gate_i, lam, h0, fresh):
    log_a = -LRU_C * gate_a * jax.nn.softplus(-lam)
    a = jnp.exp(log_a)
    mult = jnp.sqrt(-jnp.expm1(2.0 * log_a))
    if fresh:
        mult = mult.at[:, 0].set(1.0)
    b = mult * gate_i * x
    b = b.at[:, 0].add(a[:, 0] * h0.astype(F32))

    def combine(left, right):
        a1, b1 = left
        a2, b2 = right
        return a1 * a2, a2 * b1 + b2

    _, h = lax.associative_scan(combine, (a, b), axis=1)
    return h, h[:, -1]

def rwkv7_scan(r, w, k, v, kk, a, s0):
    def step(s, inp):
        r_t, w_t, k_t, v_t, kk_t, a_t = inp
        sa = jnp.einsum('bhvk,bhk->bhv', s, kk_t)
        s = (s * w_t[:, :, None, :] - sa[..., None] * (kk_t * a_t)[:, :, None, :]
             + v_t[..., None] * k_t[:, :, None, :])
        return s, jnp.einsum('bhvk,bhk->bhv', s, r_t)

    xs = tuple(jnp.moveaxis(t, 1, 0) for t in (r, w, k, v, kk, a))
    s_final, y = lax.scan(step, s0.astype(F32), xs)
    return jnp.moveaxis(y, 0, 1), s_final

def ssd_chunked(x, dt, a_neg, bm, cm, s0):
    B, T, H, P = x.shape
    N = bm.shape[-1]
    C = math.gcd(T, SSD_CHUNK)
    NC = T // C
    rep = H // bm.shape[2]
    bh = jnp.repeat(bm, rep, axis=2).reshape(B, NC, C, H, N)
    ch = jnp.repeat(cm, rep, axis=2).reshape(B, NC, C, H, N)
    xdt = (x * dt[..., None]).reshape(B, NC, C, H, P)
    cum = jnp.cumsum((dt * a_neg).reshape(B, NC, C, H), axis=2)
    mask = jnp.tril(jnp.ones((C, C), bool))[:, :, None]
    seg = cum[:, :, :, None, :] - cum[:, :, None, :, :]
    Lmat = jnp.exp(jnp.where(mask, seg, -jnp.inf))
    scores = jnp.einsum('bclhn,bcshn->bclsh', ch, bh) * Lmat
    y_diag = jnp.einsum('bclsh,bcshp->bclhp', scores, xdt)
    last = cum[:, :, -1]
    states = jnp.einsum('bcshn,bcsh,bcshp->bchpn', bh, jnp.exp(last[:, :, None] - cum), xdt)

    def step(s, inp):
        dec, cs = inp
        return s * dec[..., None, None] + cs, s

    s_final, s_prev = lax.scan(step, s0.astype(F32),
                               (jnp.moveaxis(jnp.exp(last), 1, 0), jnp.moveaxis(states, 1, 0)))
    s_prev = jnp.moveaxis(s_prev, 0, 1)
    y_off = jnp.einsum('bclhn,bchpn,bclh->bclhp', ch, s_prev, jnp.exp(cum))
    return (y_diag + y_off).reshape(B, T, H, P), s_final

def gla_mixer(z, s0, w_gate2, b_gate, norm_w):
    B, T, _ = z.shape
    qk = GLA_HEADS * GLA_DK
    q, k, v, gate, a_down = jnp.split(z.astype(F32), [qk, 2 * qk, 2 * qk + MIX_GROUP, 2 * qk + 2 * MIX_GROUP], axis=-1)
    log_alpha = jax.nn.log_sigmoid(jnp.einsum('btr,rc->btc', a_down, w_gate2) + b_gate) / GLA_GATE_TEMP
    q = q.reshape(B, T, GLA_HEADS, GLA_DK) * (GLA_DK ** -0.5)
    k = k.reshape(B, T, GLA_HEADS, GLA_DK)
    v = v.reshape(B, T, GLA_HEADS, GLA_DV)
    log_alpha = log_alpha.reshape(B, T, GLA_HEADS, GLA_DK)
    o, s = gla_chunked(q, k, v, log_alpha, s0)
    o = rmsnorm(o, norm_w).reshape(B, T, MIX_GROUP)
    return (o * jax.nn.silu(gate)).astype(z.dtype), s

def hawk_mixer(z, h0, conv_buf, conv_w, conv_b, w_a, b_a, w_i, b_i, lam, fresh):
    B, T, _ = z.shape
    xb, gb = jnp.split(z, 2, axis=-1)
    xc, new_buf = causal_conv(xb, conv_buf, conv_w, conv_b)
    xc = xc.astype(F32)
    blk = xc.reshape(B, T, LRU_BLOCKS, LRU_BLOCK)
    r = jax.nn.sigmoid(jnp.einsum('btgi,gij->btgj', blk, w_a).reshape(B, T, LRU_WIDTH) + b_a)
    i = jax.nn.sigmoid(jnp.einsum('btgi,gij->btgj', blk, w_i).reshape(B, T, LRU_WIDTH) + b_i)
    h, h_last = rg_lru(xc, r, i, lam, h0, fresh)
    y = h * jax.nn.gelu(gb.astype(F32))
    return y.astype(z.dtype), h_last, new_buf

def rwkv_mixer(z, prev, s0, mu, w0, w2, a0, a2, g2, k_k, k_a, r_k, ln_w, ln_b):
    B, T, _ = z.shape
    zf = z.astype(F32)
    shifted = jnp.concatenate([prev[:, None].astype(F32), zf[:, :-1]], axis=1)
    zm = zf + (shifted - zf) * mu
    r, k, v, zw, za, zg = jnp.split(zm, [MIX_GROUP, 2 * MIX_GROUP, 3 * MIX_GROUP,
                                         3 * MIX_GROUP + RWKV_W_RANK,
                                         3 * MIX_GROUP + RWKV_W_RANK + RWKV_A_RANK], axis=-1)
    w = jnp.exp(-RWKV_DECAY_SCALE * jax.nn.sigmoid(w0 + jnp.einsum('btr,rc->btc', jnp.tanh(zw), w2)))
    a = jax.nn.sigmoid(a0 + jnp.einsum('btr,rc->btc', za, a2))
    g = jnp.einsum('btr,rc->btc', jax.nn.sigmoid(zg), g2)
    heads = lambda t: t.reshape(B, T, RWKV_HEADS, RWKV_HEAD)
    kk = heads(k * k_k)
    kk = kk / jnp.maximum(jnp.sqrt(jnp.sum(kk * kk, axis=-1, keepdims=True)), 1e-12)
    k = k * (1.0 + (a - 1.0) * k_a)
    rh, kh, vh, wh, ah = heads(r), heads(k), heads(v), heads(w), heads(a)
    y, s = rwkv7_scan(rh, wh, kh, vh, kk, ah, s0)
    mean = jnp.mean(y, axis=-1, keepdims=True)
    var = jnp.mean(jnp.square(y - mean), axis=-1, keepdims=True)
    yn = ((y - mean) * lax.rsqrt(var + RWKV_LN_EPS)).reshape(B, T, MIX_GROUP) * ln_w + ln_b
    bonus = (jnp.sum(rh * kh * r_k, axis=-1, keepdims=True) * vh).reshape(B, T, MIX_GROUP)
    out = (yn + bonus) * g
    return out.astype(z.dtype), s, z[:, -1]

def ssd_mixer(z, conv_buf, s0, conv_w, conv_b, dt_bias, a_log, d_skip, norm_w):
    B, T, _ = z.shape
    gate, xbc, dt_raw = jnp.split(z, [MIX_GROUP, MIX_GROUP + SSD_CONV_DIM], axis=-1)
    xbc_c, new_buf = causal_conv(xbc, conv_buf, conv_w, conv_b)
    xbc_c = jax.nn.silu(xbc_c.astype(F32))
    xs, bm, cm = jnp.split(xbc_c, [MIX_GROUP, MIX_GROUP + SSD_GROUPS * SSD_STATE], axis=-1)
    dt = jax.nn.softplus(dt_raw.astype(F32) + dt_bias)
    a_neg = -jnp.exp(a_log.astype(F32))
    xh = xs.reshape(B, T, SSD_HEADS, SSD_HEADDIM)
    y, s = ssd_chunked(xh, dt, a_neg, bm.reshape(B, T, SSD_GROUPS, SSD_STATE),
                       cm.reshape(B, T, SSD_GROUPS, SSD_STATE), s0)
    y = y + d_skip[:, None] * xh
    y = y.reshape(B, T, MIX_GROUP) * jax.nn.silu(gate.astype(F32))
    return rmsnorm(y, norm_w).astype(z.dtype), s, new_buf

def hybrid_layer(x, states, p, fresh):
    gla_s, lru_h, lru_buf, rwkv_prev, rwkv_s, ssd_buf, ssd_s = states
    h = rmsnorm(x, p['norm_mix_pre'])
    proj = jnp.einsum('btd,dc->btc', h, p['w_in'])
    z_gla, z_lru, z_rwkv, z_ssd = jnp.split(proj, SPLIT_IDX, axis=-1)
    o_gla, gla_s = gla_mixer(z_gla, gla_s, p['gla_w_gate2'], p['gla_b_gate'], p['gla_norm'])
    o_lru, lru_h, lru_buf = hawk_mixer(z_lru, lru_h, lru_buf, p['lru_conv_w'], p['lru_conv_b'],
                                       p['lru_w_a'], p['lru_b_a'], p['lru_w_i'], p['lru_b_i'],
                                       p['lru_lambda'], fresh)
    o_rwkv, rwkv_s, rwkv_prev = rwkv_mixer(z_rwkv, rwkv_prev, rwkv_s, p['rwkv_mu'], p['rwkv_w0'],
                                           p['rwkv_w2'], p['rwkv_a0'], p['rwkv_a2'], p['rwkv_g2'],
                                           p['rwkv_k_k'], p['rwkv_k_a'], p['rwkv_r_k'],
                                           p['rwkv_ln_w'], p['rwkv_ln_b'])
    o_ssd, ssd_s, ssd_buf = ssd_mixer(z_ssd, ssd_buf, ssd_s, p['ssd_conv_w'], p['ssd_conv_b'],
                                      p['ssd_dt_bias'], p['ssd_a_log'], p['ssd_d'], p['ssd_norm'])
    mix = jnp.concatenate([o_gla, o_lru, o_rwkv, o_ssd], axis=-1)
    x = x + rmsnorm(jnp.einsum('btm,md->btd', mix, p['w_out']), p['norm_mix_post'])
    h = rmsnorm(x, p['norm_mlp_pre'])
    u = jnp.square(jax.nn.relu(jnp.einsum('btd,df->btf', h, p['w_up'])))
    x = x + rmsnorm(jnp.einsum('btf,fd->btd', u, p['w_down']), p['norm_mlp_post'])
    return x, (gla_s, lru_h, lru_buf, rwkv_prev, rwkv_s, ssd_buf, ssd_s)

def zero_states(b, dtype):
    return (jnp.zeros((b, GLA_HEADS, GLA_DK, GLA_DV), F32),
            jnp.zeros((b, LRU_WIDTH), F32),
            jnp.zeros((b, CONV_W - 1, LRU_WIDTH), dtype),
            jnp.zeros((b, RWKV_COLS), dtype),
            jnp.zeros((b, RWKV_HEADS, RWKV_HEAD, RWKV_HEAD), F32),
            jnp.zeros((b, CONV_W - 1, SSD_CONV_DIM), dtype),
            jnp.zeros((b, SSD_HEADS, SSD_HEADDIM, SSD_STATE), F32))

def setup_inputs(seed: int = 0) -> dict:
    key = jax.random.key(seed)
    ks = iter(jax.random.split(key, 64))
    L = DEPTH

    def nrm(shape, s):
        return s * jax.random.normal(next(ks), shape, F32)

    def gain(shape):
        return 1.0 + nrm(shape, 0.05)

    lam_u = jax.random.uniform(next(ks), (L, LRU_WIDTH), F32, minval=0.9, maxval=0.999)
    dt0 = jnp.exp(jax.random.uniform(next(ks), (L, SSD_HEADS), F32,
                                     minval=math.log(1e-3), maxval=math.log(1e-1)))
    return {
        'x_prompt': nrm((BATCH, SEQ, D_MODEL), 1.0),
        'x_sample': nrm((DEC_BATCH, DEC_SEQ, D_MODEL), 1.0),
        'state_gla': nrm((L, DEC_BATCH, GLA_HEADS, GLA_DK, GLA_DV), 0.5),
        'state_lru': nrm((L, DEC_BATCH, LRU_WIDTH), 0.5),
        'cache_lru_conv': nrm((L, DEC_BATCH, CONV_W - 1, LRU_WIDTH), 1.0),
        'cache_rwkv_shift': nrm((L, DEC_BATCH, RWKV_COLS), 1.0),
        'state_rwkv': nrm((L, DEC_BATCH, RWKV_HEADS, RWKV_HEAD, RWKV_HEAD), 0.3),
        'cache_ssd_conv': nrm((L, DEC_BATCH, CONV_W - 1, SSD_CONV_DIM), 1.0),
        'state_ssd': nrm((L, DEC_BATCH, SSD_HEADS, SSD_HEADDIM, SSD_STATE), 0.1),
        'norm_mix_pre': gain((L, D_MODEL)),
        'norm_mix_post': gain((L, D_MODEL)),
        'norm_mlp_pre': gain((L, D_MODEL)),
        'norm_mlp_post': gain((L, D_MODEL)),
        'w_in': nrm((L, D_MODEL, PROJ_COLS), D_MODEL ** -0.5),
        'w_out': nrm((L, D_MODEL, D_MODEL), D_MODEL ** -0.5),
        'w_up': nrm((L, D_MODEL, D_FF), D_MODEL ** -0.5),
        'w_down': nrm((L, D_FF, D_MODEL), D_FF ** -0.5),
        'gla_w_gate2': nrm((L, GLA_RANK, GLA_HEADS * GLA_DK), GLA_RANK ** -0.5),
        'gla_b_gate': nrm((L, GLA_HEADS * GLA_DK), 0.1),
        'gla_norm': gain((L, GLA_DV)),
        'lru_conv_w': nrm((L, CONV_W, LRU_WIDTH), 0.5),
        'lru_conv_b': nrm((L, LRU_WIDTH), 0.01),
        'lru_w_a': nrm((L, LRU_BLOCKS, LRU_BLOCK, LRU_BLOCK), LRU_BLOCK ** -0.5),
        'lru_b_a': nrm((L, LRU_WIDTH), 0.01),
        'lru_w_i': nrm((L, LRU_BLOCKS, LRU_BLOCK, LRU_BLOCK), LRU_BLOCK ** -0.5),
        'lru_b_i': nrm((L, LRU_WIDTH), 0.01),
        'lru_lambda': jnp.log(lam_u) - jnp.log1p(-lam_u),
        'rwkv_mu': jax.random.uniform(next(ks), (L, RWKV_COLS), F32),
        'rwkv_w0': nrm((L, MIX_GROUP), 1.0),
        'rwkv_w2': nrm((L, RWKV_W_RANK, MIX_GROUP), 0.1),
        'rwkv_a0': nrm((L, MIX_GROUP), 0.1),
        'rwkv_a2': nrm((L, RWKV_A_RANK, MIX_GROUP), 0.1),
        'rwkv_g2': nrm((L, RWKV_G_RANK, MIX_GROUP), RWKV_G_RANK ** -0.5),
        'rwkv_k_k': 0.85 + nrm((L, MIX_GROUP), 0.05),
        'rwkv_k_a': 1.0 + nrm((L, MIX_GROUP), 0.1),
        'rwkv_r_k': nrm((L, RWKV_HEADS, RWKV_HEAD), 0.1),
        'rwkv_ln_w': gain((L, MIX_GROUP)),
        'rwkv_ln_b': nrm((L, MIX_GROUP), 0.01),
        'ssd_conv_w': nrm((L, CONV_W, SSD_CONV_DIM), 0.5),
        'ssd_conv_b': nrm((L, SSD_CONV_DIM), 0.01),
        'ssd_dt_bias': dt0 + jnp.log(-jnp.expm1(-dt0)),
        'ssd_a_log': jnp.log(jax.random.uniform(next(ks), (L, SSD_HEADS), F32, minval=1.0, maxval=16.0)),
        'ssd_d': 1.0 + nrm((L, SSD_HEADS), 0.1),
        'ssd_norm': gain((L, MIX_GROUP)),
    }

def reference(x_prompt, x_sample, state_gla, state_lru, cache_lru_conv, cache_rwkv_shift, state_rwkv,
              cache_ssd_conv, state_ssd, norm_mix_pre, norm_mix_post, norm_mlp_pre, norm_mlp_post,
              w_in, w_out, w_up, w_down, gla_w_gate2, gla_b_gate, gla_norm,
              lru_conv_w, lru_conv_b, lru_w_a, lru_b_a, lru_w_i, lru_b_i, lru_lambda,
              rwkv_mu, rwkv_w0, rwkv_w2, rwkv_a0, rwkv_a2, rwkv_g2, rwkv_k_k, rwkv_k_a, rwkv_r_k,
              rwkv_ln_w, rwkv_ln_b, ssd_conv_w, ssd_conv_b, ssd_dt_bias, ssd_a_log, ssd_d, ssd_norm):
    y_p, y_s = x_prompt, x_sample
    new_p, new_s = [], []
    for l in range(DEPTH):
        p = {'norm_mix_pre': norm_mix_pre[l], 'norm_mix_post': norm_mix_post[l],
             'norm_mlp_pre': norm_mlp_pre[l], 'norm_mlp_post': norm_mlp_post[l],
             'w_in': w_in[l], 'w_out': w_out[l], 'w_up': w_up[l], 'w_down': w_down[l],
             'gla_w_gate2': gla_w_gate2[l], 'gla_b_gate': gla_b_gate[l], 'gla_norm': gla_norm[l],
             'lru_conv_w': lru_conv_w[l], 'lru_conv_b': lru_conv_b[l], 'lru_w_a': lru_w_a[l],
             'lru_b_a': lru_b_a[l], 'lru_w_i': lru_w_i[l], 'lru_b_i': lru_b_i[l], 'lru_lambda': lru_lambda[l],
             'rwkv_mu': rwkv_mu[l], 'rwkv_w0': rwkv_w0[l], 'rwkv_w2': rwkv_w2[l], 'rwkv_a0': rwkv_a0[l],
             'rwkv_a2': rwkv_a2[l], 'rwkv_g2': rwkv_g2[l], 'rwkv_k_k': rwkv_k_k[l], 'rwkv_k_a': rwkv_k_a[l],
             'rwkv_r_k': rwkv_r_k[l], 'rwkv_ln_w': rwkv_ln_w[l], 'rwkv_ln_b': rwkv_ln_b[l],
             'ssd_conv_w': ssd_conv_w[l], 'ssd_conv_b': ssd_conv_b[l], 'ssd_dt_bias': ssd_dt_bias[l],
             'ssd_a_log': ssd_a_log[l], 'ssd_d': ssd_d[l], 'ssd_norm': ssd_norm[l]}
        y_p, st_p = hybrid_layer(y_p, zero_states(y_p.shape[0], y_p.dtype), p, True)
        st_in = (state_gla[l], state_lru[l], cache_lru_conv[l], cache_rwkv_shift[l], state_rwkv[l],
                 cache_ssd_conv[l], state_ssd[l])
        y_s, st_s = hybrid_layer(y_s, st_in, p, False)
        new_p.append(st_p)
        new_s.append(st_s)

    def stack(sts, i):
        return jnp.stack([s[i] for s in sts], axis=0)

    return (y_p, y_s,
            stack(new_p, 0), stack(new_s, 0),
            stack(new_p, 1), stack(new_s, 1),
            stack(new_p, 2), stack(new_s, 2),
            stack(new_p, 3), stack(new_s, 3),
            stack(new_p, 4), stack(new_s, 4),
            stack(new_p, 5), stack(new_s, 5),
            stack(new_p, 6), stack(new_s, 6))


_drawn_inputs = setup_inputs


def setup_inputs(seed=0):
    import zlib

    import numpy as np

    out = dict(_drawn_inputs(seed))
    spreads = {}
    factors = {'lru_b_a': 28.024, 'lru_b_i': 8.0, 'rwkv_k_k': 7.148, 'rwkv_ln_b': 8.0}
    for name, (base, spread) in spreads.items():
        noise = np.random.default_rng([zlib.crc32(name.encode()), seed]).standard_normal(out[name].shape)
        drawn = base * np.exp(spread * noise) if base else spread * noise
        out[name] = __import__('jax').numpy.asarray(drawn.astype(out[name].dtype))
    for name, factor in factors.items():
        out[name] = (out[name] * factor).astype(out[name].dtype)
    return out
```

```python
import math
from contextlib import ExitStack

import numpy as np

import concourse.bass as bass
from concourse import mybir

F32 = mybir.dt.float32
I32 = mybir.dt.int32
ALU = mybir.AluOpType
ACT = mybir.ActivationFunctionType
AX = mybir.AxisListType

P = 128
LAYERS = 2
SEQ, DEC = 256, 8
TOK = SEQ + DEC
CH = 128
NCH = SEQ // CH
LEAD = 3
ZW = LEAD + TOK
D_MODEL, D_FF = 2048, 8192
DT, FT = D_MODEL // P, D_FF // P
EPS = 1e-6
LN_EPS = 64e-5
DECAY = math.exp(-0.5)
LRU_C = 8.0
GATE_TEMP = 16.0
GELU_K = 2.0 * math.sqrt(2.0 / math.pi)
LEVELS = 7

Z_R, Z_K, Z_V, Z_WA, Z_G = 0, 4, 8, 12, 13
Z_GQ, Z_GK, Z_GV, Z_GG, Z_GA = 14, 16, 18, 22, 26
Z_SG, Z_SX, Z_SB, Z_SC, Z_DT = 27, 31, 35, 37, 39
Z_LX, Z_LG = 40, 44
ZT = 48
RWKV_T = 14
MIX_GLA, MIX_LRU, MIX_RWKV, MIX_SSD = 0, 4, 8, 12

UNITS = ZT + DT + FT + FT
RING = 4


def places(fields):
    at, out = 0, {}
    for name, n in fields:
        out[name] = (at, n)
        at += n
    return out, at


PARAM, N_PARAM = places([
    ("mix_pre", 16), ("mix_post", 16), ("mlp_pre", 16), ("mlp_post", 16),
    ("mu", 14), ("w0", 4), ("a0", 4), ("k_k", 4), ("k_a", 4), ("r_k", 4), ("ln_w", 4), ("ln_b", 4),
    ("gla_b", 2), ("gla_norm", 1),
    ("conv_b", 12), ("conv_w", 48), ("b_a", 4), ("b_i", 4), ("lam", 4),
    ("dt_bias", 1), ("a_log", 1), ("d_skip", 4), ("ssd_norm", 4),
    ("wa2", 512), ("g2", 512), ("gate2", 256), ("lru_wa", 512), ("lru_wi", 512)])

N_GAIN = PARAM["wa2"][0]
WORK = 5936
STORES = 10

CONST, N_CONST = places([
    ("ident", 128), ("ones", 128), ("pairs", 128), ("stack", 64), ("head_sum", 32), ("head_row", 512), ("tile_sum", 16),
    ("upper_both", 256), ("level_up", LEVELS * 128), ("level_low", LEVELS * 128)])


class Signal:

    def __init__(self, sem, per_layer):
        self.sem, self.per_layer = sem, per_layer

    def value(self, layer, n):
        return layer * self.per_layer + n


class Own:

    def __init__(self, engine, sem):
        self.engine, self.sem, self.n = engine, sem, 0

    def restart(self):
        self.engine.sem_clear(self.sem)
        self.n = 0

    def done(self, instruction):
        instruction.then_inc(self.sem, 1)
        self.n += 1
        self.engine.wait_ge(self.sem, self.n)


def build(nc, d):
    ctx = ExitStack()
    with ctx:
        def sbuf(name, *shape):
            return ctx.enter_context(nc.sbuf_tensor(name, [P, *shape], F32))

        def signal(name, per_layer=1):
            return Signal(ctx.enter_context(nc.semaphore(name)), per_layer)

        ring = sbuf("ring", RING, DT * P)
        x = sbuf("x", DT, TOK)
        hy = sbuf("hy", DT * TOK)
        mix = sbuf("mix", DT, TOK)
        zu = sbuf("zu", FT * TOK)
        work = sbuf("work", WORK)
        const = sbuf("const", N_CONST)
        par = sbuf("par", N_PARAM)
        gains = sbuf("gains", LAYERS, N_GAIN)
        sq = sbuf("sq", 2, TOK)
        rstd = sbuf("rstd", TOK)
        pre = sbuf("pre", 4, TOK)
        ps = ctx.enter_context(nc.psum_tensor("ps", [P, 8, 512], F32))

        hy3 = hy[:, :].rearrange("p (n t) -> p n t", t=TOK)
        u = zu[:, :].rearrange("p (n t) -> p n t", t=TOK)
        z = zu[:, 0:ZT * ZW].rearrange("p (n t) -> p n t", t=ZW)
        TAIL = ZT * ZW

        def part(t, at, *dims):
            n = int(np.prod(dims))
            v = t[:, at:at + n]
            if len(dims) == 2:
                return v.rearrange("p (a b) -> p a b", a=dims[0])
            if len(dims) == 3:
                return v.rearrange("p (a b c) -> p a b c", a=dims[0], b=dims[1])
            return v

        def zt(tile, n=1, first=0, last=TOK):
            return z[:, tile:tile + n, LEAD + first:LEAD + last]

        def pv(name, j=0, n=1, rows=P):
            at = PARAM[name][0]
            return par[0:rows, at + j:at + j + n]

        def pb(name, n, tokens=TOK):
            at = PARAM[name][0]
            return par[:, at:at + n].unsqueeze(2).broadcast_to([P, n, tokens])

        def cv(name, at=0, n=None, rows=P):
            first, size = CONST[name]
            n = size if n is None else n
            return const[0:rows, first + at:first + at + n]

        ident = cv("ident")
        ones = cv("ones")

        loaded = [ctx.enter_context(nc.semaphore(f"weights_loaded_{j}")) for j in range(RING)]
        unit_done = signal("unit_done", UNITS)
        bank_free = signal("bank_free", ZT + DT + DT)
        x_loaded = signal("x_loaded")
        gains_loaded = signal("gains_loaded")
        own_act, own_pool, own_dve = (ctx.enter_context(nc.semaphore(n)) for n in ("own_act", "own_pool", "own_dve"))
        consts_in = signal("consts_in")
        gains_in = signal("gains_in")
        matrices_in = signal("matrices_in", 16)
        rstd_in = signal("rstd_in", 4)
        x_in = signal("x_in", DT)
        x_mid = signal("x_mid", DT)
        h_ready = signal("h_ready", 2 * DT)
        sq_ready = signal("sq_ready", 4 * DT)
        sq_used = signal("sq_used", 4 * (DT - 1))
        mean_ready = signal("mean_ready", 4)
        root_ready = signal("root_ready", 4)
        rstd_ready = signal("rstd_ready", 4)
        y_out = signal("y_out", 2 * DT)
        pre_ready = signal("pre_ready", FT)
        u_ready = signal("u_ready", FT)
        mixed = signal("mixed")
        stored = ctx.enter_context(nc.semaphore("stored"))
        n_stored = [0]
        stat_in = signal("stat_in", 6)
        stat_sum = signal("stat_sum", 6)
        stat_row = signal("stat_row", 6)
        stat_wide = signal("stat_wide", 6)
        stat_mid = signal("stat_mid", 3)
        stat_root = signal("stat_root", 4)
        KK, MEAN, VAR, BONUS, GLA_RMS, SSD_RMS = range(1, 7)
        rows = pre[:, 0, :]

        shift_in = signal("shift_in", 16)
        zm_ready = signal("zm_ready")
        lowrank_in = signal("lowrank_in")
        decay_mm, decay_sig = signal("decay_mm"), signal("decay_sig")
        rate_mm, rate_sig = signal("rate_mm"), signal("rate_sig")
        rgate_mm, rgate_out = signal("rgate_mm"), signal("rgate_out")
        cum_ready, exps_ready = signal("cum_ready"), signal("exps_ready")
        operands_ready = signal("operands_ready")
        rstate_in = signal("rstate_in", 16)
        spread_in = signal("spread_in", 6)
        spread_out = signal("spread_out", 6)
        spread_read = signal("spread_read", 6)
        rdec_ready = signal("rdec_ready")
        score1_mm, score1 = signal("score1_mm", NCH), signal("score1", NCH)
        score2_mm, score2 = signal("score2_mm", NCH), signal("score2", NCH)
        rtok_mm, rtok = signal("rtok_mm", NCH), signal("rtok", NCH)
        inv_start = signal("inv_start", NCH)
        N_INV = NCH * LEVELS * 2
        q_mm, q_out = signal("q_mm", N_INV), signal("q_out", N_INV)
        dx_mm, dx_out = signal("dx_mm", N_INV), signal("dx_out", N_INV)
        rhs_mm, rhs_out = signal("rhs_mm", NCH), signal("rhs_out", NCH)
        u_mm, un_out = signal("u_mm", NCH), signal("un_out", NCH)
        ry_mm, ry_out = signal("ry_mm", NCH), signal("ry_out", NCH)
        rh_out = signal("rh_out", NCH)
        ryT_mm, ryT_out = signal("ryT_mm", NCH), signal("ryT_out", NCH)
        centred, bonus_read = signal("centred"), signal("bonus_read")
        shift_saved = signal("shift_saved")

        prev = sbuf("prev", RWKV_T, DEC)
        shifted = sbuf("shifted", RWKV_T, DEC + 1)
        mids, ends = sbuf("mids", 4, NCH), sbuf("ends", 4, NCH)
        dec = sbuf("dec", 3, 4, DEC)

        sig = part(zu, TAIL, 4, TOK)
        rate = part(zu, TAIL + 1056, 4, TOK)
        kk = part(zu, TAIL + 2112, 4, TOK)
        mixf = mix[:, :, :].rearrange("p n t -> p (n t)")
        cum = part(mixf, 0, 4, NCH, CH)
        kb = part(mixf, 1024, 4, TOK)
        gate = mix[:, MIX_RWKV:MIX_RWKV + 4, :]
        kr = work[:, 0:2048].rearrange("p (h c j t) -> p h c j t", h=4, c=NCH, j=2)
        kt = part(work, 2048, 4, NCH, CH)
        bt = part(work, 3072, 4, NCH, CH)
        yfm = part(work, 4096, 4, TOK)
        rk = mix[:, MIX_SSD:MIX_SSD + 4, :]
        delta = part(hy, 0, RWKV_T, TOK)
        hdec = part(hy, 0, 32, 64)
        tdec = part(hy, 2048, 32, 64)
        spread = part(zu, TAIL, 16, P)
        sc1 = part(hy, 0, 8, 2, P)
        sc2 = part(hy, 2048, 8, 2, P)
        vt, ktt, btt = (part(mixf, 512 * j, 512) for j in range(3))
        un = part(mixf, 1536, 4, 2, 64)
        xx = part(zu, TAIL, 8, 2, P)
        qb = part(zu, TAIL + 2048, 8, P)
        yt = part(zu, TAIL + 3072, 512)
        hst = part(zu, TAIL + 3584, 4, 64)

        ggate_mm, ggate_x, ggate_ln = signal("ggate_mm"), signal("ggate_x"), signal("ggate_ln")
        gdist, gdist_exp, gops = signal("gdist"), signal("gdist_exp"), signal("gops")
        gtok_mm, gtok = signal("gtok_mm"), signal("gtok")
        glevel_mm, glevel = signal("glevel_mm", LEVELS + 1), signal("glevel", LEVELS + 1)
        gy_mm, gy_out, gh_out = signal("gy_mm", NCH), signal("gy_out", NCH), signal("gh_out", NCH)
        gyT_mm, gyT_out = signal("gyT_mm", NCH), signal("gyT_out", NCH)
        gstate_in = signal("gstate_in", 16)
        gval_mm, gval_read = signal("gval_mm", 4), signal("gval_read", 4)
        gdec_ready, gdec_y_mm = signal("gdec_ready"), signal("gdec_y_mm")
        gsig = signal("gsig")
        glast, gdec = sbuf("glast", 2, NCH), sbuf("gdec", 2, DEC)
        dist = part(hy, 0, LEVELS, 2, SEQ)
        kdist = part(zu, TAIL, LEVELS, 2, SEQ)
        gyt = part(hy, 3584, 512)
        glog = part(work, 0, 2, TOK)
        gcum = part(work, 528, 512)
        gcum4 = part(work, 528, 2, NCH, CH)
        gsc = part(work, 1040, 8, P)
        gvt = part(work, 2064, NCH, 512)
        gkdT = part(work, 3088, 2, NCH, CH)
        gkd = part(work, 3600, NCH, 256)
        gqc = part(work, 4112, 2, NCH, CH)
        gof = part(work, 4624, 4, TOK)
        gtmp = part(work, 4624, 2, TOK)
        gst = part(work, 5680, 2, P)
        ghd = part(hy, 0, 16, P)
        gtd = part(zu, TAIL, 16, P)
        gsq = part(zu, TAIL + 2048, 4, TOK)

        conv_in = signal("conv_in", 16)
        conv_slot, conv_dec, conv_out = signal("conv_slot"), signal("conv_dec"), signal("conv_out")
        cbuf = sbuf("cbuf", 4, 12, DEC)
        cps = sbuf("cps", 12, 3)
        cx = part(work, 0, 12, TOK)
        ctmp = part(work, 3168, 12, DEC)
        conv_z = lambda t: Z_SX + t if t < 8 else Z_LX + t - 8

        ssig, ssilu = signal("ssig"), signal("ssilu")
        sdt_x, sdt_ln, sdt_c, sdt = signal("sdt_x"), signal("sdt_ln"), signal("sdt_c"), signal("sdt")
        sdt_mm, sdt_read = signal("sdt_mm"), signal("sdt_read")
        sdec_mm, sdec_read = signal("sdec_mm"), signal("sdec_read")
        srow_mm, srow_read, sexps = signal("srow_mm"), signal("srow_read"), signal("sexps")
        ssc_mm, ssc_out = signal("ssc_mm"), signal("ssc_out")
        stok_mm, stok, sops = signal("stok_mm"), signal("stok"), signal("sops")
        sy_mm, sy_out, sh_out = signal("sy_mm", NCH), signal("sy_out", NCH), signal("sh_out", NCH)
        syT_mm, syT_out = signal("syT_mm", NCH), signal("syT_out", NCH)
        sstate_in = signal("sstate_in", 16)
        sbc_mm, sbc_read = signal("sbc_mm", 4), signal("sbc_read", 4)
        sdec_done = signal("sdec_done")
        dtr, dcum = pre[:, 1, :], pre[:, 2, :]
        acol = sbuf("acol", 1)
        dedec, sdec = sbuf("dedec", DEC), sbuf("sdec", 4, DEC)
        cumT, lastv = sbuf("cumT", NCH, 8), sbuf("lastv", NCH, 8)
        wdec, ecum, elast = sbuf("wdec", NCH, 8), sbuf("ecum", NCH, 8), sbuf("elast", NCH, 8)
        seg = part(hy, 0, 8, NCH, CH)
        xtok = part(hy, 2048, NCH, 512)
        syt = part(hy, 3072, 512)
        sst = part(hy, 3584, 512)
        xdt = part(work, 3168 + 96, 4, TOK)
        xd = part(work, 4320, NCH, 512)
        ssc = part(work, 5344, 2, NCH, CH)
        btok = part(zu, TAIL, NCH, 2, P)
        syf = part(zu, TAIL + 512, 4, TOK)
        ysq = part(zu, TAIL + 1568, 4, TOK)
        yoff = part(zu, TAIL + 1568, 512)
        stmp = part(zu, TAIL, 8, TOK)
        shd = part(hy, 0, 32, P)
        std = part(zu, TAIL + 1568, 16, P)

        ssd_mixed = signal("ssd_mixed")

        lra_mm, lra, lri_mm, lri = signal("lra_mm"), signal("lra"), signal("lri_mm"), signal("lri")
        lam_abs, lam_ready, lexp = signal("lam_abs"), signal("lam_ready"), signal("lexp")
        lmul, lroot = signal("lmul"), signal("lroot")
        gelu_in, gelu_sig = signal("gelu_in"), signal("gelu_sig")
        lru_saved, lru_in = signal("lru_saved"), signal("lru_in", 16)
        h0 = sbuf("h0", 4, DEC)
        lout = sbuf("lout", 4, DEC + 1)
        lam8, lamn, lamt = sbuf("lam8", 4), sbuf("lamn", 4), sbuf("lamt", 4)
        lr, li, lth = (part(zu, TAIL + 1056 * j, 4, TOK) for j in range(3))
        la, lm, lh, lg = (part(hy, 1056 * j, 4, TOK) for j in range(4))
        NORM_MIX, NORM_MIX_POST, NORM_MLP, NORM_MLP_POST = range(4)
        STAT = 7

        block = ctx.enter_context(nc.Block())

        @block.sync
        def _(sp):
            for j in range(RING):
                sp.dma_start(ring[:, j, :], d["weights"][j, :, :]).then_inc(loaded[j], 16)
            with sp.Fori(1, LAYERS * UNITS // RING) as g:
                for j in range(RING):
                    sp.wait_ge(unit_done.sem, (g - 1) * RING + j + 1)
                    sp.dma_start(ring[:, j, :], d["weights"][bass.ds(g * RING + j, 1), :, :]
                                 .rearrange("o p n -> p (o n)")).then_inc(loaded[j], 16)

        @block.tensor
        def _(pe):
            mm = nc.tensor.matmul
            own = None

            def dense_tile(l, turn, slot, rhs):
                pe.wait_ge(loaded[slot], (l * (UNITS // RING) + turn + 1) * 16)
                for k in range(DT):
                    last = mm(ps[:, slot, 0:TOK], ring[:, slot, k * P:(k + 1) * P], rhs[:, k, :],
                              start=(k == 0), stop=(k == DT - 1))
                last.then_inc(unit_done.sem, 1)

            def norm_sum(l, norm, j, half, first=False, last=False):
                pe.wait_ge(sq_ready.sem, l * sq_ready.per_layer + norm * DT + j + 1)
                mm(ps[:, STAT, 0:TOK], ones, sq[:, half, :], start=first, stop=last)\
                    .then_inc((mean_ready if last else sq_used).sem, 1)

            def norm_sums(l, norm):
                for j in range(DT):
                    norm_sum(l, norm, j, j % 2, first=(j == 0), last=(j == DT - 1))

            def project(l, unit, bank, per_tile, rhs, norm):
                def four(g, first, last):
                    for b in range(4):
                        pe.wait_ge(bank_free.sem, l * bank_free.per_layer + bank + g * 4 + b + 1)
                        for q in range(per_tile):
                            slot = (b * per_tile + q) % RING
                            turn = unit // RING + (g * per_tile + b * per_tile // RING)
                            pe.wait_ge(loaded[slot], (l * (UNITS // RING) + turn + 1) * 16)
                            for k in range(DT):
                                mm_ = mm(ps[:, b, 0:TOK], ring[:, slot, k * P:(k + 1) * P], rhs[:, q * DT + k, :],
                                         start=(q == 0 and k == 0), stop=(q == per_tile - 1 and k == DT - 1))
                            mm_.then_inc(unit_done.sem, 1)
                        if b or not first:
                            norm_sum(l, norm, g * 4 + b - 1, (b + 1) % 2, first=(first and b == 1))
                four(0, True, False)
                with pe.Fori(1, DT // 4) as g:
                    four(g, False, False)
                norm_sum(l, norm, DT - 1, 1, last=True)

            def head_stat(l, n, src, lhs_sum, lhs_wide, n_rows, one=False):
                pe.wait_ge(stat_in.sem, stat_in.value(l, n))
                for t in range(4):
                    last = mm(ps[0:n_rows, 4, 0:TOK], lhs_sum(t), src(t), start=(t == 0), stop=(t == 3))
                last.then_inc(stat_sum.sem, 1)
                pe.wait_ge(stat_row.sem, stat_row.value(l, n))
                for t in range(1 if one else 4):
                    last = mm(ps[:, 4 + t, 0:TOK], lhs_wide(t), rows[0:n_rows, :], start=True, stop=True)
                last.then_inc(stat_wide.sem, 1)

            def by_pair(l, n, src):
                head_stat(l, n, src, lambda t: cv("head_sum", 8 * t, 8),
                          lambda t: cv("head_row", t * P, P, 8), 8)

            def rwkv_prep(l):
                pe.wait_ge(matrices_in.sem, matrices_in.value(l, 16))
                pe.wait_ge(lowrank_in.sem, lowrank_in.value(l, 1))
                for t in range(4):
                    last = mm(ps[:, 4 + t, 0:TOK], pv("wa2", t * P, P, 64), z[0:64, Z_WA, LEAD:ZW],
                              start=True, stop=True)
                last.then_inc(decay_mm.sem, 1)
                pe.wait_ge(decay_sig.sem, decay_sig.value(l, 1))
                at = PARAM["wa2"][0]
                for t in range(4):
                    last = mm(ps[:, 4 + t, 0:TOK], par[64:P, at + t * P:at + (t + 1) * P], z[64:P, Z_WA, LEAD:ZW],
                              start=True, stop=True)
                last.then_inc(rate_mm.sem, 1)
                pe.wait_ge(rate_sig.sem, rate_sig.value(l, 1))
                for t in range(4):
                    last = mm(ps[:, 4 + t, 0:TOK], pv("g2", t * P, P), z[:, Z_G, LEAD:ZW], start=True, stop=True)
                last.then_inc(rgate_mm.sem, 1)
                pe.wait_ge(rgate_out.sem, rgate_out.value(l, 1))
                by_pair(l, KK, lambda t: rk[:, t, :])

            def rwkv_decode(l):
                pe.wait_ge(rstate_in.sem, rstate_in.value(l, 16))
                for n in range(6):
                    half = n % 2
                    pe.wait_ge(spread_in.sem, spread_in.value(l, n + 1))
                    if n >= 2:
                        pe.wait_ge(spread_read.sem, spread_read.value(l, n - 1))
                    if n == 4:
                        pe.wait_ge(rdec_ready.sem, rdec_ready.value(l, 1))
                    for i in range(16):
                        rhs = cv("stack") if n // 2 == 1 else hdec[:, half * 16 + i, :]
                        at = i % 8 * 64
                        last = mm(ps[:, 4 + 2 * half + i // 8, at:at + 64], spread[:, i, :], rhs,
                                  start=True, stop=True)
                    last.then_inc(spread_out.sem, 1)

            def rwkv_chunk(l, c):
                heads = [(i, i // 4, i % 4) for i in range(8)]
                for key, out_mm, before in ((kt, score1_mm, None), (bt, score2_mm, score1)):
                    if before is None:
                        pe.wait_ge(operands_ready.sem, operands_ready.value(l, 1))
                        pe.wait_ge(spread_read.sem, spread_read.value(l, 6))
                        if c:
                            pe.wait_ge(ryT_out.sem, ryT_out.value(l, c))
                            pe.wait_ge(rh_out.sem, rh_out.value(l, c))
                    else:
                        pe.wait_ge(before.sem, before.value(l, c + 1))
                    for i, par_, hp in heads:
                        r = slice(64 * par_, 64 * par_ + 64)
                        last = mm(ps[:, 4 + i // 2, i % 2 * 256:i % 2 * 256 + 256], key[r, hp, c, :],
                                  kr[r, hp, c, :, :].rearrange("p j t -> p (j t)"), start=True, stop=True)
                    last.then_inc(out_mm.sem, 1)
                pe.wait_ge(score2.sem, score2.value(l, c + 1))
                for j in range(3):
                    for hp in range(4):
                        src = zt(Z_V + hp, 1, c * CH, c * CH + CH).rearrange("p o t -> p (o t)") if j == 0 \
                            else (kt, bt)[j - 1][:, hp, c, :]
                        last = nc.tensor.transpose(ps[:, 4 + j, hp * P:hp * P + P], src, ident)
                last.then_inc(rtok_mm.sem, 1)
                pe.wait_ge(rtok.sem, rtok.value(l, c + 1))
                pe.wait_ge(inv_start.sem, inv_start.value(l, c + 1))
                for j in range(LEVELS):
                    n = (c * LEVELS + j) * 2
                    for half in range(2):
                        if j:
                            pe.wait_ge(dx_out.sem, dx_out.value(l, n - 1 + half))
                        for i in range(4):
                            h = half * 4 + i
                            last = mm(ps[:, 4 + half, i * P:i * P + P], sc2[:, h, 0, :], xx[:, h, 0, :],
                                      start=True, stop=True)
                        last.then_inc(q_mm.sem, 1)
                    for half in range(2):
                        pe.wait_ge(q_out.sem, q_out.value(l, n + 1 + half))
                        if half:
                            pe.wait_ge(dx_out.sem, dx_out.value(l, n + 1))
                        for i in range(4):
                            h = half * 4 + i
                            o = ps[:, 6 + i // 2, i % 2 * 256:i % 2 * 256 + 256]
                            mm(o[:, 0:P], xx[:, h, 1, :], qb[:, h, :], start=True, stop=True)
                            last = mm(o[:, P:2 * P], qb[:, h, :], xx[:, h, 1, :], start=True, stop=True)
                        last.then_inc(dx_mm.sem, 1)
                pe.wait_ge(dx_out.sem, dx_out.value(l, (c + 1) * LEVELS * 2))
                for i, par_, hp in heads:
                    r = slice(64 * par_, 64 * par_ + 64)
                    o = ps[:, 4 + par_, hp * 64:hp * 64 + 64]
                    if c:
                        mm(o, kr[r, hp, c, 0, :], hst[r, hp, :], start=True, stop=False)
                    last = mm(o, sc1[:, i, 0, :], vt[:, (2 * hp + par_) * 64:(2 * hp + par_) * 64 + 64],
                              start=(c == 0), stop=True)
                last.then_inc(rhs_mm.sem, 1)
                pe.wait_ge(rhs_out.sem, rhs_out.value(l, c + 1))
                for i, par_, hp in heads:
                    last = mm(ps[:, 6, i * 64:i * 64 + 64], xx[:, i, 1, :], un[:, hp, par_, :], start=True, stop=True)
                last.then_inc(u_mm.sem, 1)
                pe.wait_ge(un_out.sem, un_out.value(l, c + 1))
                for i, par_, hp in heads:
                    r = slice(64 * par_, 64 * par_ + 64)
                    o = ps[:, 4 + par_, hp * 64:hp * 64 + 64]
                    if c:
                        mm(o, kr[r, hp, c, 1, :], hst[r, hp, :], start=True, stop=False)
                    mm(o, sc1[:, i, 1, :], vt[:, (2 * hp + par_) * 64:(2 * hp + par_) * 64 + 64],
                       start=(c == 0), stop=False)
                    mm(o, sc2[:, i, 1, :], un[:, hp, par_, :], start=False, stop=True)
                for hp in range(4):
                    o = ps[:, 6, hp * P:hp * P + P]
                    mm(o, ktt[:, hp * P:hp * P + P], vt[:, hp * P:hp * P + P], start=True, stop=False)
                    last = mm(o, btt[:, hp * P:hp * P + P], un[:, hp, :, :].rearrange("p a b -> p (a b)"),
                              start=False, stop=True)
                last.then_inc(ry_mm.sem, 1)
                pe.wait_ge(ry_out.sem, ry_out.value(l, c + 1))
                for hp in range(4):
                    last = nc.tensor.transpose(ps[:, 7, hp * P:hp * P + P], yt[:, hp * P:hp * P + P], ident)
                last.then_inc(ryT_mm.sem, 1)

            def rwkv_post(l):
                by_pair(l, MEAN, lambda t: yfm[:, t, :])
                by_pair(l, VAR, lambda t: delta[:, t, :])
                by_pair(l, BONUS, lambda t: rk[:, t, :])

            def gla(l):
                pe.wait_ge(bonus_read.sem, bonus_read.value(l, 1))
                pe.wait_ge(matrices_in.sem, matrices_in.value(l, 16))
                for t in range(2):
                    last = mm(ps[:, 4 + t, 0:TOK], pv("gate2", t * P, P, 16), z[0:16, Z_GA, LEAD:ZW],
                              start=True, stop=True)
                last.then_inc(ggate_mm.sem, 1)
                pe.wait_ge(gops.sem, gops.value(l, 1))
                for c in range(NCH):
                    for h in range(4):
                        last = nc.tensor.transpose(ps[:, 4 + c, h * P:h * P + P],
                                                   z[:, Z_GV + h, LEAD + c * CH:LEAD + c * CH + CH], ident)
                    for hp in range(2):
                        at = (c * 2 + hp) * P
                        last = nc.tensor.transpose(ps[:, 6, at:at + P], gkdT[:, hp, c, :], ident)
                last.then_inc(gtok_mm.sem, 1)
                pe.wait_ge(gtok.sem, gtok.value(l, 1))
                for j in range(LEVELS + 1):
                    if j >= 2:
                        pe.wait_ge(glevel.sem, glevel.value(l, j - 1))
                    for a in range(2):
                        r = slice(64 * a, 64 * a + 64)
                        for hp in range(2):
                            for c in range(NCH):
                                t = slice(c * CH, c * CH + CH)
                                tz = slice(LEAD + c * CH, LEAD + c * CH + CH)
                                k_, q_ = (kdist[r, j, hp, t], dist[r, j, hp, t]) if j < LEVELS else \
                                    (z[r, Z_GK + hp, tz], z[r, Z_GQ + hp, tz])
                                at = (hp * NCH + c) * P
                                last = mm(ps[:, 4 + 2 * (j % 2) + a, at:at + P], k_, q_, start=True, stop=True)
                    last.then_inc(glevel_mm.sem, 1)
                for c in range(NCH):
                    pe.wait_ge(glevel.sem, glevel.value(l, LEVELS + 1))
                    if c:
                        pe.wait_ge(gh_out.sem, gh_out.value(l, c))
                        pe.wait_ge(gyT_out.sem, gyT_out.value(l, c))
                    for a in range(2):
                        r = slice(64 * a, 64 * a + 64)
                        for hp in range(2):
                            o = ps[:, 4 + a, hp * P:hp * P + P]
                            h = 2 * hp + a
                            if c:
                                mm(o, gqc[r, hp, c, :], gst[r, hp, :], start=True, stop=False)
                            mm(o, gsc[:, (a * 2 + hp) * NCH + c, :], gvt[:, c, h * P:h * P + P],
                               start=(c == 0), stop=True)
                    for hp in range(2):
                        last = mm(ps[:, 6, hp * 256:hp * 256 + 256], gkd[:, c, hp * P:hp * P + P],
                                  gvt[:, c, hp * 256:hp * 256 + 256], start=True, stop=True)
                    last.then_inc(gy_mm.sem, 1)
                    pe.wait_ge(gy_out.sem, gy_out.value(l, c + 1))
                    for h in range(4):
                        last = nc.tensor.transpose(ps[:, 7, h * P:h * P + P], gyt[:, h * P:h * P + P], ident)
                    last.then_inc(gyT_mm.sem, 1)
                pe.wait_ge(gyT_out.sem, gyT_out.value(l, NCH))
                for n in range(4):
                    pe.wait_ge(gh_out.sem, gh_out.value(l, NCH))
                    if n >= 2:
                        pe.wait_ge(gval_read.sem, gval_read.value(l, n - 1))
                    for b in range(2):
                        for h in range(4):
                            col = LEAD + SEQ + n * 2 + b
                            last = mm(ps[:, 4 + 2 * (n % 2) + b, h * P:h * P + P],
                                      z[:, Z_GV + h, col:col + 1].broadcast_to([P, P]), ident, start=True, stop=True)
                    last.then_inc(gval_mm.sem, 1)
                pe.wait_ge(gdec_ready.sem, gdec_ready.value(l, 1))
                for a in range(2):
                    r = slice(64 * a, 64 * a + 64)
                    for hp in range(2):
                        for b in range(DEC):
                            col = LEAD + SEQ + b
                            last = mm(ps[:, 4 + a, hp * DEC + b:hp * DEC + b + 1], ghd[r, b * 2 + hp, :],
                                      z[r, Z_GQ + hp, col:col + 1], start=True, stop=True)
                last.then_inc(gdec_y_mm.sem, 1)
                head_stat(l, GLA_RMS, lambda t: gsq[:, t, :], lambda t: cv("tile_sum", 4 * t, 4),
                          lambda t: cv("ident", t, 1, 4).broadcast_to([4, P]), 4)

            def ssd(l):
                pe.wait_ge(sdt.sem, sdt.value(l, 1))
                for t in range(4):
                    last = mm(ps[:, 4 + t, 0:TOK], cv("head_row", t * P, P, 8), dtr[0:8, :], start=True, stop=True)
                last.then_inc(sdt_mm.sem, 1)
                pe.wait_ge(sdt_read.sem, sdt_read.value(l, 1))
                for t in range(4):
                    mm(ps[:, 4, t * DEC:t * DEC + DEC], cv("head_row", t * P, P, 8), dedec[0:8, :], start=True, stop=True)
                for c in range(NCH):
                    last = mm(ps[:, 5, c * 8:c * 8 + 8], dcum[0:8, c * CH:c * CH + CH], cv("ident", 0, 8, 8),
                              start=True, stop=True)
                last.then_inc(sdec_mm.sem, 1)
                pe.wait_ge(sdec_read.sem, sdec_read.value(l, 1))
                for h in range(8):
                    last = mm(ps[:, 4 + h // 2, h % 2 * SEQ:h % 2 * SEQ + SEQ],
                              cv("ident", h, 1, 8).broadcast_to([8, P]), dcum[0:8, 0:SEQ], start=True, stop=True)
                last.then_inc(srow_mm.sem, 1)
                pe.wait_ge(srow_read.sem, srow_read.value(l, 1))
                for g in range(2):
                    for c in range(NCH):
                        t = slice(c * CH, c * CH + CH)
                        last = mm(ps[:, 4, (g * NCH + c) * P:(g * NCH + c) * P + P], cx[:, 4 + g, t], cx[:, 6 + g, t],
                                  start=True, stop=True)
                last.then_inc(ssc_mm.sem, 1)
                for c in range(NCH):
                    t = slice(c * CH, c * CH + CH)
                    for h in range(4):
                        last = nc.tensor.transpose(ps[:, 5 + c, h * P:h * P + P], xdt[:, h, t], ident)
                    for g in range(2):
                        last = nc.tensor.transpose(ps[:, 7, (c * 2 + g) * P:(c * 2 + g) * P + P], cx[:, 4 + g, t], ident)
                last.then_inc(stok_mm.sem, 1)
                pe.wait_ge(sops.sem, sops.value(l, 1))
                for c in range(NCH):
                    if c:
                        pe.wait_ge(sh_out.sem, sh_out.value(l, c))
                        pe.wait_ge(sy_out.sem, sy_out.value(l, c))
                        pe.wait_ge(syT_out.sem, syT_out.value(l, c))
                    for h in range(8):
                        last = mm(ps[:, 4, h * 64:h * 64 + 64], seg[:, h, c, :], xtok[:, c, h * 64:h * 64 + 64],
                                  start=True, stop=True)
                    for g in range(2):
                        w = slice(g * 256, g * 256 + 256)
                        if c:
                            mm(ps[:, 5, w], cx[:, 6 + g, c * CH:c * CH + CH], sst[:, w], start=True, stop=True)
                        last = mm(ps[:, 6, w], btok[:, c, g, :], xd[:, c, w], start=True, stop=True)
                    last.then_inc(sy_mm.sem, 1)
                    pe.wait_ge(sy_out.sem, sy_out.value(l, c + 1))
                    for h in range(4):
                        last = nc.tensor.transpose(ps[:, 7, h * P:h * P + P], syt[:, h * P:h * P + P], ident)
                    last.then_inc(syT_mm.sem, 1)
                pe.wait_ge(syT_out.sem, syT_out.value(l, NCH))
                for n in range(4):
                    pe.wait_ge(sh_out.sem, sh_out.value(l, NCH))
                    if n >= 2:
                        pe.wait_ge(sbc_read.sem, sbc_read.value(l, n - 1))
                    for b in range(4):
                        for g in range(2):
                            at = (b * 2 + g) * P
                            col = SEQ + (n % 2) * 4 + b
                            src = cx[:, (4 if n < 2 else 6) + g, col:col + 1]
                            last = mm(ps[:, 4 + 2 * (n % 2) + at // 512, at % 512:at % 512 + P],
                                      src.broadcast_to([P, P]), ident, start=True, stop=True)
                    last.then_inc(sbc_mm.sem, 1)
                head_stat(l, SSD_RMS, lambda t: ysq[:, t, :], lambda t: cv("ones", 0, 1),
                          lambda t: cv("ones", 0, P, 1), 1, one=True)

            def lru(l):
                for w, before, out in (("lru_wa", conv_out, lra_mm), ("lru_wi", lra, lri_mm)):
                    pe.wait_ge(before.sem, before.value(l, 1))
                    for t in range(4):
                        last = mm(ps[:, 4 + t, 0:TOK], pv(w, t * P, P), cx[:, 8 + t, :], start=True, stop=True)
                    last.then_inc(out.sem, 1)

            pe.wait_ge(consts_in.sem, 16)
            with pe.Fori(0, LAYERS) as l:
                norm_sums(l, NORM_MIX)
                with pe.Fori(0, ZT // 4) as g:
                    pe.wait_ge(h_ready.sem, h_ready.value(l, DT))
                    for j in range(4):
                        pe.wait_ge(bank_free.sem, l * bank_free.per_layer + g * 4 + j + 1)
                        dense_tile(l, g, j, hy3)
                rwkv_prep(l)
                rwkv_decode(l)
                for c in range(NCH):
                    rwkv_chunk(l, c)
                rwkv_post(l)
                gla(l)
                ssd(l)
                pe.wait_ge(ssd_mixed.sem, ssd_mixed.value(l, 1))
                lru(l)
                pe.wait_ge(mixed.sem, mixed.value(l, 1))
                project(l, ZT, ZT, 1, mix, NORM_MIX_POST)
                norm_sums(l, NORM_MLP)
                with pe.Fori(0, FT // 4) as g:
                    pe.wait_ge(h_ready.sem, h_ready.value(l, 2 * DT))
                    for j in range(4):
                        pe.wait_ge(pre_ready.sem, l * FT + g * 4 + j + 1)
                        dense_tile(l, (ZT + DT) // RING + g, j, hy3)
                pe.wait_ge(u_ready.sem, l * FT + FT + 4)
                project(l, ZT + DT + FT, ZT + DT, 4, u, NORM_MLP_POST)

        @block.scalar
        def _(act):
            A = nc.scalar.activation
            own = Own(act, own_act)

            def squares(l, norm, ready):
                with act.Fori(0, DT // 2) as g:
                    for j in range(2):
                        act.wait_ge(ready.sem, l * DT + g * 2 + j + 1)
                        act.wait_ge(sq_used.sem, l * sq_used.per_layer + norm * (DT - 1) + g * 2 + j + 1)
                        A(sq[:, j, :], x[:, bass.ds(g * 2 + j, 1), :].rearrange("p o t -> p (o t)"),
                          ACT.Square).then_inc(sq_ready.sem, 1)

            def root(l, norm):
                act.wait_ge(rstd_in.sem, rstd_in.value(l, norm + 1))
                A(rstd[:, :], rstd[:, :], ACT.Sqrt).then_inc(root_ready.sem, 1)

            def copy_out(l, norm, unit, per_tile):
                with act.Fori(0, DT // 4) as g:
                    for j in range(4):
                        act.wait_ge(unit_done.sem, l * UNITS + unit + (g * 4 + j + 1) * per_tile)
                        act.wait_ge(sq_used.sem, l * sq_used.per_layer + norm * (DT - 1) + g * 4 + j + 1)
                        A(sq[:, j % 2, :], ps[:, j, 0:TOK], ACT.Square).then_inc(sq_ready.sem, 1)
                        A(hy3[:, bass.ds(g * 4 + j, 1), :].rearrange("p o t -> p (o t)"), ps[:, j, 0:TOK],
                          ACT.Copy).then_inc(bank_free.sem, 1)

            act.dma_start(const[:, :], d["consts"]).then_inc(consts_in.sem, 16)
            act.dma_start(x[:, :, :], d["x"]).then_inc(x_loaded.sem, 16)
            act.dma_start(gains[:, :, :], d["params"][:, :, 0:N_GAIN].rearrange("l p n -> p l n")).then_inc(gains_loaded.sem, 16)
            act.wait_ge(gains_loaded.sem, 16)
            with act.Fori(0, LAYERS) as l:
                own.restart()
                act.wait_ge(x_in.sem, l * DT + DT)
                A(par[:, 0:N_GAIN], gains[:, bass.ds(l, 1), :].rearrange("p o n -> p (o n)"), ACT.Copy)\
                    .then_inc(gains_in.sem, 1)
                act.dma_start(par[:, N_GAIN:N_PARAM], d["params"][bass.ds(l, 1), :, N_GAIN:N_PARAM]
                              .rearrange("o p n -> p (o n)")).then_inc(matrices_in.sem, 16)
                squares(l, NORM_MIX, x_in)
                root(l, NORM_MIX)
                act.dma_start(prev[:, :, :], d["shift"][bass.ds(l, 1), :, :]
                              .rearrange("o p (n b) -> p (o n) b", b=DEC)).then_inc(shift_in.sem, 16)
                act.wait_ge(shift_saved.sem, l + 1)
                act.dma_start(d["shift_out"][bass.ds(l, 1), :, :, :].rearrange("o p n b -> p (o n) b"),
                              shifted[:, :, :]).then_inc(stored, 16)
                act.wait_ge(zm_ready.sem, l + 1)
                act.dma_start(part(hy, 0, 2048), d["rwkv_state"][bass.ds(l, 1), :, :]
                              .rearrange("o p n -> p (o n)")).then_inc(rstate_in.sem, 16)
                own.done(A(z[0:64, Z_WA, LEAD:ZW], z[0:64, Z_WA, LEAD:ZW], ACT.Tanh))
                A(z[:, Z_G, LEAD:ZW], z[:, Z_G, LEAD:ZW], ACT.Sigmoid).then_inc(lowrank_in.sem, 1)
                act.wait_ge(decay_mm.sem, l + 1)
                for t in range(4):
                    last = A(sig[:, t, :], ps[:, 4 + t, 0:TOK], ACT.Sigmoid, bias=pv("w0", t))
                last.then_inc(decay_sig.sem, 1)
                act.wait_ge(rate_mm.sem, l + 1)
                for t in range(4):
                    last = A(rate[:, t, :], ps[:, 4 + t, 0:TOK], ACT.Sigmoid, bias=pv("a0", t))
                last.then_inc(rate_sig.sem, 1)
                act.wait_ge(rgate_mm.sem, l + 1)
                A(gate, ps[:, 4:8, 0:TOK], ACT.Copy).then_inc(rgate_out.sem, 1)
                act.wait_ge(stat_sum.sem, stat_sum.value(l, KK))
                A(rows[0:8, :], ps[0:8, 4, 0:TOK], ACT.Sqrt).then_inc(stat_root.sem, 1)
                act.wait_ge(cum_ready.sem, l + 1)
                own.done(A(kt, cum, ACT.Exp, scale=DECAY))
                for h in range(4):
                    own.done(A(kr[:, h, :, 1, :], cum[:, h, :, :], ACT.Exp, scale=-DECAY))
                    own.done(A(kr[:, h, :, 0, :], kr[:, h, :, 0, :], ACT.Exp, scale=-DECAY))
                own.done(A(ends[:, :, :], ends[:, :, :], ACT.Exp, scale=-DECAY))
                own.done(A(mids[:, :, :], mids[:, :, :], ACT.Exp, scale=-DECAY))
                A(dec[:, 0, :, :], sig[:, :, SEQ:TOK], ACT.Exp, scale=-DECAY).then_inc(exps_ready.sem, 1)
                act.wait_ge(spread_read.sem, spread_read.value(l, 6))
                act.dma_start(d["rwkv_s"][bass.ds(l, 1), :, :].rearrange("o p n -> p (o n)"), part(hy, 0, 2048))\
                    .then_inc(stored, 16)
                for c in range(NCH):
                    act.wait_ge(rtok_mm.sem, rtok_mm.value(l, c + 1))
                    for j, t in enumerate((vt, ktt, btt)):
                        last = A(t, ps[:, 4 + j, :], ACT.Copy)
                    last.then_inc(rtok.sem, 1)
                    act.wait_ge(rhs_mm.sem, rhs_mm.value(l, c + 1))
                    for a in range(2):
                        last = A(un[:, :, a, :], ps[:, 4 + a, 0:256].rearrange("p (h v) -> p h v", h=4), ACT.Copy)
                    last.then_inc(rhs_out.sem, 1)
                    act.wait_ge(u_mm.sem, u_mm.value(l, c + 1))
                    for a in range(2):
                        last = A(un[:, :, a, :], ps[:, 6, a * 256:a * 256 + 256].rearrange("p (h v) -> p h v", h=4),
                                 ACT.Copy, scale=-1.0)
                    last.then_inc(un_out.sem, 1)
                    act.wait_ge(ry_mm.sem, ry_mm.value(l, c + 1))
                    ytv = yt.rearrange("p (h a v) -> p h a v", h=4, a=2)
                    for a in range(2):
                        last = A(ytv[:, :, a, :], ps[:, 4 + a, 0:256].rearrange("p (h v) -> p h v", h=4), ACT.Copy)
                    last.then_inc(ry_out.sem, 1)
                    act.wait_ge(ryT_mm.sem, ryT_mm.value(l, c + 1))
                    A(yfm[:, :, c * CH:c * CH + CH], ps[:, 7, :].rearrange("p (h t) -> p h t", h=4), ACT.Copy)\
                        .then_inc(ryT_out.sem, 1)
                act.wait_ge(rh_out.sem, rh_out.value(l, NCH))
                act.dma_start(d["rwkv_p"][bass.ds(l, 1), :, :].rearrange("o p n -> p (o n)"), part(zu, TAIL + 3584, 256))\
                    .then_inc(stored, 16)
                act.wait_ge(centred.sem, l + 1)
                A(delta[:, 0:4, :], yfm, ACT.Square).then_inc(stat_in.sem, 1)
                act.wait_ge(stat_mid.sem, stat_mid.value(l, 1))
                A(rows[0:8, :], rows[0:8, :], ACT.Sqrt).then_inc(stat_root.sem, 1)

                A(mix[:, MIX_GLA:MIX_GLA + 4, :], zt(Z_GG, 4), ACT.Sigmoid).then_inc(gsig.sem, 1)
                act.wait_ge(ggate_x.sem, l + 1)
                own.done(A(gtmp, glog, ACT.Abs))
                own.done(A(gtmp, gtmp, ACT.Exp, scale=-1.0))
                A(gtmp, gtmp, ACT.Ln, bias=1.0).then_inc(ggate_ln.sem, 1)
                act.wait_ge(gdist.sem, l + 1)
                own.done(A(gqc, gcum4, ACT.Exp, scale=1.0 / GATE_TEMP))
                own.done(A(gkdT, gkdT, ACT.Exp, scale=-1.0 / GATE_TEMP))
                own.done(A(glast[:, :, :], gcum4[:, :, :, CH - 1], ACT.Exp, scale=1.0 / GATE_TEMP))
                own.done(A(gdec[:, :, :], glog[:, :, SEQ:TOK], ACT.Exp, scale=1.0 / GATE_TEMP))
                distf = part(hy, 0, LEVELS * 512)
                own.done(A(distf, distf, ACT.Abs))
                A(distf, distf, ACT.Exp, scale=-1.0 / GATE_TEMP).then_inc(gdist_exp.sem, 1)
                act.wait_ge(gtok_mm.sem, l + 1)
                A(gvt, ps[:, 4:6, :], ACT.Copy)
                A(gkd, ps[:, 6, :].rearrange("p (c n) -> p c n", c=NCH), ACT.Copy).then_inc(gtok.sem, 1)
                act.wait_ge(glevel.sem, glevel.value(l, LEVELS + 1))
                act.dma_start(part(hy, 0, 2048), d["gla_state"][bass.ds(l, 1), :, :]
                              .rearrange("o p n -> p (o n)")).then_inc(gstate_in.sem, 16)
                for c in range(NCH):
                    act.wait_ge(gy_mm.sem, gy_mm.value(l, c + 1))
                    gyv = gyt.rearrange("p (h a v) -> p h a v", h=2, a=2)
                    for a in range(2):
                        last = A(gyv[:, :, a, :], ps[:, 4 + a, 0:256].rearrange("p (h v) -> p h v", h=2), ACT.Copy)
                    last.then_inc(gy_out.sem, 1)
                    act.wait_ge(gyT_mm.sem, gyT_mm.value(l, c + 1))
                    A(gof[:, :, c * CH:c * CH + CH], ps[:, 7, :].rearrange("p (h t) -> p h t", h=4), ACT.Copy)\
                        .then_inc(gyT_out.sem, 1)
                act.wait_ge(gh_out.sem, gh_out.value(l, NCH))
                act.dma_start(d["gla_p"][bass.ds(l, 1), :, :].rearrange("o p n -> p (o n)"), part(work, 5680, 256))\
                    .then_inc(stored, 16)
                act.wait_ge(gdec_ready.sem, l + 1)
                act.dma_start(d["gla_s"][bass.ds(l, 1), :, :].rearrange("o p n -> p (o n)"), part(hy, 0, 2048))\
                    .then_inc(stored, 16)
                act.wait_ge(gdec_y_mm.sem, l + 1)
                gofv = gof.rearrange("p (h a) t -> p h a t", a=2)
                for a in range(2):
                    last = A(gofv[:, :, a, SEQ:TOK], ps[:, 4 + a, 0:2 * DEC].rearrange("p (h b) -> p h b", h=2), ACT.Copy)
                own.done(last)
                A(gsq, gof, ACT.Square).then_inc(stat_in.sem, 1)
                act.wait_ge(stat_mid.sem, stat_mid.value(l, 2))
                A(rows[0:4, :], rows[0:4, :], ACT.Sqrt).then_inc(stat_root.sem, 1)

                act.dma_start(cbuf[:, 0:3, :, :].rearrange("p i n b -> p (i n b)"), d["conv"][bass.ds(l, 1), :, :]
                              .rearrange("o p n -> p (o n)")).then_inc(conv_in.sem, 16)
                act.dma_start(h0[:, :, :].rearrange("p n b -> p (n b)"), d["lru_state"][bass.ds(l, 1), :, :]
                              .rearrange("o p n -> p (o n)")).then_inc(lru_in.sem, 16)
                act.wait_ge(conv_slot.sem, l + 1)
                act.dma_start(d["conv_p"][bass.ds(l, 1), :, :, :].rearrange("o p n b -> p (o n b)"),
                              cps[:, :, :].rearrange("p n b -> p (n b)")).then_inc(stored, 16)
                act.dma_start(d["conv_s"][bass.ds(l, 1), :, :, :, :].rearrange("o p i n b -> p (o i n b)"),
                              cbuf[:, :, :, :].rearrange("p i n b -> p (i n b)")).then_inc(stored, 16)

                A(mix[:, MIX_SSD:MIX_SSD + 4, :], zt(Z_SG, 4), ACT.Sigmoid)
                act.wait_ge(conv_out.sem, l + 1)
                A(stmp, cx[:, 0:8, :], ACT.Sigmoid).then_inc(ssig.sem, 1)
                act.wait_ge(sdt_x.sem, l + 1)
                own.done(A(acol[0:8, :], pv("a_log", rows=8), ACT.Exp))
                own.done(A(dcum[0:8, :], dtr[0:8, :], ACT.Abs))
                own.done(A(dcum[0:8, :], dcum[0:8, :], ACT.Exp, scale=-1.0))
                A(dcum[0:8, :], dcum[0:8, :], ACT.Ln, bias=1.0).then_inc(sdt_ln.sem, 1)
                act.wait_ge(sdt_c.sem, l + 1)
                A(dedec[0:8, :], dcum[0:8, SEQ:TOK], ACT.Exp).then_inc(sdt.sem, 1)
                act.wait_ge(srow_read.sem, l + 1)
                own.done(A(seg, seg, ACT.Exp))
                own.done(A(ecum[:, :, :], cumT[:, :, :], ACT.Exp))
                own.done(A(wdec[:, :, :], wdec[:, :, :], ACT.Exp))
                A(elast[:, :, :], lastv[:, :, :], ACT.Exp).then_inc(sexps.sem, 1)
                act.wait_ge(stok_mm.sem, l + 1)
                A(xtok, ps[:, 5:7, :], ACT.Copy)
                A(part(zu, TAIL, 512), ps[:, 7, :], ACT.Copy).then_inc(stok.sem, 1)
                for c in range(NCH):
                    act.wait_ge(syT_mm.sem, syT_mm.value(l, c + 1))
                    A(syf[:, :, c * CH:c * CH + CH], ps[:, 7, :].rearrange("p (h t) -> p h t", h=4), ACT.Copy)\
                        .then_inc(syT_out.sem, 1)
                act.wait_ge(sh_out.sem, sh_out.value(l, NCH))
                act.dma_start(d["ssd_p"][bass.ds(l, 1), :, :].rearrange("o p n -> p (o n)"), sst).then_inc(stored, 16)
                act.wait_ge(stored, l * 16 * STORES + 16 * 8)
                act.dma_start(part(hy, 0, 4096), d["ssd_state"][bass.ds(l, 1), :, :]
                              .rearrange("o p n -> p (o n)")).then_inc(sstate_in.sem, 16)
                act.wait_ge(sbc_read.sem, sbc_read.value(l, 3))
                act.dma_start(d["ssd_s"][bass.ds(l, 1), :, :].rearrange("o p n -> p (o n)"), part(hy, 0, 4096))\
                    .then_inc(stored, 16)
                act.wait_ge(sdec_done.sem, l + 1)
                A(ysq, syf, ACT.Square).then_inc(stat_in.sem, 1)
                act.wait_ge(stat_mid.sem, stat_mid.value(l, 3))
                A(rows[0:1, :], rows[0:1, :], ACT.Sqrt).then_inc(stat_root.sem, 1)

                act.wait_ge(ssd_mixed.sem, l + 1)
                act.wait_ge(lra_mm.sem, l + 1)
                for t in range(4):
                    last = A(lr[:, t, :], ps[:, 4 + t, 0:TOK], ACT.Sigmoid, bias=pv("b_a", t))
                last.then_inc(lra.sem, 1)
                act.wait_ge(lri_mm.sem, l + 1)
                for t in range(4):
                    last = A(li[:, t, :], ps[:, 4 + t, 0:TOK], ACT.Sigmoid, bias=pv("b_i", t))
                last.then_inc(lri.sem, 1)
                act.wait_ge(gelu_in.sem, l + 1)
                A(lg, lg, ACT.Sigmoid, scale=GELU_K).then_inc(gelu_sig.sem, 1)
                own.done(A(lamt[:, :], pv("lam", n=4), ACT.Abs))
                own.done(A(lamt[:, :], lamt[:, :], ACT.Exp, scale=-1.0))
                A(lamt[:, :], lamt[:, :], ACT.Ln, bias=1.0).then_inc(lam_abs.sem, 1)
                act.wait_ge(lam_ready.sem, l + 1)
                for t in range(4):
                    A(la[:, t, :], lr[:, t, :], ACT.Exp, scale=lamn[:, t:t + 1])
                    last = A(lth[:, t, :], lr[:, t, :], ACT.Tanh, scale=lam8[:, t:t + 1])
                last.then_inc(lexp.sem, 1)
                act.wait_ge(lmul.sem, l + 1)
                A(lm, lm, ACT.Sqrt).then_inc(lroot.sem, 1)
                act.wait_ge(lru_saved.sem, l + 1)
                act.dma_start(d["lru"][bass.ds(l, 1), :, :, :].rearrange("o p n b -> p (o n b)"),
                              lout[:, :, :].rearrange("p n b -> p (n b)")).then_inc(stored, 16)
                act.wait_ge(stored, l * 16 * STORES + 16 * STORES)
                copy_out(l, NORM_MIX_POST, ZT, 1)
                root(l, NORM_MIX_POST)
                squares(l, NORM_MLP, x_mid)
                root(l, NORM_MLP)
                with act.Fori(0, FT // 4) as g:
                    for j in range(4):
                        act.wait_ge(pre_ready.sem, l * FT + g * 4 + j + 5)
                        A(u[:, bass.ds(g * 4 + j, 1), :].rearrange("p o t -> p (o t)"), pre[:, j, :],
                          ACT.Square).then_inc(u_ready.sem, 1)
                copy_out(l, NORM_MLP_POST, ZT + DT + FT, 4)
                root(l, NORM_MLP_POST)
            act.wait_ge(x_in.sem, (LAYERS + 1) * DT)
            act.dma_start(d["y"], x[:, :, :]).then_inc(stored, 16)
            act.wait_ge(stored, 16 * (LAYERS * STORES + 1))

        @block.gpsimd
        def _(pool):
            own = Own(pool, own_pool)

            def scale_h(l, which, name, ready, j):
                pool.wait_ge(ready.sem, ready.value(l, j + 1))
                nc.gpsimd.tensor_tensor(hy3[:, j, :], x[:, j, :],
                                        pv(name, j).broadcast_to([P, TOK]), ALU.mult).then_inc(h_ready.sem, 1)

            with pool.Fori(0, LAYERS) as l:
                own.restart()
                pool.wait_ge(gains_in.sem, l + 1)
                for j in range(DT):
                    scale_h(l, 0, "mix_pre", x_in, j)
                pool.wait_ge(operands_ready.sem, l + 1)
                for n in range(6):
                    half = n % 2
                    vec = (dec[:, 1, :, half * 4:half * 4 + 4],
                           z[:, Z_V:Z_V + 4, LEAD + SEQ + half * 4:LEAD + SEQ + half * 4 + 4],
                           z[:, Z_R:Z_R + 4, LEAD + SEQ + half * 4:LEAD + SEQ + half * 4 + 4])[n // 2]
                    if n:
                        pool.wait_ge(spread_out.sem, spread_out.value(l, n))
                    nc.gpsimd.tensor_tensor(
                        spread[:, :, :].rearrange("p (b h) m -> p b h m", b=4),
                        cv("pairs").unsqueeze(1).unsqueeze(1).broadcast_to([P, 4, 4, P]),
                        vec.rearrange("p h b -> p b h").unsqueeze(3).broadcast_to([P, 4, 4, P]), ALU.mult)\
                        .then_inc(spread_in.sem, 1)

                pool.wait_ge(conv_slot.sem, l + 1)
                taps = [pv("conv_w", 12 * i, 12).unsqueeze(2).broadcast_to([P, 12, DEC]) for i in range(4)]
                cdec = cx[:, :, SEQ:TOK]
                own.done(nc.gpsimd.tensor_tensor(cdec, cbuf[:, 0, :, :], taps[0], ALU.mult))
                own.done(nc.gpsimd.tensor_tensor(cdec, cdec, pv("conv_b", n=12).unsqueeze(2)
                                                 .broadcast_to([P, 12, DEC]), ALU.add))
                for i in range(1, 4):
                    own.done(nc.gpsimd.tensor_tensor(ctmp, cbuf[:, i, :, :], taps[i], ALU.mult))
                    last = nc.gpsimd.tensor_tensor(cdec, cdec, ctmp, ALU.add)
                    if i < 3:
                        own.done(last)
                last.then_inc(conv_dec.sem, 1)
                for j in range(DT):
                    scale_h(l, 1, "mlp_pre", x_mid, j)

        @block.vector
        def _(dve):
            v = nc.vector
            own = Own(dve, own_dve)

            def inv_rms(l, norm):
                dve.wait_ge(mean_ready.sem, mean_ready.value(l, norm + 1))
                v.tensor_scalar(rstd[:, :], ps[:, STAT, 0:TOK], 1.0 / D_MODEL, EPS, ALU.mult, ALU.add)\
                    .then_inc(rstd_in.sem, 1)
                dve.wait_ge(root_ready.sem, root_ready.value(l, norm + 1))
                own.done(v.reciprocal(rstd[:, :], rstd[:, :]))

            def update_x(l, name, out):
                for j in range(DT):
                    own.done(v.scalar_tensor_tensor(pre[:, j % 4, :], hy3[:, j, :], pv(name, j), rstd[:, :],
                                                    ALU.mult, ALU.mult))
                    v.tensor_tensor(x[:, j, :], x[:, j, :], pre[:, j % 4, :], ALU.add).then_inc(out.sem, 1)

            v.memset(pre[:, 0, 0:1], 0.0).then_inc(bank_free.sem, 4)
            v.memset(pre[:, 1, 0:1], 0.0).then_inc(pre_ready.sem, 4)
            v.memset(pre[:, 1, 1:2], 0.0).then_inc(u_ready.sem, 4)
            v.memset(pre[:, 1, 2:3], 0.0).then_inc(sq_used.sem, 2)
            dve.wait_ge(x_loaded.sem, 16)
            v.memset(pre[:, 2, 0:1], 0.0).then_inc(x_in.sem, DT)
            dve.wait_ge(consts_in.sem, 16)
            with dve.Fori(0, LAYERS) as l:
                own.restart()
                dve.wait_ge(gains_in.sem, l + 1)
                own.done(v.memset(z[:, :, 0:LEAD], 0.0))
                inv_rms(l, NORM_MIX)
                with dve.Fori(0, ZT // 4) as g:
                    for j in range(4):
                        dve.wait_ge(unit_done.sem, l * UNITS + g * 4 + j + 1)
                        v.tensor_tensor(z[:, bass.ds(g * 4 + j, 1), LEAD:ZW].rearrange("p o t -> p (o t)"),
                                        ps[:, j, 0:TOK], rstd[:, :], ALU.mult).then_inc(bank_free.sem, 1)
                dve.wait_ge(bank_free.sem, l * bank_free.per_layer + ZT + 4)
                dve.wait_ge(shift_in.sem, l * 16 + 16)
                own.done(v.tensor_copy(shifted[:, :, :], z[:, 0:RWKV_T, LEAD + SEQ - 1:ZW]))
                v.tensor_tensor(delta[:, :, 0:SEQ], z[:, 0:RWKV_T, LEAD - 1:LEAD - 1 + SEQ],
                                zt(0, RWKV_T, 0, SEQ), ALU.subtract).then_inc(shift_saved.sem, 1)
                own.done(v.tensor_tensor(delta[:, :, SEQ:TOK], prev[:, :, :], zt(0, RWKV_T, SEQ, TOK), ALU.subtract))
                own.done(v.tensor_tensor(delta, delta, pb("mu", RWKV_T), ALU.mult))
                v.tensor_tensor(zt(0, RWKV_T), zt(0, RWKV_T), delta, ALU.add).then_inc(zm_ready.sem, 1)
                dve.wait_ge(zm_ready.sem, l + 1)
                own.done(v.tensor_tensor(kk, zt(Z_K, 4), pb("k_k", 4), ALU.mult))
                dve.wait_ge(decay_sig.sem, l + 1)
                for h in range(4):
                    for c in range(NCH):
                        own.done(v.tensor_tensor_scan(cum[:, h, c, :], ones, sig[:, h, c * CH:c * CH + CH], 0.0,
                                                      ALU.mult, ALU.add))
                own.done(v.tensor_copy(mids[:, :, :], cum[:, :, :, CH // 2 - 1]))
                own.done(v.tensor_tensor(cum, cum, mids[:, :, :].unsqueeze(3).broadcast_to([P, 4, NCH, CH]),
                                         ALU.subtract))
                own.done(v.tensor_copy(ends[:, :, :], cum[:, :, :, CH - 1]))
                v.tensor_tensor(kr[:, :, :, 0, :], cum, sig[:, :, 0:SEQ].rearrange("p h (c t) -> p h c t", c=NCH),
                                ALU.subtract).then_inc(cum_ready.sem, 1)
                dve.wait_ge(rgate_out.sem, l + 1)
                v.tensor_tensor(rk, kk, kk, ALU.mult).then_inc(stat_in.sem, 1)
                dve.wait_ge(stat_root.sem, stat_root.value(l, 1))
                own.done(v.tensor_scalar(rows[0:8, :], rows[0:8, :], 1e-12, None, ALU.max))
                v.reciprocal(rows[0:8, :], rows[0:8, :]).then_inc(stat_row.sem, 1)
                dve.wait_ge(stat_wide.sem, stat_wide.value(l, KK))
                own.done(v.tensor_tensor(kk, kk, ps[:, 4:8, 0:TOK], ALU.mult))
                own.done(v.scalar_tensor_tensor(rk, rate, -1.0, pb("k_a", 4), ALU.add, ALU.mult))
                own.done(v.scalar_tensor_tensor(zt(Z_K, 4), rk, 1.0, zt(Z_K, 4), ALU.add, ALU.mult))
                own.done(v.tensor_tensor(kb, kk, rate, ALU.mult))
                own.done(v.tensor_copy(dec[:, 1, :, :], kk[:, :, SEQ:TOK]))
                own.done(v.tensor_copy(dec[:, 2, :, :], kb[:, :, SEQ:TOK]))
                own.done(v.tensor_tensor(rk, zt(Z_R, 4), zt(Z_K, 4), ALU.mult))
                own.done(v.tensor_tensor(rk, rk, pb("r_k", 4), ALU.mult))
                dve.wait_ge(exps_ready.sem, l + 1)
                chunks = lambda t: t.rearrange("p h (c t) -> p h c t", c=NCH)
                own.done(v.tensor_tensor(bt, kt, chunks(kb[:, :, 0:SEQ]), ALU.mult))
                own.done(v.tensor_tensor(kt, kt, chunks(zt(Z_K, 4, 0, SEQ)), ALU.mult))
                own.done(v.tensor_tensor(kr[:, :, :, 1, :], kr[:, :, :, 1, :], chunks(zt(Z_R, 4, 0, SEQ)), ALU.mult))
                v.tensor_tensor(kr[:, :, :, 0, :], kr[:, :, :, 0, :], chunks(kk[:, :, 0:SEQ]), ALU.mult)\
                    .then_inc(operands_ready.sem, 1)

                def along(vec):
                    return vec.rearrange("p h b -> p b h").unsqueeze(3).broadcast_to([P, vec.shape[2], 4, 64])

                hd4 = hdec.rearrange("p (b h) v -> p b h v", b=DEC)
                td4 = tdec.rearrange("p (b h) v -> p b h v", b=DEC)

                def spread_ps(half):
                    return ps[:, 4 + 2 * half:6 + 2 * half, :].rearrange("p a (b h v) -> p (a b) h v", b=2, h=4)

                for n in range(2):
                    dve.wait_ge(spread_out.sem, spread_out.value(l, n + 1))
                    v.tensor_tensor(td4[:, n * 4:n * 4 + 4], spread_ps(n), along(dec[:, 2, :, n * 4:n * 4 + 4]),
                                    ALU.mult).then_inc(spread_read.sem, 1)
                own.done(v.tensor_tensor(hd4, hd4, along(dec[:, 0, :, :]), ALU.mult))
                own.done(v.tensor_tensor(hdec, hdec, tdec, ALU.subtract))
                for n in range(2):
                    dve.wait_ge(spread_out.sem, spread_out.value(l, n + 3))
                    kn = z[:, Z_K:Z_K + 4, LEAD + SEQ + n * 4:LEAD + SEQ + n * 4 + 4]
                    v.tensor_tensor(td4[:, n * 4:n * 4 + 4], spread_ps(n), along(kn), ALU.mult)\
                        .then_inc(spread_read.sem, 1)
                dve.wait_ge(spread_read.sem, spread_read.value(l, 4))
                v.tensor_tensor(hdec, hdec, tdec, ALU.add).then_inc(rdec_ready.sem, 1)
                for n in range(2):
                    dve.wait_ge(spread_out.sem, spread_out.value(l, n + 5))
                    half = tdec[:, n * 16:n * 16 + 16, :]
                    v.tensor_tensor(half, ps[:, 4 + 2 * n:6 + 2 * n, :].rearrange("p a (i v) -> p (a i) v", v=64),
                                    cv("stack").unsqueeze(1).broadcast_to([P, 16, 64]), ALU.mult)\
                        .then_inc(spread_read.sem, 1)
                dve.wait_ge(spread_read.sem, spread_read.value(l, 6))
                own.done(v.tensor_reduce(dec[:, 0, :, :].rearrange("p h b -> p b h"), td4, AX.X, ALU.add))

                for c in range(NCH):
                    if c == 0:
                        dve.wait_ge(stored, l * 16 * STORES + 32)
                    dve.wait_ge(score1_mm.sem, score1_mm.value(l, c + 1))
                    both = cv("upper_both").unsqueeze(1).broadcast_to([P, 8, 256])
                    v.tensor_tensor(sc1.rearrange("p i j t -> p i (j t)"),
                                    ps[:, 4:8, :].rearrange("p a (i t) -> p (a i) t", i=2), both, ALU.mult)\
                        .then_inc(score1.sem, 1)
                    v.tensor_copy(xx.rearrange("p i j t -> p (i j) t"), ident.unsqueeze(1).broadcast_to([P, 16, P]))\
                        .then_inc(inv_start.sem, 1)
                    dve.wait_ge(score2_mm.sem, score2_mm.value(l, c + 1))
                    v.tensor_tensor(sc2.rearrange("p i j t -> p i (j t)"),
                                    ps[:, 4:8, :].rearrange("p a (i t) -> p (a i) t", i=2), both, ALU.mult)\
                        .then_inc(score2.sem, 1)
                    for j in range(LEVELS):
                        n = (c * LEVELS + j) * 2
                        for half in range(2):
                            dve.wait_ge(q_mm.sem, q_mm.value(l, n + 1 + half))
                            v.tensor_tensor(qb[:, 4 * half:4 * half + 4, :],
                                            ps[:, 4 + half, :].rearrange("p (i t) -> p i t", i=4),
                                            cv("level_low", j * P, P).unsqueeze(1).broadcast_to([P, 4, P]), ALU.mult)\
                                .then_inc(q_out.sem, 1)
                        for half in range(2):
                            dve.wait_ge(dx_mm.sem, dx_mm.value(l, n + 1 + half))
                            xh = xx[:, 4 * half:4 * half + 4].rearrange("p i j t -> p (i j t)")
                            v.tensor_tensor(xh, xh, ps[:, 6:8, :].rearrange("p a t -> p (a t)"), ALU.subtract)\
                                .then_inc(dx_out.sem, 1)
                    dve.wait_ge(ry_mm.sem, ry_mm.value(l, c + 1))
                    hv = ps[:, 6, :].rearrange("p (h m) -> p h m", h=4)
                    for a in range(2):
                        r = slice(64 * a, 64 * a + 64)
                        if c:
                            own.done(v.tensor_tensor(hst[r], hst[r], hv[r, :, 64 * a:64 * a + 64], ALU.add))
                        else:
                            own.done(v.tensor_copy(hst[r], hv[r, :, 64 * a:64 * a + 64]))
                    last = v.tensor_tensor(hst, hst, ends[:, :, c].unsqueeze(2).broadcast_to([P, 4, 64]), ALU.mult)
                    if c < NCH - 1:
                        own.done(last)
                        last = v.tensor_tensor(hst, hst, mids[:, :, c + 1].unsqueeze(2).broadcast_to([P, 4, 64]),
                                               ALU.mult)
                    last.then_inc(rh_out.sem, 1)

                dve.wait_ge(ryT_out.sem, ryT_out.value(l, NCH))
                v.tensor_copy(yfm[:, :, SEQ:TOK], dec[:, 0, :, :]).then_inc(stat_in.sem, 1)
                dve.wait_ge(stat_sum.sem, stat_sum.value(l, MEAN))
                v.tensor_scalar(rows[0:8, :], ps[0:8, 4, 0:TOK], 1.0 / 64, None, ALU.mult).then_inc(stat_row.sem, 1)
                dve.wait_ge(stat_wide.sem, stat_wide.value(l, MEAN))
                v.tensor_tensor(yfm, yfm, ps[:, 4:8, 0:TOK], ALU.subtract).then_inc(centred.sem, 1)
                dve.wait_ge(stat_sum.sem, stat_sum.value(l, VAR))
                v.tensor_scalar(rows[0:8, :], ps[0:8, 4, 0:TOK], 1.0 / 64, LN_EPS, ALU.mult, ALU.add)\
                    .then_inc(stat_mid.sem, 1)
                dve.wait_ge(stat_root.sem, stat_root.value(l, 2))
                v.reciprocal(rows[0:8, :], rows[0:8, :]).then_inc(stat_row.sem, 1)
                dve.wait_ge(stat_wide.sem, stat_wide.value(l, VAR))
                v.tensor_tensor(yfm, yfm, ps[:, 4:8, 0:TOK], ALU.mult).then_inc(stat_in.sem, 1)
                dve.wait_ge(stat_in.sem, stat_in.value(l, BONUS))
                own.done(v.tensor_tensor(yfm, yfm, pb("ln_w", 4), ALU.mult))
                own.done(v.tensor_tensor(yfm, yfm, pb("ln_b", 4), ALU.add))
                dve.wait_ge(stat_sum.sem, stat_sum.value(l, BONUS))
                v.tensor_copy(rows[0:8, :], ps[0:8, 4, 0:TOK]).then_inc(stat_row.sem, 1)
                dve.wait_ge(stat_wide.sem, stat_wide.value(l, BONUS))
                v.tensor_tensor(rk, zt(Z_V, 4), ps[:, 4:8, 0:TOK], ALU.mult).then_inc(bonus_read.sem, 1)
                dve.wait_ge(bonus_read.sem, l + 1)
                own.done(v.tensor_tensor(yfm, yfm, rk, ALU.add))
                own.done(v.tensor_tensor(gate, gate, yfm, ALU.mult))


                dve.wait_ge(ggate_mm.sem, l + 1)
                v.tensor_tensor(glog, ps[:, 4:6, 0:TOK], pb("gla_b", 2), ALU.add).then_inc(ggate_x.sem, 1)
                own.done(v.memset(gsc, 0.0))
                own.done(v.tensor_scalar(zt(Z_GQ, 2), zt(Z_GQ, 2), 0.125, None, ALU.mult))
                dve.wait_ge(gsig.sem, l + 1)
                gate_gla = mix[:, MIX_GLA:MIX_GLA + 4, :]
                own.done(v.tensor_tensor(gate_gla, gate_gla, zt(Z_GG, 4), ALU.mult))
                dve.wait_ge(ggate_ln.sem, l + 1)
                own.done(v.scalar_tensor_tensor(glog, glog, 0.0, gtmp, ALU.min, ALU.subtract))
                for hp in range(2):
                    for c in range(NCH):
                        last = v.tensor_tensor_scan(gcum4[:, hp, c, :], ones, glog[:, hp, c * CH:c * CH + CH], 0.0,
                                                    ALU.mult, ALU.add)
                own.done(last)
                for j in range(LEVELS):
                    b = 1 << j
                    cum_b = gcum.rearrange("p (n m) -> p n m", m=2 * b)
                    v.tensor_tensor(part(hy, j * 512, 512).rearrange("p (n m) -> p n m", m=2 * b), cum_b,
                                    cum_b[:, :, b - 1:b].broadcast_to([P, 256 // b, 2 * b]), ALU.subtract)
                v.tensor_tensor(gkdT, gcum4, gcum4[:, :, :, CH - 1:CH].broadcast_to([P, 2, NCH, CH]), ALU.subtract)\
                    .then_inc(gdist.sem, 1)
                dve.wait_ge(gdist_exp.sem, l + 1)
                gk, gq = zt(Z_GK, 2, 0, SEQ), zt(Z_GQ, 2, 0, SEQ)
                own.done(v.tensor_tensor(kdist, dist, gk.unsqueeze(1).broadcast_to([P, LEVELS, 2, SEQ]), ALU.mult))
                own.done(v.tensor_tensor(dist, dist, gq.unsqueeze(1).broadcast_to([P, LEVELS, 2, SEQ]), ALU.mult))
                own.done(v.tensor_tensor(gqc, gqc, gq.rearrange("p h (c t) -> p h c t", c=NCH), ALU.mult))
                v.tensor_tensor(gkdT, gkdT, gk.rearrange("p h (c t) -> p h c t", c=NCH), ALU.mult)\
                    .then_inc(gops.sem, 1)
                for j in range(LEVELS + 1):
                    mask = cv("level_up", j * P, P) if j < LEVELS else ident
                    dve.wait_ge(glevel_mm.sem, glevel_mm.value(l, j + 1))
                    own.done(v.memset(pre[:, 3, 0:1], 0.0))
                    bank = 4 + 2 * (j % 2)
                    v.copy_predicated(gsc, mask.bitcast(I32).unsqueeze(1).broadcast_to([P, 8, P]),
                                      ps[:, bank:bank + 2, :].rearrange("p a (i t) -> p (a i) t", t=P))\
                        .then_inc(glevel.sem, 1)
                for c in range(NCH):
                    dve.wait_ge(gy_mm.sem, gy_mm.value(l, c + 1))
                    if c:
                        own.done(v.tensor_tensor(gst, gst, glast[:, :, c].unsqueeze(2).broadcast_to([P, 2, P]), ALU.mult))
                    hv = ps[:, 6, :].rearrange("p (h m) -> p h m", h=2)
                    for a in range(2):
                        r = slice(64 * a, 64 * a + 64)
                        if c:
                            last = v.tensor_tensor(gst[r], gst[r], hv[r, :, P * a:P * a + P], ALU.add)
                        else:
                            last = v.tensor_copy(gst[r], hv[r, :, P * a:P * a + P])
                    last.then_inc(gh_out.sem, 1)
                ghd4 = ghd.rearrange("p (b h) v -> p b h v", b=DEC)
                gtd4 = gtd.rearrange("p (b h) v -> p b h v", b=DEC)
                for n in range(4):
                    dve.wait_ge(gval_mm.sem, gval_mm.value(l, n + 1))
                    vals = ps[:, 4 + 2 * (n % 2):6 + 2 * (n % 2), :].rearrange("p b (h a v) -> p b h a v", h=2, a=2)
                    kn = z[:, Z_GK:Z_GK + 2, LEAD + SEQ + n * 2:LEAD + SEQ + n * 2 + 2]\
                        .rearrange("p h b -> p b h").unsqueeze(3).broadcast_to([P, 2, 2, P])
                    for a in range(2):
                        r = slice(64 * a, 64 * a + 64)
                        last = v.tensor_tensor(gtd4[r, n * 2:n * 2 + 2], vals[r, :, :, a, :], kn[r], ALU.mult)
                    last.then_inc(gval_read.sem, 1)
                dve.wait_ge(gstate_in.sem, l * 16 + 16)
                own.done(v.tensor_tensor(ghd4, ghd4, gdec[:, :, :].rearrange("p h b -> p b h").unsqueeze(3)
                                         .broadcast_to([P, DEC, 2, P]), ALU.mult))
                v.tensor_tensor(ghd, ghd, gtd, ALU.add).then_inc(gdec_ready.sem, 1)
                dve.wait_ge(stat_sum.sem, stat_sum.value(l, GLA_RMS))
                v.tensor_scalar(rows[0:4, :], ps[0:4, 4, 0:TOK], 1.0 / P, EPS, ALU.mult, ALU.add)\
                    .then_inc(stat_mid.sem, 1)
                dve.wait_ge(stat_root.sem, stat_root.value(l, 3))
                v.reciprocal(rows[0:4, :], rows[0:4, :]).then_inc(stat_row.sem, 1)
                dve.wait_ge(stat_wide.sem, stat_wide.value(l, GLA_RMS))
                own.done(v.tensor_scalar(gof, gof, pv("gla_norm"), None, ALU.mult))
                own.done(v.tensor_tensor(gof, gof, ps[:, 4:8, 0:TOK], ALU.mult))
                own.done(v.tensor_tensor(gate_gla, gate_gla, gof, ALU.mult))

                dve.wait_ge(conv_in.sem, l * 16 + 16)
                for first, zf, n in ((0, Z_SX, 8), (8, Z_LX, 4)):
                    v.tensor_copy(cps[:, first:first + n, :], z[:, zf:zf + n, LEAD + SEQ - 3:LEAD + SEQ])
                    last = v.tensor_copy(cbuf[:, 3, first:first + n, :], zt(zf, n, SEQ, TOK))
                last.then_inc(conv_slot.sem, 1)
                for i in range(4):
                    for t in range(12):
                        src = z[:, conv_z(t), i:i + SEQ]
                        w = pv("conv_w", 12 * i + t)
                        if i == 0:
                            last = v.tensor_scalar(cx[:, t, 0:SEQ], src, w, pv("conv_b", t), ALU.mult, ALU.add)
                        else:
                            last = v.scalar_tensor_tensor(cx[:, t, 0:SEQ], src, w, cx[:, t, 0:SEQ], ALU.mult, ALU.add)
                    own.done(last)
                dve.wait_ge(conv_dec.sem, l + 1)
                v.tensor_scalar(dtr[0:8, :], z[0:8, Z_DT, LEAD:ZW], pv("dt_bias", rows=8), None, ALU.add)\
                    .then_inc(conv_out.sem, 1)

                dve.wait_ge(conv_out.sem, l + 1)
                gate_ssd = mix[:, MIX_SSD:MIX_SSD + 4, :]
                dve.wait_ge(ssig.sem, l + 1)
                own.done(v.tensor_tensor(gate_ssd, gate_ssd, zt(Z_SG, 4), ALU.mult))
                v.tensor_tensor(cx[:, 0:8, :], cx[:, 0:8, :], stmp, ALU.mult).then_inc(sdt_x.sem, 1)
                dve.wait_ge(sdt_ln.sem, l + 1)
                own.done(v.scalar_tensor_tensor(dtr[0:8, :], dtr[0:8, :], 0.0, dcum[0:8, :], ALU.max, ALU.add))
                own.done(v.tensor_scalar(rows[0:8, :], dtr[0:8, :], acol[0:8, :], -1.0, ALU.mult, ALU.mult))
                for c in range(NCH):
                    last = v.tensor_tensor_scan(dcum[0:8, c * CH:c * CH + CH], ones[0:8, :],
                                                rows[0:8, c * CH:c * CH + CH], 0.0, ALU.mult, ALU.add)
                own.done(last)
                v.tensor_copy(dcum[0:8, SEQ:TOK], rows[0:8, SEQ:TOK]).then_inc(sdt_c.sem, 1)
                dve.wait_ge(sdt_mm.sem, l + 1)
                v.tensor_tensor(xdt, cx[:, 0:4, :], ps[:, 4:8, 0:TOK], ALU.mult).then_inc(sdt_read.sem, 1)
                dve.wait_ge(sdec_mm.sem, l + 1)
                v.tensor_copy(sdec[:, :, :], ps[:, 4, 0:4 * DEC].rearrange("p (h b) -> p h b", h=4))
                v.tensor_copy(cumT[:, :, :], ps[:, 5, 0:NCH * 8].rearrange("p (c h) -> p c h", c=NCH))\
                    .then_inc(sdec_read.sem, 1)
                dve.wait_ge(srow_mm.sem, l + 1)
                rowps = ps[:, 4:8, :].rearrange("p a (i c t) -> p (a i) c t", i=2, c=NCH)
                own.done(v.tensor_copy(lastv[:, :, :], rowps[:, :, :, CH - 1].rearrange("p h c -> p c h")))
                for h in range(8):
                    for c in range(NCH):
                        v.tensor_scalar(seg[:, h, c, :], rowps[:, h, c, :], cumT[:, c, h:h + 1], 0.0,
                                        ALU.subtract, ALU.min)
                v.tensor_tensor(wdec[:, :, :], lastv[:, :, :], cumT[:, :, :], ALU.subtract).then_inc(srow_read.sem, 1)
                dve.wait_ge(ssc_mm.sem, l + 1)
                own.done(v.tensor_tensor(ssc.rearrange("p g c t -> p (g c) t"),
                                         ps[:, 4, :].rearrange("p (i t) -> p i t", i=4),
                                         cv("upper_both", P, P).unsqueeze(1).broadcast_to([P, 4, P]), ALU.mult))
                dve.wait_ge(sexps.sem, l + 1)
                segv = seg.rearrange("p (g h) c t -> p g h (c t)", g=2)
                own.done(v.tensor_tensor(segv, segv, ssc.rearrange("p g c t -> p g (c t)").unsqueeze(2)
                                         .broadcast_to([P, 2, 4, SEQ]), ALU.mult))
                dve.wait_ge(stok.sem, l + 1)
                v.tensor_tensor(xd.rearrange("p c (h v) -> p c h v", h=8), xtok.rearrange("p c (h v) -> p c h v", h=8),
                                wdec[:, :, :].unsqueeze(3).broadcast_to([P, NCH, 8, 64]), ALU.mult)\
                    .then_inc(sops.sem, 1)
                for c in range(NCH):
                    dve.wait_ge(sy_mm.sem, sy_mm.value(l, c + 1))
                    by_head = lambda t: t.rearrange("p (h v) -> p h v", h=8)
                    if c:
                        own.done(v.tensor_tensor(by_head(yoff), by_head(ps[:, 5, :]),
                                                 ecum[:, c, :].unsqueeze(2).broadcast_to([P, 8, 64]), ALU.mult))
                        v.tensor_tensor(syt, yoff, ps[:, 4, :], ALU.add).then_inc(sy_out.sem, 1)
                        own.done(v.tensor_tensor(by_head(sst), by_head(sst),
                                                 elast[:, c, :].unsqueeze(2).broadcast_to([P, 8, 64]), ALU.mult))
                        v.tensor_tensor(sst, sst, ps[:, 6, :], ALU.add).then_inc(sh_out.sem, 1)
                    else:
                        v.tensor_copy(syt, ps[:, 4, :]).then_inc(sy_out.sem, 1)
                        v.tensor_copy(sst, ps[:, 6, :]).then_inc(sh_out.sem, 1)
                dve.wait_ge(sstate_in.sem, l * 16 + 16)
                shd4 = shd.rearrange("p (b h) n -> p b h n", b=DEC)
                own.done(v.tensor_tensor(shd4, shd4, sdec[:, :, :].rearrange("p h b -> p b h").unsqueeze(3)
                                         .broadcast_to([P, DEC, 4, P]), ALU.mult))
                std4 = std.rearrange("p (b h) n -> p b h n", b=4)
                for n in range(4):
                    b0 = (n % 2) * 4
                    dve.wait_ge(sbc_mm.sem, sbc_mm.value(l, n + 1))
                    bc = ps[:, 4 + 2 * (n % 2):6 + 2 * (n % 2), :].rearrange("p a (b g n) -> p (a b) g n", b=2, g=2)
                    for g in range(2):
                        hs = slice(2 * g, 2 * g + 2)
                        other = xdt[:, hs, SEQ + b0:SEQ + b0 + 4].rearrange("p h b -> p b h").unsqueeze(3)\
                            .broadcast_to([P, 4, 2, P]) if n < 2 else shd4[:, b0:b0 + 4, hs, :]
                        last = v.tensor_tensor(std4[:, :, hs, :], bc[:, :, g, :].unsqueeze(2).broadcast_to([P, 4, 2, P]),
                                               other, ALU.mult)
                    if n < 2:
                        own.done(last)
                        v.tensor_tensor(shd4[:, b0:b0 + 4], shd4[:, b0:b0 + 4], std4, ALU.add)\
                            .then_inc(sbc_read.sem, 1)
                        dve.wait_ge(sbc_read.sem, sbc_read.value(l, n + 1))
                    else:
                        last.then_inc(sbc_read.sem, 1)
                        dve.wait_ge(sbc_read.sem, sbc_read.value(l, n + 1))
                        own.done(v.tensor_reduce(syf[:, :, SEQ + b0:SEQ + b0 + 4].rearrange("p h b -> p b h"), std4,
                                                 AX.X, ALU.add))
                dve.wait_ge(syT_out.sem, syT_out.value(l, NCH))
                own.done(v.tensor_tensor(cx[:, 0:4, :], cx[:, 0:4, :], pb("d_skip", 4), ALU.mult))
                own.done(v.tensor_tensor(syf, syf, cx[:, 0:4, :], ALU.add))
                v.tensor_tensor(syf, syf, gate_ssd, ALU.mult).then_inc(sdec_done.sem, 1)
                dve.wait_ge(stat_sum.sem, stat_sum.value(l, SSD_RMS))
                v.tensor_scalar(rows[0:1, :], ps[0:1, 4, 0:TOK], 1.0 / 512, EPS, ALU.mult, ALU.add)\
                    .then_inc(stat_mid.sem, 1)
                dve.wait_ge(stat_root.sem, stat_root.value(l, 4))
                v.reciprocal(rows[0:1, :], rows[0:1, :]).then_inc(stat_row.sem, 1)
                own.done(v.tensor_tensor(syf, syf, pb("ssd_norm", 4), ALU.mult))
                dve.wait_ge(stat_wide.sem, stat_wide.value(l, SSD_RMS))
                v.tensor_tensor(gate_ssd, syf, ps[:, 4, 0:TOK].unsqueeze(1).broadcast_to([P, 4, TOK]), ALU.mult)\
                    .then_inc(ssd_mixed.sem, 1)

                dve.wait_ge(stored, l * 16 * STORES + 16 * 9)
                dve.wait_ge(lru_in.sem, l * 16 + 16)
                lgz = zt(Z_LG, 4)
                own.done(v.tensor_tensor(lg, lgz, lgz, ALU.mult))
                own.done(v.tensor_scalar(lg, lg, 0.044715, 1.0, ALU.mult, ALU.add))
                v.tensor_tensor(lg, lg, lgz, ALU.mult).then_inc(gelu_in.sem, 1)
                own.done(v.tensor_scalar(lam8[:, :], pv("lam", n=4), -1.0, 0.0, ALU.mult, ALU.max))
                dve.wait_ge(lam_abs.sem, l + 1)
                own.done(v.tensor_tensor(lam8[:, :], lam8[:, :], lamt[:, :], ALU.add))
                own.done(v.tensor_scalar(lamn[:, :], lam8[:, :], -LRU_C, None, ALU.mult))
                v.tensor_scalar(lam8[:, :], lam8[:, :], LRU_C, None, ALU.mult).then_inc(lam_ready.sem, 1)
                dve.wait_ge(gelu_sig.sem, l + 1)
                own.done(v.tensor_tensor(lgz, lgz, lg, ALU.mult))
                dve.wait_ge(lexp.sem, l + 1)
                own.done(v.tensor_scalar(lm, lth, 1.0, None, ALU.add))
                own.done(v.reciprocal(lm, lm))
                v.scalar_tensor_tensor(lm, lm, 2.0, lth, ALU.mult, ALU.mult).then_inc(lmul.sem, 1)
                own.done(v.tensor_tensor(li, li, cx[:, 8:12, :], ALU.mult))
                dve.wait_ge(lroot.sem, l + 1)
                own.done(v.memset(lm[:, :, 0:1], 1.0))
                own.done(v.tensor_tensor(li, li, lm, ALU.mult))
                for t in range(4):
                    v.tensor_tensor_scan(lh[:, t, 0:SEQ], la[:, t, 0:SEQ], li[:, t, 0:SEQ], 0.0, ALU.mult, ALU.add)
                own.done(v.tensor_tensor(lh[:, :, SEQ:TOK], la[:, :, SEQ:TOK], h0[:, :, :], ALU.mult))
                own.done(v.tensor_tensor(lh[:, :, SEQ:TOK], lh[:, :, SEQ:TOK], li[:, :, SEQ:TOK], ALU.add))
                v.tensor_copy(lout[:, :, :], lh[:, :, SEQ - 1:TOK]).then_inc(lru_saved.sem, 1)
                v.tensor_tensor(mix[:, MIX_LRU:MIX_LRU + 4, :], lh, lgz, ALU.mult).then_inc(mixed.sem, 1)
                inv_rms(l, NORM_MIX_POST)
                update_x(l, "mix_post", x_mid)
                inv_rms(l, NORM_MLP)
                with dve.Fori(0, FT // 4) as g:
                    for j in range(4):
                        dve.wait_ge(unit_done.sem, l * UNITS + ZT + DT + g * 4 + j + 1)
                        dve.wait_ge(u_ready.sem, l * FT + g * 4 + j + 1)
                        v.scalar_tensor_tensor(pre[:, j, :], ps[:, j, 0:TOK], 0.0, rstd[:, :],
                                               ALU.max, ALU.mult).then_inc(pre_ready.sem, 1)
                inv_rms(l, NORM_MLP_POST)
                update_x(l, "mlp_post", x_in)


def _tiles(a):
    return np.swapaxes(a.reshape(a.shape[:-1] + (-1, P)), -1, -2)


def _weights(w_in, w_out, w_up, w_down):
    L = LAYERS
    gla, lru, rwkv, ssd = 0, 1552, 2576, 4368
    out = np.zeros((L, UNITS, P, DT, P), np.float32)

    def columns(first, w):
        n = w.shape[2] // P
        out[:, first:first + n] = w.reshape(L, DT, P, n, P).transpose(0, 3, 2, 1, 4)

    columns(Z_R, w_in[:, :, rwkv:rwkv + 14 * P])
    columns(Z_GQ, w_in[:, :, gla:gla + 12 * P])
    out[:, Z_GA, :, :, 0:16] = w_in[:, :, gla + 12 * P:gla + 12 * P + 16].reshape(L, DT, P, 16).transpose(0, 2, 1, 3)
    columns(Z_SG, w_in[:, :, ssd:ssd + 12 * P])
    out[:, Z_DT, :, :, 0:8] = w_in[:, :, ssd + 12 * P:ssd + 12 * P + 8].reshape(L, DT, P, 8).transpose(0, 2, 1, 3)
    columns(Z_LX, w_in[:, :, lru:lru + 8 * P])
    columns(ZT, w_out)
    columns(ZT + DT, w_up)
    down = w_down.reshape(L, FT // DT, DT, P, DT, P).transpose(0, 4, 1, 3, 2, 5)
    out[:, ZT + DT + FT:] = down.reshape(L, FT, P, DT, P)
    return out.reshape(L * UNITS, P, DT * P)


def _params(i):
    L = LAYERS
    out = np.zeros((L, P, N_PARAM), np.float32)

    def put(name, a):
        at, n = PARAM[name]
        out[:, 0:a.shape[1], at:at + a.shape[2]] = a

    def block(w):
        full = np.zeros((L, P, 4, P), np.float32)
        full[:, 0:64, :, 0:64] = w[:, 0::2].transpose(0, 2, 1, 3)
        full[:, 64:, :, 64:] = w[:, 1::2].transpose(0, 2, 1, 3)
        return full.reshape(L, P, 512)

    for name, key in [("mix_pre", "norm_mix_pre"), ("mix_post", "norm_mix_post"), ("mlp_pre", "norm_mlp_pre"),
                      ("mlp_post", "norm_mlp_post"), ("mu", "rwkv_mu"), ("w0", "rwkv_w0"), ("a0", "rwkv_a0"),
                      ("k_k", "rwkv_k_k"), ("k_a", "rwkv_k_a"), ("ln_w", "rwkv_ln_w"), ("ln_b", "rwkv_ln_b"),
                      ("gla_b", "gla_b_gate"), ("gla_norm", "gla_norm"), ("b_a", "lru_b_a"), ("b_i", "lru_b_i"),
                      ("lam", "lru_lambda"), ("ssd_norm", "ssd_norm")]:
        put(name, _tiles(i[key]))
    put("r_k", _tiles(i["rwkv_r_k"].reshape(L, 512)))
    put("d_skip", _tiles(np.repeat(i["ssd_d"], 64, axis=1)))
    put("conv_b", np.concatenate([_tiles(i["ssd_conv_b"]), _tiles(i["lru_conv_b"])], 2))
    conv = np.concatenate([_tiles(i["ssd_conv_w"]), _tiles(i["lru_conv_w"])], 3)
    put("conv_w", conv.transpose(0, 2, 1, 3).reshape(L, P, 48))
    put("dt_bias", i["ssd_dt_bias"][:, :, None])
    put("a_log", i["ssd_a_log"][:, :, None])
    put("wa2", np.concatenate([i["rwkv_w2"], i["rwkv_a2"]], 1))
    put("g2", i["rwkv_g2"])
    put("gate2", i["gla_w_gate2"])
    put("lru_wa", block(i["lru_w_a"]))
    put("lru_wi", block(i["lru_w_i"]))
    return out


def _consts():
    out = np.zeros((P, N_CONST), np.float32)

    def put(name, a):
        at, n = CONST[name]
        out[0:a.shape[0], at:at + n] = a.reshape(a.shape[0], n)

    i = np.arange(P)
    put("ident", np.eye(P))
    put("ones", np.ones((P, P)))
    put("pairs", i[:, None] // 64 == i[None, :] // 64)
    put("stack", i[:, None] % 64 == np.arange(64)[None, :])
    h = np.arange(8)
    put("head_sum", (2 * np.arange(4)[None, :, None] + i[:, None, None] // 64) == h[None, None, :])
    put("head_row", (2 * np.arange(4)[None, :, None] + i[None, None, :] // 64) == h[:, None, None])
    put("tile_sum", np.broadcast_to(np.arange(4)[None, :, None] == np.arange(4)[None, None, :], (P, 4, 4)))
    up = i[:, None] <= i[None, :]
    put("upper_both", np.concatenate([i[:, None] < i[None, :], up], 1))
    lv = []
    for j in range(LEVELS):
        b = 1 << j
        s, t = i[:, None], i[None, :]
        lv.append((s // (2 * b) == t // (2 * b)) & (s // b % 2 == 0) & (t // b % 2 == 1))
    lv = np.stack(lv)
    put("level_up", lv.transpose(1, 0, 2))
    put("level_low", lv.transpose(2, 0, 1))
    return out


def _keyed(s):
    L, B, H, K, V = s.shape
    return s.reshape(L, B, H // 2, 2, K, V).transpose(0, 3, 4, 1, 2, 5).reshape(L, P, B * (H // 2) * V)


def kernel(**inputs):
    import concourse.bacc as bacc
    from concourse.bass_utils import run_bass_kernel_spmd

    i = {k: np.asarray(v) for k, v in inputs.items()}
    L = LAYERS
    x = np.concatenate([i["x_prompt"][0], i["x_sample"][:, 0]], 0)
    conv = np.concatenate([_tiles(i["cache_ssd_conv"]), _tiles(i["cache_lru_conv"])], 4)
    arrays = {
        "x": x.T.reshape(DT, P, TOK).transpose(1, 0, 2),
        "weights": _weights(i["w_in"], i["w_out"], i["w_up"], i["w_down"]),
        "params": _params(i),
        "consts": _consts(),
        "gla_state": _keyed(i["state_gla"]),
        "rwkv_state": _keyed(i["state_rwkv"].transpose(0, 1, 2, 4, 3)),
        "ssd_state": _keyed(i["state_ssd"]),
        "lru_state": i["state_lru"].reshape(L, DEC, 4, P).transpose(0, 3, 2, 1).reshape(L, P, 4 * DEC),
        "shift": i["cache_rwkv_shift"].reshape(L, DEC, RWKV_T, P).transpose(0, 3, 2, 1).reshape(L, P, RWKV_T * DEC),
        "conv": conv.transpose(0, 3, 2, 4, 1).reshape(L, P, 3 * 12 * DEC),
    }
    outs = {
        "y": (P, DT, TOK), "gla_p": (L, P, 256), "gla_s": (L, P, 2048), "lru": (L, P, 4, 9),
        "shift_out": (L, P, RWKV_T, 9), "rwkv_p": (L, P, 256), "rwkv_s": (L, P, 2048),
        "conv_p": (L, P, 12, 3), "conv_s": (L, P, 4, 12, DEC), "ssd_p": (L, P, 512), "ssd_s": (L, P, 4096),
    }
    nc = bacc.Bacc("TRN2", target_bir_lowering=False, num_devices=1)
    feed, aps = {}, {}
    for name, a in arrays.items():
        feed["in_" + name] = np.ascontiguousarray(a)
        aps[name] = nc.dram_tensor("in_" + name, a.shape, F32, kind="ExternalInput").ap()
    for name, shape in outs.items():
        aps[name] = nc.dram_tensor("out_" + name, shape, F32, kind="ExternalOutput").ap()
    build(nc, aps)
    r = run_bass_kernel_spmd(nc, [feed], core_ids=[0])
    o = {name: r.results[0]["out_" + name] for name in outs}

    def unkeyed(s, B, hp):
        s = s.reshape(L, 2, 64, B, hp, -1).transpose(0, 3, 4, 1, 2, 5)
        return np.ascontiguousarray(s.reshape(L, B, 2 * hp, 64, -1))

    y = o["y"].transpose(2, 1, 0).reshape(TOK, D_MODEL)
    lru = o["lru"].transpose(0, 3, 2, 1).reshape(L, 9, 512)
    shift = o["shift_out"].transpose(0, 3, 2, 1).reshape(L, 9, RWKV_T * P)
    conv_p = o["conv_p"].transpose(0, 3, 2, 1).reshape(L, 1, 3, 12 * P)
    conv_s = o["conv_s"].transpose(0, 4, 2, 3, 1).reshape(L, DEC, 4, 12 * P)[:, :, 1:]
    ssd_p = o["ssd_p"].reshape(L, 1, P, 8, 64).transpose(0, 1, 3, 4, 2)
    c = np.ascontiguousarray
    return (c(y[None, :SEQ]), c(y[SEQ:, None]),
            unkeyed(o["gla_p"], 1, 2), unkeyed(o["gla_s"], DEC, 2),
            c(lru[:, 0:1]), c(lru[:, 1:]),
            c(conv_p[..., 1024:]), c(conv_s[..., 1024:]),
            c(shift[:, 0:1]), c(shift[:, 1:]),
            c(unkeyed(o["rwkv_p"], 1, 4).swapaxes(3, 4)), c(unkeyed(o["rwkv_s"], DEC, 4).swapaxes(3, 4)),
            c(conv_p[..., :1024]), c(conv_s[..., :1024]),
            c(ssd_p), unkeyed(o["ssd_s"], DEC, 4))
```

```python
import math
from contextlib import ExitStack

import numpy as np

import concourse.bass as bass
from concourse import mybir

F32 = mybir.dt.float32
F32R = mybir.dt.float32r
I32 = mybir.dt.int32
ALU = mybir.AluOpType
ACT = mybir.ActivationFunctionType
AX = mybir.AxisListType

P = 128
LAYERS = 2
SEQ, DEC = 256, 8
TOK = SEQ + DEC
CH = 128
NCH = SEQ // CH
LEAD = 3
ZW = LEAD + TOK
D_MODEL, D_FF = 2048, 8192
DT, FT = D_MODEL // P, D_FF // P
EPS = 1e-6
LN_EPS = 64e-5
DECAY = math.exp(-0.5)
LRU_C = 8.0
GATE_TEMP = 16.0
GELU_K = 2.0 * math.sqrt(2.0 / math.pi)
LEVELS = 7

Z_R, Z_K, Z_V, Z_WA, Z_G = 0, 4, 8, 12, 13
Z_GQ, Z_GK, Z_GV, Z_GG, Z_GA = 14, 16, 18, 22, 26
Z_SG, Z_SX, Z_SB, Z_SC, Z_DT = 27, 31, 35, 37, 39
Z_LX, Z_LG = 40, 44
ZT = 48
RWKV_T, GLA_T, SSD_T = 14, 27, 40
MIX_GLA, MIX_LRU, MIX_RWKV, MIX_SSD = 0, 4, 8, 12

UNITS = ZT + DT + FT + FT
SPLIT = DT + FT + FT
QUARTERS = FT // DT
RING = 4


def places(fields):
    at, out = 0, {}
    for name, n in fields:
        out[name] = (at, n)
        at += n
    return out, at


PARAM, N_PARAM = places([
    ("mix_pre", 16), ("mix_post", 16), ("mlp_pre", 16), ("mlp_post", 16),
    ("mu", 14), ("w0", 4), ("a0", 4), ("k_k", 4), ("k_a", 4), ("r_k", 4), ("ln_w", 4), ("ln_b", 4),
    ("gla_b", 2), ("gla_norm", 1),
    ("conv_b", 12), ("conv_w", 48), ("b_a", 4), ("b_i", 4), ("lam", 4),
    ("dt_bias", 1), ("a_log", 1), ("d_skip", 4), ("ssd_norm", 4),
    ("wa2", 512), ("g2", 512), ("gate2", 256), ("lru_wa", 512), ("lru_wi", 512)])

N_GAIN = PARAM["wa2"][0]
WORK = 5936
STORES = 10

CONST, N_CONST = places([
    ("ident", 128), ("ones", 128), ("pairs", 128), ("stack", 64), ("head_sum", 32), ("head_row", 512), ("tile_sum", 16),
    ("upper_both", 256), ("level_up", LEVELS * 128), ("level_low", LEVELS * 128)])


class Signal:

    def __init__(self, sem, per_layer):
        self.sem, self.per_layer = sem, per_layer

    def value(self, layer, n):
        return layer * self.per_layer + n


class Own:

    def __init__(self, engine, sem):
        self.engine, self.sem, self.n = engine, sem, 0

    def restart(self):
        self.engine.sem_clear(self.sem)
        self.n = 0

    def done(self, instruction):
        instruction.then_inc(self.sem, 1)
        self.n += 1
        self.engine.wait_ge(self.sem, self.n)


def build(nc, d):
    ctx = ExitStack()
    with ctx:
        def sbuf(name, *shape):
            address[name] = -(-nc.sbuf_base // 32) * 32
            return ctx.enter_context(nc.sbuf_tensor(name, [P, *shape], F32))

        def rounded(name, over, first, *shape):
            return nc.alloc_sbuf_tensor_at(name, [P, *shape], F32R, offset=address[over] + 4 * first)

        address = {}

        def signal(name, per_layer=1):
            return Signal(ctx.enter_context(nc.semaphore(name)), per_layer)

        ring = sbuf("ring", RING, DT * P)
        x = sbuf("x", DT, TOK)
        hy = sbuf("hy", DT * TOK)
        mix = sbuf("mix", DT, TOK)
        zu = sbuf("zu", FT * TOK)
        work = sbuf("work", WORK)
        const = sbuf("const", N_CONST)
        par = sbuf("par", N_PARAM)
        gains = sbuf("gains", LAYERS, N_GAIN)
        sq = sbuf("sq", 2, TOK)
        rstd = sbuf("rstd", TOK)
        pre = sbuf("pre", 4, TOK)
        pool_mark = sbuf("pool_mark", 1)
        ps = ctx.enter_context(nc.psum_tensor("ps", [P, 8, 512], F32))

        xs = x[:, :, :].rearrange("p n t -> p (n t)")
        hy3 = hy[:, :].rearrange("p (n t) -> p n t", t=TOK)
        y3 = mix[:, :, :]
        z = zu[:, 0:ZT * ZW].rearrange("p (n t) -> p n t", t=ZW)
        TAIL = ZT * ZW

        def part(t, at, *dims):
            n = int(np.prod(dims))
            v = t[:, at:at + n]
            if len(dims) == 2:
                return v.rearrange("p (a b) -> p a b", a=dims[0])
            if len(dims) == 3:
                return v.rearrange("p (a b c) -> p a b c", a=dims[0], b=dims[1])
            return v

        w_hi = rounded("w_hi", "zu", 0, 2, DT * P)
        w_lo = rounded("w_lo", "ring", 0, RING, DT * P)
        u_hi = rounded("u_hi", "zu", 2 * DT * P, DT, TOK)
        u_lo = rounded("u_lo", "zu", 2 * DT * P + DT * TOK, DT, TOK)
        mix_hi, mix_lo = u_hi, rounded("mix_lo", "mix", 0, DT, TOK)
        h_hi = rounded("h_hi", "zu", 2 * DT * P + 2 * DT * TOK, DT, TOK)
        h_lo = rounded("h_lo", "hy", 0, DT, TOK)
        in_w_hi = rounded("in_w_hi", "work", 0, 2, DT * P)
        in_h_hi = rounded("in_h_hi", "mix", 0, DT, TOK)
        in_h_lo = rounded("in_h_lo", "x", 0, DT, TOK)

        def f32(view):
            return view.bitcast(F32)

        def zt(tile, n=1, first=0, last=TOK):
            return z[:, tile:tile + n, LEAD + first:LEAD + last]

        def pv(name, j=0, n=1, rows=P):
            at = PARAM[name][0]
            return par[0:rows, at + j:at + j + n]

        def pb(name, n, tokens=TOK):
            at = PARAM[name][0]
            return par[:, at:at + n].unsqueeze(2).broadcast_to([P, n, tokens])

        def cv(name, at=0, n=None, rows=P):
            first, size = CONST[name]
            n = size if n is None else n
            return const[0:rows, first + at:first + at + n]

        ident = cv("ident")
        ones = cv("ones")

        loaded = [ctx.enter_context(nc.semaphore(f"weights_loaded_{j}")) for j in range(RING)]
        unit_done = signal("unit_done", UNITS)
        bank_free = signal("bank_free", UNITS)
        x_loaded = signal("x_loaded")
        gains_loaded = signal("gains_loaded")
        own_act, own_pool, own_dve = (ctx.enter_context(nc.semaphore(n)) for n in ("own_act", "own_pool", "own_dve"))
        consts_in = signal("consts_in")
        gains_in = signal("gains_in")
        matrices_in = signal("matrices_in", 16)
        rstd_in = signal("rstd_in", 4)
        x_saved, x_back = signal("x_saved", 16), signal("x_back", 16)
        z_ready = signal("z_ready", ZT - RWKV_T)
        x_in = signal("x_in", DT)
        x_mid = signal("x_mid", DT)
        h_ready = signal("h_ready", 2 * DT)
        sq_ready = signal("sq_ready", 4 * DT)
        sq_used = signal("sq_used", 4 * (DT - 1))
        mean_ready = signal("mean_ready", 4)
        root_ready = signal("root_ready", 4)
        hi_ready, lo_ready = signal("hi_ready", SPLIT), signal("lo_ready", SPLIT)
        in_hi_ready, in_lo_ready = signal("in_hi_ready", RWKV_T), signal("in_lo_ready", RWKV_T)
        in_h_hi_ready, in_h_split = signal("in_h_hi_ready", 4), signal("in_h_split", 4)
        mix_hi_ready, mix_split = signal("mix_hi_ready", 3), signal("mix_split", 2)
        h_hi_ready, h_split = signal("h_hi_ready", 4), signal("h_split", 4)
        u_hi_ready, u_split = signal("u_hi_ready", FT), signal("u_split", FT)
        y_clear = signal("y_clear")
        mixed = signal("mixed")
        stored = ctx.enter_context(nc.semaphore("stored"))
        n_stored = [0]
        stat_in = signal("stat_in", 6)
        stat_sum = signal("stat_sum", 6)
        stat_row = signal("stat_row", 6)
        stat_wide = signal("stat_wide", 6)
        stat_mid = signal("stat_mid", 3)
        stat_root = signal("stat_root", 4)
        KK, MEAN, VAR, BONUS, GLA_RMS, SSD_RMS = range(1, 7)
        rows = pre[:, 0, :]

        shift_in = signal("shift_in", 16)
        zm_ready = signal("zm_ready")
        lowrank_in = signal("lowrank_in")
        decay_mm, decay_sig = signal("decay_mm"), signal("decay_sig")
        rate_mm, rate_sig = signal("rate_mm"), signal("rate_sig")
        rgate_mm, rgate_out = signal("rgate_mm"), signal("rgate_out")
        cum_ready, exps_ready = signal("cum_ready"), signal("exps_ready")
        operands_ready = signal("operands_ready")
        rstate_in = signal("rstate_in", 16)
        spread_in = signal("spread_in", 6)
        spread_out = signal("spread_out", 6)
        spread_read = signal("spread_read", 6)
        rdec_ready = signal("rdec_ready")
        score1_mm, score1 = signal("score1_mm", NCH), signal("score1", NCH)
        score2_mm, score2 = signal("score2_mm", NCH), signal("score2", NCH)
        rtok_mm, rtok = signal("rtok_mm", NCH), signal("rtok", NCH)
        N_INV = NCH * LEVELS * 2
        q_mm, q_out = signal("q_mm", N_INV), signal("q_out", N_INV)
        dx_mm, dx_out = signal("dx_mm", N_INV - 2 * NCH), signal("dx_out", N_INV)
        rhs_mm, rhs_out = signal("rhs_mm", NCH), signal("rhs_out", NCH)
        u_mm, un_out = signal("u_mm", NCH), signal("un_out", NCH)
        ry_mm, ry_out = signal("ry_mm", NCH), signal("ry_out", NCH)
        rh_out = signal("rh_out", NCH)
        ryT_mm, ryT_out = signal("ryT_mm", NCH), signal("ryT_out", NCH)
        centred, bonus_read = signal("centred"), signal("bonus_read")
        shift_saved = signal("shift_saved")

        prev = sbuf("prev", RWKV_T, DEC)
        shifted = sbuf("shifted", RWKV_T, DEC + 1)
        mids, ends = sbuf("mids", 4, NCH), sbuf("ends", 4, NCH)
        dec = sbuf("dec", 3, 4, DEC)

        sig = part(zu, TAIL, 4, TOK)
        rate = part(zu, TAIL + 1056, 4, TOK)
        kk = part(zu, TAIL + 2112, 4, TOK)
        mixf = mix[:, :, :].rearrange("p n t -> p (n t)")
        cum = part(mixf, 0, 4, NCH, CH)
        kb = part(mixf, 1024, 4, TOK)
        gate = mix[:, MIX_RWKV:MIX_RWKV + 4, :]
        kr = work[:, 0:2048].rearrange("p (h c j t) -> p h c j t", h=4, c=NCH, j=2)
        kt = part(work, 2048, 4, NCH, CH)
        bt = part(work, 3072, 4, NCH, CH)
        yfm = part(work, 4096, 4, TOK)
        rk = mix[:, MIX_SSD:MIX_SSD + 4, :]
        delta = part(xs, 0, RWKV_T, TOK)
        hdec = part(xs, 0, 32, 64)
        tdec = part(xs, 2048, 32, 64)
        spread = part(zu, TAIL, 16, P)
        sc1 = part(xs, 0, 8, 2, P)
        sc2 = part(xs, 2048, 8, 2, P)
        vt, ktt, btt = (part(mixf, 512 * j, 512) for j in range(3))
        un = part(mixf, 1536, 4, 2, 64)
        xx = part(zu, TAIL, 8, 2, P)
        qb = part(zu, TAIL + 2048, 8, P)
        yt = part(zu, TAIL + 3072, 512)
        hst = part(zu, TAIL + 3584, 4, 64)

        ggate_mm, ggate_x, ggate_ln = signal("ggate_mm"), signal("ggate_x"), signal("ggate_ln")
        gdist, gdist_exp, gops = signal("gdist"), signal("gdist_exp"), signal("gops")
        gtok_mm, gtok = signal("gtok_mm"), signal("gtok")
        glevel_mm, glevel = signal("glevel_mm", LEVELS + 1), signal("glevel", LEVELS + 1)
        gy_mm, gy_out, gh_out = signal("gy_mm", NCH), signal("gy_out", NCH), signal("gh_out", NCH)
        gyT_mm, gyT_out = signal("gyT_mm", NCH), signal("gyT_out", NCH)
        gstate_in = signal("gstate_in", 16)
        gval_mm, gval_read = signal("gval_mm", 4), signal("gval_read", 4)
        gdec_ready, gdec_y_mm = signal("gdec_ready"), signal("gdec_y_mm")
        gsig = signal("gsig")
        glast, gdec = sbuf("glast", 2, NCH), sbuf("gdec", 2, DEC)
        dist = part(xs, 0, LEVELS, 2, SEQ)
        kdist = part(zu, TAIL, LEVELS, 2, SEQ)
        gyt = part(xs, 3584, 512)
        glog = part(work, 0, 2, TOK)
        gcum = part(work, 528, 512)
        gcum4 = part(work, 528, 2, NCH, CH)
        gsc = part(work, 1040, 8, P)
        gvt = part(work, 2064, NCH, 512)
        gkdT = part(work, 3088, 2, NCH, CH)
        gkd = part(work, 3600, NCH, 256)
        gqc = part(work, 4112, 2, NCH, CH)
        gof = part(work, 4624, 4, TOK)
        gtmp = part(work, 4624, 2, TOK)
        gst = part(work, 5680, 2, P)
        ghd = part(xs, 0, 16, P)
        gtd = part(zu, TAIL, 16, P)
        gsq = part(zu, TAIL + 2048, 4, TOK)

        conv_in = signal("conv_in", 16)
        conv_slot, conv_dec, conv_out = signal("conv_slot"), signal("conv_dec"), signal("conv_out")
        lconv_slot, lconv_out = signal("lconv_slot"), signal("lconv_out")
        cbuf = sbuf("cbuf", 4, 12, DEC)
        cps = sbuf("cps", 12, 3)
        cx = part(work, 0, 12, TOK)
        ctmp = part(work, 3168, 12, DEC)
        conv_z = lambda t: Z_SX + t if t < 8 else Z_LX + t - 8

        ssig = signal("ssig")
        sdt_x, sdt_ln, sdt_c, sdt = signal("sdt_x"), signal("sdt_ln"), signal("sdt_c"), signal("sdt")
        sdt_mm, sdt_read = signal("sdt_mm"), signal("sdt_read")
        sdec_mm, sdec_read = signal("sdec_mm"), signal("sdec_read")
        srow_mm, srow_read, sexps = signal("srow_mm"), signal("srow_read"), signal("sexps")
        ssc_mm = signal("ssc_mm")
        stok_mm, stok, sops = signal("stok_mm"), signal("stok"), signal("sops")
        sy_mm, sy_out, sh_out = signal("sy_mm", NCH), signal("sy_out", NCH), signal("sh_out", NCH)
        syT_mm, syT_out = signal("syT_mm", NCH), signal("syT_out", NCH)
        sstate_in = signal("sstate_in", 16)
        sbc_mm, sbc_read = signal("sbc_mm", 4), signal("sbc_read", 4)
        sdec_done = signal("sdec_done")
        dtr, dcum = pre[:, 1, :], pre[:, 2, :]
        acol = sbuf("acol", 1)
        dedec, sdec = sbuf("dedec", DEC), sbuf("sdec", 4, DEC)
        cumT, lastv = sbuf("cumT", NCH, 8), sbuf("lastv", NCH, 8)
        wdec, ecum, elast = sbuf("wdec", NCH, 8), sbuf("ecum", NCH, 8), sbuf("elast", NCH, 8)
        seg = part(xs, 0, 8, NCH, CH)
        xtok = part(xs, 2048, NCH, 512)
        syt = part(xs, 3072, 512)
        sst = part(xs, 3584, 512)
        xdt = part(work, 3168 + 96, 4, TOK)
        xd = part(work, 4320, NCH, 512)
        ssc = part(work, 5344, 2, NCH, CH)
        btok = part(zu, TAIL, NCH, 2, P)
        syf = part(zu, TAIL + 512, 4, TOK)
        ysq = part(zu, TAIL + 1568, 4, TOK)
        yoff = part(zu, TAIL + 1568, 512)
        stmp = part(zu, TAIL, 8, TOK)
        shd = part(xs, 0, 32, P)
        std = part(zu, TAIL + 1568, 16, P)

        ssd_mixed = signal("ssd_mixed")
        skip_ready, lru_pre = signal("skip_ready"), signal("lru_pre")

        lra_mm, lra, lri_mm, lri = signal("lra_mm"), signal("lra"), signal("lri_mm"), signal("lri")
        lam_abs, lam_ready, lexp = signal("lam_abs"), signal("lam_ready"), signal("lexp")
        lmul, lroot = signal("lmul"), signal("lroot")
        gelu_in, gelu_sig = signal("gelu_in"), signal("gelu_sig")
        lru_saved, lru_in = signal("lru_saved"), signal("lru_in", 16)
        h0 = sbuf("h0", 4, DEC)
        lout = sbuf("lout", 4, DEC + 1)
        lam8, lamn, lamt = sbuf("lam8", 4), sbuf("lamn", 4), sbuf("lamt", 4)
        lr, li, lth, lg = (part(hy, 1056 * j, 4, TOK) for j in range(4))
        la, lm, lh = (part(zu, 4096 + DT * TOK + 1056 * j, 4, TOK) for j in range(3))
        NORM_MIX, NORM_MIX_POST, NORM_MLP, NORM_MLP_POST = range(4)
        STAT = 7

        block = ctx.enter_context(nc.Block())

        @block.sync
        def _(sp):
            sp.wait_ge(x_loaded.sem, 16)
            for j in range(RING):
                sp.dma_start(ring[:, j, :], d["weights"][j, :, :]).then_inc(loaded[j], 16)
            with sp.Fori(1, LAYERS * UNITS // RING) as g:
                for j in range(RING):
                    sp.wait_ge(unit_done.sem, (g - 1) * RING + j + 1)
                    sp.dma_start(ring[:, j, :], d["weights"][bass.ds(g * RING + j, 1), :, :]
                                 .rearrange("o p n -> p (o n)")).then_inc(loaded[j], 16)

        @block.tensor
        def _(pe):
            mm = nc.tensor.matmul
            own = None

            def norm_sum(l, norm, j, half, first=False, last=False):
                pe.wait_ge(sq_ready.sem, l * sq_ready.per_layer + norm * DT + j + 1)
                mm(ps[:, STAT, 0:TOK], ones, sq[:, half, :], start=first, stop=last)\
                    .then_inc((mean_ready if last else sq_used).sem, 1)

            def norm_sums(l, norm):
                for j in range(DT):
                    norm_sum(l, norm, j, j % 2, first=(j == 0), last=(j == DT - 1))

            def products(j, w_hi, hi, lo, ahead=None):
                for k in range(DT):
                    if ahead:
                        ahead(k)
                    wh, wl = (t[:, slot, k * P:(k + 1) * P] for t, slot in ((w_hi, j % 2), (w_lo, j)))
                    mm(ps[:, j, 0:TOK], wh, hi[:, k, :], start=(k == 0), stop=False)
                    mm(ps[:, j, 0:TOK], wh, lo[:, k, :], start=False, stop=False)
                    last = mm(ps[:, j, 0:TOK], wl, hi[:, k, :], start=False, stop=(k == DT - 1))
                last.then_inc(unit_done.sem, 1)

            def split_tile(l, m, j, hi, lo, ahead=None):
                pe.wait_ge(bank_free.sem, l * UNITS + ZT + m + 1)
                pe.wait_ge(lo_ready.sem, l * SPLIT + m + 1)
                products(j, w_hi, hi, lo, ahead)

            def in_tile(l, unit, j):
                pe.wait_ge(in_h_split.sem, in_h_split.value(l, 4))
                pe.wait_ge(bank_free.sem, l * UNITS + unit + 1)
                pe.wait_ge(in_lo_ready.sem, l * RWKV_T + unit + 1)
                products(j, in_w_hi, in_h_hi, in_h_lo)

            done = [RWKV_T * DT]

            def fill(l, n):
                for at in range(done[0], min(done[0] + n, ZT * DT)):
                    unit, k = at // DT, at % DT
                    slot = unit % RING
                    if k == 0:
                        pe.wait_ge(bank_free.sem, l * UNITS + unit + 1)
                        pe.wait_ge(loaded[slot], (l * (UNITS // RING) + unit // RING + 1) * 16)
                    last = mm(ps[:, slot, 0:TOK], ring[:, slot, k * P:(k + 1) * P], hy3[:, k, :],
                              start=(k == 0), stop=(k == DT - 1))
                    if k == DT - 1:
                        last.then_inc(unit_done.sem, 1)
                    done[0] = at + 1

            def fill_to(l, unit):
                fill(l, max(unit * DT - done[0], 0))

            def head_stat(l, n, src, lhs_sum, lhs_wide, n_rows, one=False, fills=(0, 0)):
                fill(l, fills[0])
                pe.wait_ge(stat_in.sem, stat_in.value(l, n))
                for t in range(4):
                    last = mm(ps[0:n_rows, 4, 0:TOK], lhs_sum(t), src(t), start=(t == 0), stop=(t == 3))
                last.then_inc(stat_sum.sem, 1)
                fill(l, fills[1])
                pe.wait_ge(stat_row.sem, stat_row.value(l, n))
                for t in range(1 if one else 4):
                    last = mm(ps[:, 4 + t, 0:TOK], lhs_wide(t), rows[0:n_rows, :], start=True, stop=True)
                last.then_inc(stat_wide.sem, 1)

            def by_pair(l, n, src, fills):
                head_stat(l, n, src, lambda t: cv("head_sum", 8 * t, 8),
                          lambda t: cv("head_row", t * P, P, 8), 8, fills=fills)

            def rwkv_prep(l):
                fill(l, 40)
                pe.wait_ge(matrices_in.sem, matrices_in.value(l, 16))
                pe.wait_ge(lowrank_in.sem, lowrank_in.value(l, 1))
                for t in range(4):
                    last = mm(ps[:, 4 + t, 0:TOK], pv("wa2", t * P, P, 64), z[0:64, Z_WA, LEAD:ZW],
                              start=True, stop=True)
                last.then_inc(decay_mm.sem, 1)
                fill(l, 4)
                pe.wait_ge(decay_sig.sem, decay_sig.value(l, 1))
                at = PARAM["wa2"][0]
                for t in range(4):
                    last = mm(ps[:, 4 + t, 0:TOK], par[64:P, at + t * P:at + (t + 1) * P], z[64:P, Z_WA, LEAD:ZW],
                              start=True, stop=True)
                last.then_inc(rate_mm.sem, 1)
                fill(l, 4)
                pe.wait_ge(rate_sig.sem, rate_sig.value(l, 1))
                for t in range(4):
                    last = mm(ps[:, 4 + t, 0:TOK], pv("g2", t * P, P), z[:, Z_G, LEAD:ZW], start=True, stop=True)
                last.then_inc(rgate_mm.sem, 1)
                pe.wait_ge(rgate_out.sem, rgate_out.value(l, 1))
                by_pair(l, KK, lambda t: rk[:, t, :], (6, 7))

            def rwkv_decode(l):
                fill(l, 40)
                pe.wait_ge(rstate_in.sem, rstate_in.value(l, 16))
                for n in range(6):
                    half = n % 2
                    if n:
                        fill(l, 9)
                    pe.wait_ge(spread_in.sem, spread_in.value(l, n + 1))
                    if n >= 2:
                        pe.wait_ge(spread_read.sem, spread_read.value(l, n - 1))
                    if n == 4:
                        pe.wait_ge(rdec_ready.sem, rdec_ready.value(l, 1))
                    for i in range(16):
                        rhs = cv("stack") if n // 2 == 1 else hdec[:, half * 16 + i, :]
                        at = i % 8 * 64
                        last = mm(ps[:, 4 + 2 * half + i // 8, at:at + 64], spread[:, i, :], rhs,
                                  start=True, stop=True)
                    last.then_inc(spread_out.sem, 1)

            def rwkv_chunk(l, c):
                heads = [(i, i // 4, i % 4) for i in range(8)]
                for key, out_mm, before in ((kt, score1_mm, None), (bt, score2_mm, score1)):
                    fill(l, 4 if before is None else 6)
                    if before is None:
                        pe.wait_ge(operands_ready.sem, operands_ready.value(l, 1))
                        pe.wait_ge(spread_read.sem, spread_read.value(l, 6))
                        if c:
                            pe.wait_ge(ryT_out.sem, ryT_out.value(l, c))
                            pe.wait_ge(rh_out.sem, rh_out.value(l, c))
                    else:
                        pe.wait_ge(before.sem, before.value(l, c + 1))
                    for i, par_, hp in heads:
                        r = slice(64 * par_, 64 * par_ + 64)
                        last = mm(ps[:, 4 + i // 2, i % 2 * 256:i % 2 * 256 + 256], key[r, hp, c, :],
                                  kr[r, hp, c, :, :].rearrange("p j t -> p (j t)"), start=True, stop=True)
                    last.then_inc(out_mm.sem, 1)
                fill(l, 6)
                pe.wait_ge(score2.sem, score2.value(l, c + 1))
                for j in range(3):
                    for hp in range(4):
                        src = zt(Z_V + hp, 1, c * CH, c * CH + CH).rearrange("p o t -> p (o t)") if j == 0 \
                            else (kt, bt)[j - 1][:, hp, c, :]
                        last = nc.tensor.transpose(ps[:, 4 + j, hp * P:hp * P + P], src, ident)
                last.then_inc(rtok_mm.sem, 1)
                fill(l, 4)
                pe.wait_ge(rtok.sem, rtok.value(l, c + 1))
                for j in range(LEVELS):
                    n = (c * LEVELS + j) * 2
                    for half in range(2):
                        if j:
                            pe.wait_ge(dx_out.sem, dx_out.value(l, n - 1 + half))
                        for i in range(4):
                            h = half * 4 + i
                            last = mm(ps[:, 4 + half, i * P:i * P + P], sc2[:, h, 0, :], xx[:, h, 0, :] if j else ident,
                                      start=True, stop=True)
                        last.then_inc(q_mm.sem, 1)
                    if j == 0:
                        fill(l, 8)
                        continue
                    for half in range(2):
                        if half:
                            fill(l, 4)
                        pe.wait_ge(q_out.sem, q_out.value(l, n + 1 + half))
                        if half:
                            pe.wait_ge(dx_out.sem, dx_out.value(l, n + 1))
                        for i in range(4):
                            h = half * 4 + i
                            o = ps[:, 6 + i // 2, i % 2 * 256:i % 2 * 256 + 256]
                            if j < LEVELS - 1:
                                mm(o[:, 0:P], xx[:, h, 1, :], qb[:, h, :], start=True, stop=True)
                            last = mm(o[:, P:2 * P], qb[:, h, :], xx[:, h, 1, :], start=True, stop=True)
                        last.then_inc(dx_mm.sem, 1)
                fill(l, 3)
                pe.wait_ge(dx_out.sem, dx_out.value(l, (c + 1) * LEVELS * 2))
                for i, par_, hp in heads:
                    r = slice(64 * par_, 64 * par_ + 64)
                    o = ps[:, 4 + par_, hp * 64:hp * 64 + 64]
                    if c:
                        mm(o, kr[r, hp, c, 0, :], hst[r, hp, :], start=True, stop=False)
                    last = mm(o, sc1[:, i, 0, :], vt[:, (2 * hp + par_) * 64:(2 * hp + par_) * 64 + 64],
                              start=(c == 0), stop=True)
                last.then_inc(rhs_mm.sem, 1)
                fill(l, 2)
                pe.wait_ge(rhs_out.sem, rhs_out.value(l, c + 1))
                for i, par_, hp in heads:
                    last = mm(ps[:, 6, i * 64:i * 64 + 64], xx[:, i, 1, :], un[:, hp, par_, :], start=True, stop=True)
                last.then_inc(u_mm.sem, 1)
                fill(l, 2)
                pe.wait_ge(un_out.sem, un_out.value(l, c + 1))
                for i, par_, hp in heads:
                    r = slice(64 * par_, 64 * par_ + 64)
                    o = ps[:, 4 + par_, hp * 64:hp * 64 + 64]
                    if c:
                        mm(o, kr[r, hp, c, 1, :], hst[r, hp, :], start=True, stop=False)
                    mm(o, sc1[:, i, 1, :], vt[:, (2 * hp + par_) * 64:(2 * hp + par_) * 64 + 64],
                       start=(c == 0), stop=False)
                    mm(o, sc2[:, i, 1, :], un[:, hp, par_, :], start=False, stop=True)
                for hp in range(4):
                    o = ps[:, 6, hp * P:hp * P + P]
                    mm(o, ktt[:, hp * P:hp * P + P], vt[:, hp * P:hp * P + P], start=True, stop=False)
                    last = mm(o, btt[:, hp * P:hp * P + P], un[:, hp, :, :].rearrange("p a b -> p (a b)"),
                              start=False, stop=True)
                last.then_inc(ry_mm.sem, 1)
                fill(l, 2)
                pe.wait_ge(ry_out.sem, ry_out.value(l, c + 1))
                for hp in range(4):
                    last = nc.tensor.transpose(ps[:, 7, hp * P:hp * P + P], yt[:, hp * P:hp * P + P], ident)
                last.then_inc(ryT_mm.sem, 1)

            def rwkv_post(l):
                by_pair(l, MEAN, lambda t: yfm[:, t, :], (3, 0))
                by_pair(l, VAR, lambda t: delta[:, t, :], (6, 7))
                by_pair(l, BONUS, lambda t: rk[:, t, :], (3, 2))

            def gla(l):
                fill_to(l, GLA_T)
                pe.wait_ge(z_ready.sem, z_ready.value(l, GLA_T - RWKV_T))
                pe.wait_ge(bonus_read.sem, bonus_read.value(l, 1))
                pe.wait_ge(matrices_in.sem, matrices_in.value(l, 16))
                for t in range(2):
                    last = mm(ps[:, 4 + t, 0:TOK], pv("gate2", t * P, P, 16), z[0:16, Z_GA, LEAD:ZW],
                              start=True, stop=True)
                last.then_inc(ggate_mm.sem, 1)
                fill(l, 68)
                pe.wait_ge(gops.sem, gops.value(l, 1))
                for c in range(NCH):
                    for h in range(4):
                        last = nc.tensor.transpose(ps[:, 4 + c, h * P:h * P + P],
                                                   z[:, Z_GV + h, LEAD + c * CH:LEAD + c * CH + CH], ident)
                    for hp in range(2):
                        at = (c * 2 + hp) * P
                        last = nc.tensor.transpose(ps[:, 6, at:at + P], gkdT[:, hp, c, :], ident)
                last.then_inc(gtok_mm.sem, 1)
                fill(l, 4)
                pe.wait_ge(gtok.sem, gtok.value(l, 1))
                for j in range(LEVELS + 1):
                    if j >= 2:
                        pe.wait_ge(glevel.sem, glevel.value(l, j - 1))
                    for a in range(2):
                        r = slice(64 * a, 64 * a + 64)
                        for hp in range(2):
                            for c in range(NCH):
                                t = slice(c * CH, c * CH + CH)
                                tz = slice(LEAD + c * CH, LEAD + c * CH + CH)
                                k_, q_ = (kdist[r, j, hp, t], dist[r, j, hp, t]) if j < LEVELS else \
                                    (z[r, Z_GK + hp, tz], z[r, Z_GQ + hp, tz])
                                at = (hp * NCH + c) * P
                                last = mm(ps[:, 4 + 2 * (j % 2) + a, at:at + P], k_, q_, start=True, stop=True)
                    last.then_inc(glevel_mm.sem, 1)
                for c in range(NCH):
                    pe.wait_ge(glevel.sem, glevel.value(l, LEVELS + 1))
                    if c:
                        pe.wait_ge(gh_out.sem, gh_out.value(l, c))
                        pe.wait_ge(gyT_out.sem, gyT_out.value(l, c))
                    for a in range(2):
                        r = slice(64 * a, 64 * a + 64)
                        for hp in range(2):
                            o = ps[:, 4 + a, hp * P:hp * P + P]
                            h = 2 * hp + a
                            if c:
                                mm(o, gqc[r, hp, c, :], gst[r, hp, :], start=True, stop=False)
                            mm(o, gsc[:, (a * 2 + hp) * NCH + c, :], gvt[:, c, h * P:h * P + P],
                               start=(c == 0), stop=True)
                    for hp in range(2):
                        last = mm(ps[:, 6, hp * 256:hp * 256 + 256], gkd[:, c, hp * P:hp * P + P],
                                  gvt[:, c, hp * 256:hp * 256 + 256], start=True, stop=True)
                    last.then_inc(gy_mm.sem, 1)
                    fill(l, 2)
                    pe.wait_ge(gy_out.sem, gy_out.value(l, c + 1))
                    for h in range(4):
                        last = nc.tensor.transpose(ps[:, 7, h * P:h * P + P], gyt[:, h * P:h * P + P], ident)
                    last.then_inc(gyT_mm.sem, 1)
                pe.wait_ge(gyT_out.sem, gyT_out.value(l, NCH))
                for n in range(4):
                    pe.wait_ge(gh_out.sem, gh_out.value(l, NCH))
                    if n >= 2:
                        pe.wait_ge(gval_read.sem, gval_read.value(l, n - 1))
                    for b in range(2):
                        for h in range(4):
                            col = LEAD + SEQ + n * 2 + b
                            last = mm(ps[:, 4 + 2 * (n % 2) + b, h * P:h * P + P],
                                      z[:, Z_GV + h, col:col + 1].broadcast_to([P, P]), ident, start=True, stop=True)
                    last.then_inc(gval_mm.sem, 1)
                fill(l, 14)
                pe.wait_ge(gdec_ready.sem, gdec_ready.value(l, 1))
                for a in range(2):
                    r = slice(64 * a, 64 * a + 64)
                    for hp in range(2):
                        for b in range(DEC):
                            col = LEAD + SEQ + b
                            last = mm(ps[:, 4 + a, hp * DEC + b:hp * DEC + b + 1], ghd[r, b * 2 + hp, :],
                                      z[r, Z_GQ + hp, col:col + 1], start=True, stop=True)
                last.then_inc(gdec_y_mm.sem, 1)
                head_stat(l, GLA_RMS, lambda t: gsq[:, t, :], lambda t: cv("tile_sum", 4 * t, 4),
                          lambda t: cv("ident", t, 1, 4).broadcast_to([4, P]), 4, fills=(3, 7))

            def lru(l):
                pe.wait_ge(bank_free.sem, l * UNITS + ZT + 4)
                for w, before, out in (("lru_wa", lconv_out, lra_mm), ("lru_wi", lra, lri_mm)):
                    pe.wait_ge(before.sem, before.value(l, 1))
                    for t in range(4):
                        last = mm(ps[:, t, 0:TOK], pv(w, t * P, P), cx[:, 8 + t, :], start=True, stop=True)
                    last.then_inc(out.sem, 1)

            def ssd(l):
                fill(l, 72)
                pe.wait_ge(sdt.sem, sdt.value(l, 1))
                for t in range(4):
                    last = mm(ps[:, 4 + t, 0:TOK], cv("head_row", t * P, P, 8), dtr[0:8, :], start=True, stop=True)
                last.then_inc(sdt_mm.sem, 1)
                fill(l, 4)
                pe.wait_ge(sdt_read.sem, sdt_read.value(l, 1))
                for t in range(4):
                    mm(ps[:, 4, t * DEC:t * DEC + DEC], cv("head_row", t * P, P, 8), dedec[0:8, :], start=True, stop=True)
                for c in range(NCH):
                    last = mm(ps[:, 5, c * 8:c * 8 + 8], dcum[0:8, c * CH:c * CH + CH], cv("ident", 0, 8, 8),
                              start=True, stop=True)
                last.then_inc(sdec_mm.sem, 1)
                pe.wait_ge(sdec_read.sem, sdec_read.value(l, 1))
                for h in range(8):
                    last = mm(ps[:, 4 + h // 2, h % 2 * SEQ:h % 2 * SEQ + SEQ],
                              cv("ident", h, 1, 8).broadcast_to([8, P]), dcum[0:8, 0:SEQ], start=True, stop=True)
                last.then_inc(srow_mm.sem, 1)
                fill(l, 11)
                pe.wait_ge(srow_read.sem, srow_read.value(l, 1))
                for g in range(2):
                    for c in range(NCH):
                        t = slice(c * CH, c * CH + CH)
                        last = mm(ps[:, 4, (g * NCH + c) * P:(g * NCH + c) * P + P], cx[:, 4 + g, t], cx[:, 6 + g, t],
                                  start=True, stop=True)
                last.then_inc(ssc_mm.sem, 1)
                for c in range(NCH):
                    t = slice(c * CH, c * CH + CH)
                    for h in range(4):
                        last = nc.tensor.transpose(ps[:, 5 + c, h * P:h * P + P], xdt[:, h, t], ident)
                    for g in range(2):
                        last = nc.tensor.transpose(ps[:, 7, (c * 2 + g) * P:(c * 2 + g) * P + P], cx[:, 4 + g, t], ident)
                last.then_inc(stok_mm.sem, 1)
                fill(l, 7)
                pe.wait_ge(sops.sem, sops.value(l, 1))
                for c in range(NCH):
                    if c:
                        pe.wait_ge(sh_out.sem, sh_out.value(l, c))
                        pe.wait_ge(sy_out.sem, sy_out.value(l, c))
                        pe.wait_ge(syT_out.sem, syT_out.value(l, c))
                    for h in range(8):
                        last = mm(ps[:, 4, h * 64:h * 64 + 64], seg[:, h, c, :], xtok[:, c, h * 64:h * 64 + 64],
                                  start=True, stop=True)
                    for g in range(2):
                        w = slice(g * 256, g * 256 + 256)
                        if c:
                            mm(ps[:, 5, w], cx[:, 6 + g, c * CH:c * CH + CH], sst[:, w], start=True, stop=True)
                        last = mm(ps[:, 6, w], btok[:, c, g, :], xd[:, c, w], start=True, stop=True)
                    last.then_inc(sy_mm.sem, 1)
                    pe.wait_ge(sy_out.sem, sy_out.value(l, c + 1))
                    for h in range(4):
                        last = nc.tensor.transpose(ps[:, 7, h * P:h * P + P], syt[:, h * P:h * P + P], ident)
                    last.then_inc(syT_mm.sem, 1)
                fill_to(l, ZT)
                pe.wait_ge(syT_out.sem, syT_out.value(l, NCH))
                for n in range(4):
                    if n == 2:
                        lru(l)
                    pe.wait_ge(sh_out.sem, sh_out.value(l, NCH))
                    if n >= 2:
                        pe.wait_ge(sbc_read.sem, sbc_read.value(l, n - 1))
                    for b in range(4):
                        for g in range(2):
                            at = (b * 2 + g) * P
                            col = SEQ + (n % 2) * 4 + b
                            src = cx[:, (4 if n < 2 else 6) + g, col:col + 1]
                            last = mm(ps[:, 4 + 2 * (n % 2) + at // 512, at % 512:at % 512 + P],
                                      src.broadcast_to([P, P]), ident, start=True, stop=True)
                    last.then_inc(sbc_mm.sem, 1)
                head_stat(l, SSD_RMS, lambda t: ysq[:, t, :], lambda t: cv("ones", 0, 1),
                          lambda t: cv("ones", 0, P, 1), 1, one=True)

            pe.wait_ge(consts_in.sem, 16)
            with pe.Fori(0, LAYERS) as l:
                norm_sums(l, NORM_MIX)
                with pe.Fori(0, RWKV_T // 4) as g:
                    for j in range(4):
                        in_tile(l, g * 4 + j, j)
                for unit in range(RWKV_T // 4 * 4, RWKV_T):
                    in_tile(l, unit, unit % 4)
                rwkv_prep(l)
                rwkv_decode(l)
                for c in range(NCH):
                    rwkv_chunk(l, c)
                rwkv_post(l)
                gla(l)
                fill_to(l, SSD_T)
                ssd(l)
                pe.wait_ge(mixed.sem, mixed.value(l, 1))
                pe.wait_ge(mix_split.sem, mix_split.value(l, 2))

                def four_out(g, first):
                    for j in range(4):
                        split_tile(l, g * 4 + j, j, mix_hi, mix_lo)
                        if j or not first:
                            norm_sum(l, NORM_MIX_POST, g * 4 + j - 1, (j + 1) % 2, first=(first and j == 1))
                four_out(0, True)
                with pe.Fori(1, DT // 4) as g:
                    four_out(g, False)
                norm_sum(l, NORM_MIX_POST, DT - 1, 1, last=True)
                norm_sums(l, NORM_MLP)
                with pe.Fori(0, QUARTERS) as q:
                    with pe.Fori(0, DT // 4) as g:
                        pe.wait_ge(h_split.sem, h_split.value(l, 4))
                        for j in range(4):
                            split_tile(l, DT + q * 2 * DT + g * 4 + j, j, h_hi, h_lo)
                    with pe.Fori(0, DT // 4) as g:
                        for j in range(4):
                            def features(k):
                                if j == 0 and k >= DT - 4:
                                    pe.wait_ge(u_split.sem, l * FT + q * DT + k + 1 + 2)
                            split_tile(l, 2 * DT + q * 2 * DT + g * 4 + j, j, u_hi, u_lo, features)
                norm_sums(l, NORM_MLP_POST)

        @block.scalar
        def _(act):
            A = nc.scalar.activation
            own = Own(act, own_act)

            def squares(l, norm, ready, level, of):
                with act.Fori(0, DT // 2) as g:
                    for j in range(2):
                        act.wait_ge(ready.sem, level + g * 2 + j + 1)
                        act.wait_ge(sq_used.sem, l * sq_used.per_layer + norm * (DT - 1) + g * 2 + j + 1)
                        A(sq[:, j, :], of[:, bass.ds(g * 2 + j, 1), :].rearrange("p o t -> p (o t)"),
                          ACT.Square).then_inc(sq_ready.sem, 1)

            def root(l, norm):
                act.wait_ge(rstd_in.sem, rstd_in.value(l, norm + 1))
                A(rstd[:, :], rstd[:, :], ACT.Sqrt).then_inc(root_ready.sem, 1)

            def in_weight_hi(l, unit, j):
                act.wait_ge(loaded[j], (l * UNITS + unit - j) * (16 // RING) + 16)
                A(in_w_hi[:, j % 2, :], ring[:, j, :], ACT.Copy).then_inc(in_hi_ready.sem, 1)

            def weight_hi(l, m, j):
                act.wait_ge(loaded[j], (l * UNITS + ZT + m - j) * (16 // RING) + 16)
                act.wait_ge(unit_done.sem, l * UNITS + ZT + m - 1)
                A(w_hi[:, j % 2, :], ring[:, j, :], ACT.Copy).then_inc(hi_ready.sem, 1)

            act.dma_start(x[:, :, :], d["x"]).then_inc(x_loaded.sem, 16)
            act.dma_start(const[:, :], d["consts"]).then_inc(consts_in.sem, 16)
            act.dma_start(gains[:, :, :], d["params"][:, :, 0:N_GAIN].rearrange("l p n -> p l n")).then_inc(gains_loaded.sem, 16)
            act.wait_ge(gains_loaded.sem, 16)
            with act.Fori(0, LAYERS) as l:
                own.restart()
                act.wait_ge(x_in.sem, l * DT + DT)
                A(par[:, 0:N_GAIN], gains[:, bass.ds(l, 1), :].rearrange("p o n -> p (o n)"), ACT.Copy)\
                    .then_inc(gains_in.sem, 1)
                act.dma_start(par[:, N_GAIN:N_PARAM], d["params"][bass.ds(l, 1), :, N_GAIN:N_PARAM]
                              .rearrange("o p n -> p (o n)")).then_inc(matrices_in.sem, 16)
                act.dma_start(d["x_kept"], x[:, :, :]).then_inc(x_saved.sem, 16)
                in_weight_hi(l, 0, 0)
                in_weight_hi(l, 1, 1)
                squares(l, NORM_MIX, x_in, l * DT, x)
                for j in range(4):
                    act.wait_ge(h_ready.sem, h_ready.value(l, 4 * j + 4))
                    A(in_h_hi[:, 4 * j:4 * j + 4, :], hy3[:, 4 * j:4 * j + 4, :], ACT.Copy).then_inc(in_h_hi_ready.sem, 1)
                root(l, NORM_MIX)
                with act.Fori(0, (RWKV_T - 2) // 4) as g:
                    for j in range(4):
                        act.wait_ge(unit_done.sem, l * UNITS + g * 4 + j + 1)
                        in_weight_hi(l, g * 4 + j + 2, (j + 2) % 4)
                out = [RWKV_T]

                def out_of_banks(n):
                    for unit in range(out[0], RWKV_T + n):
                        act.wait_ge(unit_done.sem, l * UNITS + unit + 1)
                        A(z[:, unit, LEAD:ZW], ps[:, unit % 4, 0:TOK], ACT.Copy).then_inc(bank_free.sem, 1)
                        out[0] = unit + 1

                act.dma_start(prev[:, :, :], d["shift"][bass.ds(l, 1), :, :]
                              .rearrange("o p (n b) -> p (o n) b", b=DEC)).then_inc(shift_in.sem, 16)
                act.wait_ge(shift_saved.sem, l + 1)
                act.dma_start(d["shift_out"][bass.ds(l, 1), :, :, :].rearrange("o p n b -> p (o n) b"),
                              shifted[:, :, :]).then_inc(stored, 16)
                act.wait_ge(zm_ready.sem, l + 1)
                act.dma_start(part(xs, 0, 2048), d["rwkv_state"][bass.ds(l, 1), :, :]
                              .rearrange("o p n -> p (o n)")).then_inc(rstate_in.sem, 16)
                own.done(A(z[0:64, Z_WA, LEAD:ZW], z[0:64, Z_WA, LEAD:ZW], ACT.Tanh))
                A(z[:, Z_G, LEAD:ZW], z[:, Z_G, LEAD:ZW], ACT.Sigmoid).then_inc(lowrank_in.sem, 1)
                act.wait_ge(decay_mm.sem, l + 1)
                for t in range(4):
                    last = A(sig[:, t, :], ps[:, 4 + t, 0:TOK], ACT.Sigmoid, bias=pv("w0", t))
                last.then_inc(decay_sig.sem, 1)
                out_of_banks(2)
                act.wait_ge(rate_mm.sem, l + 1)
                for t in range(4):
                    last = A(rate[:, t, :], ps[:, 4 + t, 0:TOK], ACT.Sigmoid, bias=pv("a0", t))
                last.then_inc(rate_sig.sem, 1)
                act.wait_ge(rgate_mm.sem, l + 1)
                A(gate, ps[:, 4:8, 0:TOK], ACT.Copy).then_inc(rgate_out.sem, 1)
                out_of_banks(3)
                act.wait_ge(stat_sum.sem, stat_sum.value(l, KK))
                A(rows[0:8, :], ps[0:8, 4, 0:TOK], ACT.Sqrt).then_inc(stat_root.sem, 1)
                act.wait_ge(cum_ready.sem, l + 1)
                own.done(A(kt, cum, ACT.Exp, scale=DECAY))
                for h in range(4):
                    own.done(A(kr[:, h, :, 1, :], cum[:, h, :, :], ACT.Exp, scale=-DECAY))
                    own.done(A(kr[:, h, :, 0, :], kr[:, h, :, 0, :], ACT.Exp, scale=-DECAY))
                own.done(A(ends[:, :, :], ends[:, :, :], ACT.Exp, scale=-DECAY))
                own.done(A(mids[:, :, :], mids[:, :, :], ACT.Exp, scale=-DECAY))
                A(dec[:, 0, :, :], sig[:, :, SEQ:TOK], ACT.Exp, scale=-DECAY).then_inc(exps_ready.sem, 1)
                out_of_banks(9)
                act.wait_ge(spread_read.sem, spread_read.value(l, 6))
                act.dma_start(d["rwkv_s"][bass.ds(l, 1), :, :].rearrange("o p n -> p (o n)"), part(xs, 0, 2048))\
                    .then_inc(stored, 16)
                for c in range(NCH):
                    act.wait_ge(rtok_mm.sem, rtok_mm.value(l, c + 1))
                    for j, t in enumerate((vt, ktt, btt)):
                        last = A(t, ps[:, 4 + j, :], ACT.Copy)
                    last.then_inc(rtok.sem, 1)
                    out_of_banks(10 + 3 * c)
                    act.wait_ge(rhs_mm.sem, rhs_mm.value(l, c + 1))
                    for a in range(2):
                        last = A(un[:, :, a, :], ps[:, 4 + a, 0:256].rearrange("p (h v) -> p h v", h=4), ACT.Copy)
                    last.then_inc(rhs_out.sem, 1)
                    out_of_banks(12 + 3 * c)
                    act.wait_ge(u_mm.sem, u_mm.value(l, c + 1))
                    for a in range(2):
                        last = A(un[:, :, a, :], ps[:, 6, a * 256:a * 256 + 256].rearrange("p (h v) -> p h v", h=4),
                                 ACT.Copy, scale=-1.0)
                    last.then_inc(un_out.sem, 1)
                    act.wait_ge(ry_mm.sem, ry_mm.value(l, c + 1))
                    ytv = yt.rearrange("p (h a v) -> p h a v", h=4, a=2)
                    for a in range(2):
                        last = A(ytv[:, :, a, :], ps[:, 4 + a, 0:256].rearrange("p (h v) -> p h v", h=4), ACT.Copy)
                    last.then_inc(ry_out.sem, 1)
                    act.wait_ge(ryT_mm.sem, ryT_mm.value(l, c + 1))
                    A(yfm[:, :, c * CH:c * CH + CH], ps[:, 7, :].rearrange("p (h t) -> p h t", h=4), ACT.Copy)\
                        .then_inc(ryT_out.sem, 1)
                act.wait_ge(rh_out.sem, rh_out.value(l, NCH))
                act.dma_start(d["rwkv_p"][bass.ds(l, 1), :, :].rearrange("o p n -> p (o n)"), part(zu, TAIL + 3584, 256))\
                    .then_inc(stored, 16)
                act.wait_ge(centred.sem, l + 1)
                A(delta[:, 0:4, :], yfm, ACT.Square).then_inc(stat_in.sem, 1)
                act.wait_ge(stat_mid.sem, stat_mid.value(l, 1))
                A(rows[0:8, :], rows[0:8, :], ACT.Sqrt).then_inc(stat_root.sem, 1)

                out_of_banks(17)
                act.wait_ge(z_ready.sem, z_ready.value(l, GLA_T - RWKV_T))
                A(mix[:, MIX_GLA:MIX_GLA + 4, :], zt(Z_GG, 4), ACT.Sigmoid).then_inc(gsig.sem, 1)
                act.wait_ge(ggate_x.sem, l + 1)
                own.done(A(gtmp, glog, ACT.Abs))
                own.done(A(gtmp, gtmp, ACT.Exp, scale=-1.0))
                A(gtmp, gtmp, ACT.Ln, bias=1.0).then_inc(ggate_ln.sem, 1)
                out_of_banks(18)
                act.wait_ge(gdist.sem, l + 1)
                own.done(A(gqc, gcum4, ACT.Exp, scale=1.0 / GATE_TEMP))
                own.done(A(gkdT, gkdT, ACT.Exp, scale=-1.0 / GATE_TEMP))
                own.done(A(glast[:, :, :], gcum4[:, :, :, CH - 1], ACT.Exp, scale=1.0 / GATE_TEMP))
                own.done(A(gdec[:, :, :], glog[:, :, SEQ:TOK], ACT.Exp, scale=1.0 / GATE_TEMP))
                distf = part(xs, 0, LEVELS * 512)
                own.done(A(distf, distf, ACT.Abs))
                A(distf, distf, ACT.Exp, scale=-1.0 / GATE_TEMP).then_inc(gdist_exp.sem, 1)
                out_of_banks(21)
                act.wait_ge(gtok_mm.sem, l + 1)
                A(gvt, ps[:, 4:6, :], ACT.Copy)
                A(gkd, ps[:, 6, :].rearrange("p (c n) -> p c n", c=NCH), ACT.Copy).then_inc(gtok.sem, 1)
                act.wait_ge(glevel.sem, glevel.value(l, LEVELS + 1))
                act.dma_start(part(xs, 0, 2048), d["gla_state"][bass.ds(l, 1), :, :]
                              .rearrange("o p n -> p (o n)")).then_inc(gstate_in.sem, 16)
                for c in range(NCH):
                    act.wait_ge(gy_mm.sem, gy_mm.value(l, c + 1))
                    gyv = gyt.rearrange("p (h a v) -> p h a v", h=2, a=2)
                    for a in range(2):
                        last = A(gyv[:, :, a, :], ps[:, 4 + a, 0:256].rearrange("p (h v) -> p h v", h=2), ACT.Copy)
                    last.then_inc(gy_out.sem, 1)
                    act.wait_ge(gyT_mm.sem, gyT_mm.value(l, c + 1))
                    A(gof[:, :, c * CH:c * CH + CH], ps[:, 7, :].rearrange("p (h t) -> p h t", h=4), ACT.Copy)\
                        .then_inc(gyT_out.sem, 1)
                act.wait_ge(gh_out.sem, gh_out.value(l, NCH))
                act.dma_start(d["gla_p"][bass.ds(l, 1), :, :].rearrange("o p n -> p (o n)"), part(work, 5680, 256))\
                    .then_inc(stored, 16)
                out_of_banks(22)
                act.wait_ge(gdec_ready.sem, l + 1)
                act.dma_start(d["gla_s"][bass.ds(l, 1), :, :].rearrange("o p n -> p (o n)"), part(xs, 0, 2048))\
                    .then_inc(stored, 16)
                act.wait_ge(gdec_y_mm.sem, l + 1)
                gofv = gof.rearrange("p (h a) t -> p h a t", a=2)
                for a in range(2):
                    last = A(gofv[:, :, a, SEQ:TOK], ps[:, 4 + a, 0:2 * DEC].rearrange("p (h b) -> p h b", h=2), ACT.Copy)
                own.done(last)
                A(gsq, gof, ACT.Square).then_inc(stat_in.sem, 1)
                act.wait_ge(stat_mid.sem, stat_mid.value(l, 2))
                A(rows[0:4, :], rows[0:4, :], ACT.Sqrt).then_inc(stat_root.sem, 1)

                out_of_banks(SSD_T - RWKV_T)

                act.dma_start(cbuf[:, 0:3, :, :].rearrange("p i n b -> p (i n b)"), d["conv"][bass.ds(l, 1), :, :]
                              .rearrange("o p n -> p (o n)")).then_inc(conv_in.sem, 16)
                act.dma_start(h0[:, :, :].rearrange("p n b -> p (n b)"), d["lru_state"][bass.ds(l, 1), :, :]
                              .rearrange("o p n -> p (o n)")).then_inc(lru_in.sem, 16)

                act.wait_ge(z_ready.sem, z_ready.value(l, SSD_T - RWKV_T))
                A(mix[:, MIX_SSD:MIX_SSD + 4, :], zt(Z_SG, 4), ACT.Sigmoid)
                act.wait_ge(conv_out.sem, l + 1)
                A(stmp, cx[:, 0:8, :], ACT.Sigmoid).then_inc(ssig.sem, 1)
                own.done(A(lamt[:, :], pv("lam", n=4), ACT.Abs))
                own.done(A(lamt[:, :], lamt[:, :], ACT.Exp, scale=-1.0))
                A(lamt[:, :], lamt[:, :], ACT.Ln, bias=1.0).then_inc(lam_abs.sem, 1)
                act.wait_ge(sdt_x.sem, l + 1)
                own.done(A(acol[0:8, :], pv("a_log", rows=8), ACT.Exp))
                own.done(A(dcum[0:8, :], dtr[0:8, :], ACT.Abs))
                own.done(A(dcum[0:8, :], dcum[0:8, :], ACT.Exp, scale=-1.0))
                A(dcum[0:8, :], dcum[0:8, :], ACT.Ln, bias=1.0).then_inc(sdt_ln.sem, 1)
                out_of_banks(28)
                act.wait_ge(sdt_c.sem, l + 1)
                A(dedec[0:8, :], dcum[0:8, SEQ:TOK], ACT.Exp).then_inc(sdt.sem, 1)
                act.wait_ge(srow_read.sem, l + 1)
                own.done(A(seg, seg, ACT.Exp))
                own.done(A(ecum[:, :, :], cumT[:, :, :], ACT.Exp))
                own.done(A(wdec[:, :, :], wdec[:, :, :], ACT.Exp))
                A(elast[:, :, :], lastv[:, :, :], ACT.Exp).then_inc(sexps.sem, 1)
                act.wait_ge(stok_mm.sem, l + 1)
                A(xtok, ps[:, 5:7, :], ACT.Copy)
                A(part(zu, TAIL, 512), ps[:, 7, :], ACT.Copy).then_inc(stok.sem, 1)
                out_of_banks(30)
                for c in range(NCH):
                    act.wait_ge(syT_mm.sem, syT_mm.value(l, c + 1))
                    A(syf[:, :, c * CH:c * CH + CH], ps[:, 7, :].rearrange("p (h t) -> p h t", h=4), ACT.Copy)\
                        .then_inc(syT_out.sem, 1)
                act.wait_ge(sh_out.sem, sh_out.value(l, NCH))
                act.dma_start(d["ssd_p"][bass.ds(l, 1), :, :].rearrange("o p n -> p (o n)"), sst).then_inc(stored, 16)
                act.wait_ge(stored, l * 16 * STORES + 16 * 6)
                act.dma_start(part(xs, 0, 4096), d["ssd_state"][bass.ds(l, 1), :, :]
                              .rearrange("o p n -> p (o n)")).then_inc(sstate_in.sem, 16)
                out_of_banks(ZT - RWKV_T)
                act.wait_ge(lra_mm.sem, l + 1)
                for t in range(4):
                    last = A(lr[:, t, :], ps[:, t, 0:TOK], ACT.Sigmoid, bias=pv("b_a", t))
                last.then_inc(lra.sem, 1)
                act.wait_ge(lri_mm.sem, l + 1)
                for t in range(4):
                    last = A(li[:, t, :], ps[:, t, 0:TOK], ACT.Sigmoid, bias=pv("b_i", t))
                last.then_inc(lri.sem, 1)
                act.wait_ge(gelu_in.sem, l + 1)
                A(lg, lg, ACT.Sigmoid, scale=GELU_K).then_inc(gelu_sig.sem, 1)
                act.wait_ge(lam_ready.sem, l + 1)
                for t in range(4):
                    A(la[:, t, :], lr[:, t, :], ACT.Exp, scale=lamn[:, t:t + 1])
                    last = A(lth[:, t, :], lr[:, t, :], ACT.Tanh, scale=lam8[:, t:t + 1])
                last.then_inc(lexp.sem, 1)
                weight_hi(l, 0, 0)
                weight_hi(l, 1, 1)
                for at in (MIX_GLA, MIX_RWKV):
                    last = A(mix_hi[:, at:at + 4, :], mix[:, at:at + 4, :], ACT.Copy)
                last.then_inc(mix_hi_ready.sem, 1)

                act.wait_ge(sbc_read.sem, sbc_read.value(l, 3))
                act.dma_start(d["ssd_s"][bass.ds(l, 1), :, :].rearrange("o p n -> p (o n)"), part(xs, 0, 4096))\
                    .then_inc(stored, 16)
                act.wait_ge(lconv_slot.sem, l + 1)
                act.dma_start(d["conv_p"][bass.ds(l, 1), :, :, :].rearrange("o p n b -> p (o n b)"),
                              cps[:, :, :].rearrange("p n b -> p (n b)")).then_inc(stored, 16)
                act.dma_start(d["conv_s"][bass.ds(l, 1), :, :, :, :].rearrange("o p i n b -> p (o i n b)"),
                              cbuf[:, :, :, :].rearrange("p i n b -> p (i n b)")).then_inc(stored, 16)
                act.wait_ge(sdec_done.sem, l + 1)
                A(ysq, syf, ACT.Square).then_inc(stat_in.sem, 1)
                act.wait_ge(stat_mid.sem, stat_mid.value(l, 3))
                A(rows[0:1, :], rows[0:1, :], ACT.Sqrt).then_inc(stat_root.sem, 1)
                act.wait_ge(lmul.sem, l + 1)
                A(lm, lm, ACT.Sqrt).then_inc(lroot.sem, 1)

                act.wait_ge(ssd_mixed.sem, l + 1)
                A(mix_hi[:, MIX_SSD:MIX_SSD + 4, :], mix[:, MIX_SSD:MIX_SSD + 4, :], ACT.Copy).then_inc(mix_hi_ready.sem, 1)
                act.wait_ge(lru_saved.sem, l + 1)
                act.dma_start(d["lru"][bass.ds(l, 1), :, :, :].rearrange("o p n b -> p (o n b)"),
                              lout[:, :, :].rearrange("p n b -> p (n b)")).then_inc(stored, 16)
                act.wait_ge(mixed.sem, mixed.value(l, 1))
                A(mix_hi[:, MIX_LRU:MIX_LRU + 4, :], mix[:, MIX_LRU:MIX_LRU + 4, :], ACT.Copy)\
                    .then_inc(mix_hi_ready.sem, 1)
                act.wait_ge(stored, l * 16 * STORES + 16 * STORES)
                act.dma_start(x[:, :, :], d["x_kept"]).then_inc(x_back.sem, 16)
                with act.Fori(0, DT // 4) as g:
                    for j in range(4):
                        act.wait_ge(unit_done.sem, l * UNITS + ZT + g * 4 + j + 1)
                        weight_hi(l, g * 4 + j + 2, (j + 2) % 4)
                        act.wait_ge(sq_used.sem, l * sq_used.per_layer + NORM_MIX_POST * (DT - 1) + g * 4 + j + 1)
                        A(sq[:, j % 2, :], ps[:, j, 0:TOK], ACT.Square).then_inc(sq_ready.sem, 1)
                        A(hy3[:, bass.ds(g * 4 + j, 1), :].rearrange("p o t -> p (o t)"), ps[:, j, 0:TOK],
                          ACT.Copy).then_inc(bank_free.sem, 1)
                root(l, NORM_MIX_POST)
                squares(l, NORM_MLP, x_mid, l * DT, x)
                for j in range(4):
                    act.wait_ge(h_ready.sem, h_ready.value(l, DT + 4 * j + 4))
                    A(h_hi[:, 4 * j:4 * j + 4, :], hy3[:, 4 * j:4 * j + 4, :], ACT.Copy).then_inc(h_hi_ready.sem, 1)
                root(l, NORM_MLP)

                def up(q):
                    with act.Fori(0, DT // 4) as g:
                        for j in range(4):
                            m = DT + q * 2 * DT + g * 4 + j
                            act.wait_ge(unit_done.sem, l * UNITS + ZT + m + 1)
                            weight_hi(l, m + 2, (j + 2) % 4)
                            act.wait_ge(bank_free.sem, l * UNITS + ZT + m + 1 + 4)
                            act.wait_ge(u_split.sem, l * FT + q * DT + g * 4 + j + 1)
                            A(sq[:, j % 2, :], pre[:, j, :], ACT.Square)
                            A(u_hi[:, bass.ds(g * 4 + j, 1), :].rearrange("p o t -> p (o t)"), pre[:, j, :],
                              ACT.Square).then_inc(u_hi_ready.sem, 1)

                def down(q, groups):
                    with act.Fori(0, groups) as g:
                        for j in range(4):
                            m = 2 * DT + q * 2 * DT + g * 4 + j
                            act.wait_ge(unit_done.sem, l * UNITS + ZT + m + 1)
                            weight_hi(l, m + 2, (j + 2) % 4)

                with act.Fori(0, QUARTERS - 1) as q:
                    up(q)
                    down(q, DT // 4)
                up(QUARTERS - 1)
                down(QUARTERS - 1, DT // 4 - 1)
                for m in range(SPLIT - 4, SPLIT - 2):
                    act.wait_ge(unit_done.sem, l * UNITS + ZT + m + 1)
                    weight_hi(l, m + 2, (m + 2) % 4)
                squares(l, NORM_MLP_POST, bank_free, (l + 1) * UNITS - DT + 4, y3)
                root(l, NORM_MLP_POST)
            act.wait_ge(x_in.sem, (LAYERS + 1) * DT)
            act.dma_start(d["y"], x[:, :, :]).then_inc(stored, 16)
            act.wait_ge(stored, 16 * (LAYERS * STORES + 1))

        @block.gpsimd
        def _(pool):
            own = Own(pool, own_pool)

            def scale_h(l, which, name, ready, j):
                pool.wait_ge(ready.sem, ready.value(l, j + 1))
                nc.gpsimd.tensor_tensor(hy3[:, j, :], x[:, j, :],
                                        pv(name, j).broadcast_to([P, TOK]), ALU.mult).then_inc(h_ready.sem, 1)

            def scale_z(l, first, end):
                for unit in range(first, end):
                    pool.wait_ge(bank_free.sem, l * UNITS + unit + 1 + 4)
                    tile = z[:, unit, LEAD:ZW]
                    nc.gpsimd.tensor_tensor(tile, tile, rstd[:, :], ALU.mult).then_inc(z_ready.sem, 1)

            with pool.Fori(0, LAYERS) as l:
                own.restart()
                pool.wait_ge(gains_in.sem, l + 1)
                for j in range(DT):
                    scale_h(l, 0, "mix_pre", x_in, j)
                pool.wait_ge(operands_ready.sem, l + 1)
                for n in range(6):
                    half = n % 2
                    vec = (dec[:, 1, :, half * 4:half * 4 + 4],
                           z[:, Z_V:Z_V + 4, LEAD + SEQ + half * 4:LEAD + SEQ + half * 4 + 4],
                           z[:, Z_R:Z_R + 4, LEAD + SEQ + half * 4:LEAD + SEQ + half * 4 + 4])[n // 2]
                    if n:
                        pool.wait_ge(spread_out.sem, spread_out.value(l, n))
                    nc.gpsimd.tensor_tensor(
                        spread[:, :, :].rearrange("p (b h) m -> p b h m", b=4),
                        cv("pairs").unsqueeze(1).unsqueeze(1).broadcast_to([P, 4, 4, P]),
                        vec.rearrange("p h b -> p b h").unsqueeze(3).broadcast_to([P, 4, 4, P]), ALU.mult)\
                        .then_inc(spread_in.sem, 1)

                def conv_decoded(first, n, slot, out):
                    if slot:
                        pool.wait_ge(slot.sem, l + 1)
                    cdec, tmp = cx[:, first:first + n, SEQ:TOK], ctmp[:, first:first + n, :]
                    along = lambda name, at: pv(name, at + first, n).unsqueeze(2).broadcast_to([P, n, DEC])
                    own.done(nc.gpsimd.tensor_tensor(cdec, cbuf[:, 0, first:first + n, :], along("conv_w", 0), ALU.mult))
                    own.done(nc.gpsimd.tensor_tensor(cdec, cdec, along("conv_b", 0), ALU.add))
                    for i in range(1, 4):
                        own.done(nc.gpsimd.tensor_tensor(tmp, cbuf[:, i, first:first + n, :],
                                                         along("conv_w", 12 * i), ALU.mult))
                        last = nc.gpsimd.tensor_tensor(cdec, cdec, tmp, ALU.add)
                        if i < 3:
                            own.done(last)
                    last.then_inc(out.sem, 1)

                scale_z(l, RWKV_T, SSD_T)
                conv_decoded(0, 8, conv_slot, conv_dec)
                lx = lambda i: z[:, Z_LX:Z_LX + 4, i:i + SEQ]
                pool.wait_ge(sdt_read.sem, l + 1)
                nc.gpsimd.tensor_tensor(cx[:, 0:4, :], cx[:, 0:4, :], pb("d_skip", 4), ALU.mult).then_inc(skip_ready.sem, 1)
                scale_z(l, SSD_T, Z_LG)
                pool.wait_ge(z_ready.sem, z_ready.value(l, Z_LG - RWKV_T))
                own.done(nc.gpsimd.tensor_tensor(cx[:, 8:12, 0:SEQ], lx(0), pb("conv_w", 12, SEQ)[:, 8:12], ALU.mult))
                nc.gpsimd.tensor_copy(cps[:, 8:12, :], z[:, Z_LX:Z_LX + 4, LEAD + SEQ - 3:LEAD + SEQ])
                own.done(nc.gpsimd.tensor_copy(cbuf[:, 3, 8:12, :], zt(Z_LX, 4, SEQ, TOK)))
                nc.gpsimd.tensor_copy(pool_mark[:, :], ident[:, 0:1]).then_inc(lconv_slot.sem, 1)
                tap = part(zu, 4096 + DT * TOK, 4, SEQ)
                pool.wait_ge(conv_out.sem, l + 1)
                for i in range(1, 4):
                    own.done(nc.gpsimd.tensor_tensor(tap, lx(i), pb("conv_w", 48, SEQ)[:, 12 * i + 8:12 * i + 12], ALU.mult))
                    own.done(nc.gpsimd.tensor_tensor(cx[:, 8:12, 0:SEQ], cx[:, 8:12, 0:SEQ], tap, ALU.add))
                own.done(nc.gpsimd.tensor_tensor(cx[:, 8:12, 0:SEQ], cx[:, 8:12, 0:SEQ],
                                                 pb("conv_b", 12, SEQ)[:, 8:12], ALU.add))
                conv_decoded(8, 4, None, lconv_out)
                scale_z(l, Z_LG, ZT)
                lgz = zt(Z_LG, 4)
                pool.wait_ge(z_ready.sem, z_ready.value(l, ZT - RWKV_T))
                own.done(nc.gpsimd.tensor_tensor(lg, lgz, lgz, ALU.mult))
                own.done(nc.gpsimd.tensor_scalar(lg, lg, 0.044715, 1.0, ALU.mult, ALU.add))
                nc.gpsimd.tensor_tensor(lg, lg, lgz, ALU.mult).then_inc(gelu_in.sem, 1)
                pool.wait_ge(lri.sem, l + 1)
                nc.gpsimd.tensor_tensor(li, li, cx[:, 8:12, :], ALU.mult)
                pool.wait_ge(gelu_sig.sem, l + 1)
                nc.gpsimd.tensor_tensor(lgz, lgz, lg, ALU.mult).then_inc(lru_pre.sem, 1)
                for j in range(2):
                    pool.wait_ge(hi_ready.sem, l * SPLIT + j + 1)
                    nc.gpsimd.tensor_tensor(w_lo[:, j, :], ring[:, j, :], f32(w_hi[:, j, :]), ALU.subtract)\
                        .then_inc(lo_ready.sem, 1)
                for n, tiles in enumerate(((MIX_GLA, MIX_RWKV), (MIX_SSD,))):
                    pool.wait_ge(mix_hi_ready.sem, mix_hi_ready.value(l, n + 1))
                    for at in tiles:
                        last = nc.gpsimd.tensor_tensor(mix_lo[:, at:at + 4, :], mix[:, at:at + 4, :],
                                                       f32(mix_hi[:, at:at + 4, :]), ALU.subtract)
                last.then_inc(mix_split.sem, 1)
                for j in range(DT):
                    scale_h(l, 1, "mlp_pre", x_mid, j)
                pool.wait_ge(unit_done.sem, l * UNITS + ZT + DT)
                own.done(nc.gpsimd.tensor_tensor(pool_mark[:, :], ident[:, 0:1], ident[:, 0:1], ALU.mult))
                nc.gpsimd.memset(mix[:, :, :], 0.0).then_inc(y_clear.sem, 1)

        @block.vector
        def _(dve):
            v = nc.vector
            own = Own(dve, own_dve)

            def inv_rms(l, norm):
                dve.wait_ge(mean_ready.sem, mean_ready.value(l, norm + 1))
                v.tensor_scalar(rstd[:, :], ps[:, STAT, 0:TOK], 1.0 / D_MODEL, EPS, ALU.mult, ALU.add)\
                    .then_inc(rstd_in.sem, 1)
                dve.wait_ge(root_ready.sem, root_ready.value(l, norm + 1))
                own.done(v.reciprocal(rstd[:, :], rstd[:, :]))

            def in_weight_lo(l, unit, j):
                dve.wait_ge(in_hi_ready.sem, l * RWKV_T + unit + 1)
                v.tensor_tensor(w_lo[:, j, :], ring[:, j, :], f32(in_w_hi[:, j % 2, :]), ALU.subtract)\
                    .then_inc(in_lo_ready.sem, 1)

            def weight_lo(l, m, j):
                dve.wait_ge(hi_ready.sem, l * SPLIT + m + 1)
                v.tensor_tensor(w_lo[:, j, :], ring[:, j, :], f32(w_hi[:, j % 2, :]), ALU.subtract)\
                    .then_inc(lo_ready.sem, 1)

            def update_x(l, name, y, out, base):
                def add(j):
                    v.tensor_tensor(x[:, j:j + 2, :], x[:, j:j + 2, :], pre[:, j % 4:j % 4 + 2, :], ALU.add)\
                        .then_inc(out.sem, 2)

                for j in range(0, DT, 2):
                    if j >= 4:
                        dve.wait_ge(out.sem, base + j - 2)
                    for i in range(j, j + 2):
                        last = v.scalar_tensor_tensor(pre[:, i % 4, :], y[:, i, :], pv(name, i), rstd[:, :],
                                                      ALU.mult, ALU.mult)
                    last.then_inc(own.sem, 1)
                    own.n += 1
                    if j:
                        dve.wait_ge(own.sem, own.n - 1)
                        add(j - 2)
                dve.wait_ge(own.sem, own.n)
                add(DT - 2)

            v.memset(pre[:, 0, 0:1], 0.0).then_inc(bank_free.sem, 4)
            v.memset(pre[:, 1, 1:2], 0.0).then_inc(u_split.sem, 2)
            v.memset(pre[:, 1, 2:3], 0.0).then_inc(sq_used.sem, 2)
            dve.wait_ge(x_loaded.sem, 16)
            v.memset(pre[:, 2, 0:1], 0.0).then_inc(x_in.sem, DT)
            dve.wait_ge(consts_in.sem, 16)
            with dve.Fori(0, LAYERS) as l:
                own.restart()
                dve.wait_ge(gains_in.sem, l + 1)
                own.done(v.memset(z[:, :, 0:LEAD], 0.0))
                in_weight_lo(l, 0, 0)
                in_weight_lo(l, 1, 1)
                dve.wait_ge(x_saved.sem, l * 16 + 16)
                for j in range(4):
                    dve.wait_ge(in_h_hi_ready.sem, in_h_hi_ready.value(l, j + 1))
                    v.tensor_tensor(in_h_lo[:, 4 * j:4 * j + 4, :], hy3[:, 4 * j:4 * j + 4, :],
                                    f32(in_h_hi[:, 4 * j:4 * j + 4, :]), ALU.subtract).then_inc(in_h_split.sem, 1)
                inv_rms(l, NORM_MIX)
                def out_of_bank(unit, bank):
                    dve.wait_ge(unit_done.sem, l * UNITS + unit + 1)
                    v.tensor_tensor(z[:, bass.ds(unit, 1), LEAD:ZW].rearrange("p o t -> p (o t)"),
                                    ps[:, bank, 0:TOK], rstd[:, :], ALU.mult).then_inc(bank_free.sem, 1)

                with dve.Fori(0, RWKV_T // 4) as g:
                    for j in range(4):
                        out_of_bank(g * 4 + j, j)
                        in_weight_lo(l, g * 4 + j + 2, (j + 2) % 4)
                for unit in range(RWKV_T // 4 * 4, RWKV_T):
                    out_of_bank(unit, unit % 4)
                dve.wait_ge(bank_free.sem, l * bank_free.per_layer + RWKV_T + 4)
                dve.wait_ge(shift_in.sem, l * 16 + 16)
                own.done(v.tensor_copy(shifted[:, :, :], z[:, 0:RWKV_T, LEAD + SEQ - 1:ZW]))
                v.tensor_tensor(delta[:, :, 0:SEQ], z[:, 0:RWKV_T, LEAD - 1:LEAD - 1 + SEQ],
                                zt(0, RWKV_T, 0, SEQ), ALU.subtract).then_inc(shift_saved.sem, 1)
                own.done(v.tensor_tensor(delta[:, :, SEQ:TOK], prev[:, :, :], zt(0, RWKV_T, SEQ, TOK), ALU.subtract))
                own.done(v.tensor_tensor(delta, delta, pb("mu", RWKV_T), ALU.mult))
                v.tensor_tensor(zt(0, RWKV_T), zt(0, RWKV_T), delta, ALU.add).then_inc(zm_ready.sem, 1)
                dve.wait_ge(zm_ready.sem, l + 1)
                own.done(v.tensor_tensor(kk, zt(Z_K, 4), pb("k_k", 4), ALU.mult))
                dve.wait_ge(decay_sig.sem, l + 1)
                for h in range(4):
                    for c in range(NCH):
                        own.done(v.tensor_tensor_scan(cum[:, h, c, :], ones, sig[:, h, c * CH:c * CH + CH], 0.0,
                                                      ALU.mult, ALU.add))
                own.done(v.tensor_copy(mids[:, :, :], cum[:, :, :, CH // 2 - 1]))
                own.done(v.tensor_tensor(cum, cum, mids[:, :, :].unsqueeze(3).broadcast_to([P, 4, NCH, CH]),
                                         ALU.subtract))
                own.done(v.tensor_copy(ends[:, :, :], cum[:, :, :, CH - 1]))
                v.tensor_tensor(kr[:, :, :, 0, :], cum, sig[:, :, 0:SEQ].rearrange("p h (c t) -> p h c t", c=NCH),
                                ALU.subtract).then_inc(cum_ready.sem, 1)
                dve.wait_ge(rgate_out.sem, l + 1)
                v.tensor_tensor(rk, kk, kk, ALU.mult).then_inc(stat_in.sem, 1)
                dve.wait_ge(stat_root.sem, stat_root.value(l, 1))
                own.done(v.tensor_scalar(rows[0:8, :], rows[0:8, :], 1e-12, None, ALU.max))
                v.reciprocal(rows[0:8, :], rows[0:8, :]).then_inc(stat_row.sem, 1)
                dve.wait_ge(stat_wide.sem, stat_wide.value(l, KK))
                own.done(v.tensor_tensor(kk, kk, ps[:, 4:8, 0:TOK], ALU.mult))
                own.done(v.scalar_tensor_tensor(rk, rate, -1.0, pb("k_a", 4), ALU.add, ALU.mult))
                own.done(v.scalar_tensor_tensor(zt(Z_K, 4), rk, 1.0, zt(Z_K, 4), ALU.add, ALU.mult))
                own.done(v.tensor_tensor(kb, kk, rate, ALU.mult))
                own.done(v.tensor_copy(dec[:, 1, :, :], kk[:, :, SEQ:TOK]))
                own.done(v.tensor_copy(dec[:, 2, :, :], kb[:, :, SEQ:TOK]))
                own.done(v.tensor_tensor(rk, zt(Z_R, 4), zt(Z_K, 4), ALU.mult))
                own.done(v.tensor_tensor(rk, rk, pb("r_k", 4), ALU.mult))
                dve.wait_ge(exps_ready.sem, l + 1)
                chunks = lambda t: t.rearrange("p h (c t) -> p h c t", c=NCH)
                own.done(v.tensor_tensor(bt, kt, chunks(kb[:, :, 0:SEQ]), ALU.mult))
                own.done(v.tensor_tensor(kt, kt, chunks(zt(Z_K, 4, 0, SEQ)), ALU.mult))
                own.done(v.tensor_tensor(kr[:, :, :, 1, :], kr[:, :, :, 1, :], chunks(zt(Z_R, 4, 0, SEQ)), ALU.mult))
                v.tensor_tensor(kr[:, :, :, 0, :], kr[:, :, :, 0, :], chunks(kk[:, :, 0:SEQ]), ALU.mult)\
                    .then_inc(operands_ready.sem, 1)

                def along(vec):
                    return vec.rearrange("p h b -> p b h").unsqueeze(3).broadcast_to([P, vec.shape[2], 4, 64])

                hd4 = hdec.rearrange("p (b h) v -> p b h v", b=DEC)
                td4 = tdec.rearrange("p (b h) v -> p b h v", b=DEC)

                def spread_ps(half):
                    return ps[:, 4 + 2 * half:6 + 2 * half, :].rearrange("p a (b h v) -> p (a b) h v", b=2, h=4)

                for n in range(2):
                    dve.wait_ge(spread_out.sem, spread_out.value(l, n + 1))
                    v.tensor_tensor(td4[:, n * 4:n * 4 + 4], spread_ps(n), along(dec[:, 2, :, n * 4:n * 4 + 4]),
                                    ALU.mult).then_inc(spread_read.sem, 1)
                own.done(v.tensor_tensor(hd4, hd4, along(dec[:, 0, :, :]), ALU.mult))
                own.done(v.tensor_tensor(hdec, hdec, tdec, ALU.subtract))
                for n in range(2):
                    dve.wait_ge(spread_out.sem, spread_out.value(l, n + 3))
                    kn = z[:, Z_K:Z_K + 4, LEAD + SEQ + n * 4:LEAD + SEQ + n * 4 + 4]
                    v.tensor_tensor(td4[:, n * 4:n * 4 + 4], spread_ps(n), along(kn), ALU.mult)\
                        .then_inc(spread_read.sem, 1)
                dve.wait_ge(spread_read.sem, spread_read.value(l, 4))
                v.tensor_tensor(hdec, hdec, tdec, ALU.add).then_inc(rdec_ready.sem, 1)
                for n in range(2):
                    dve.wait_ge(spread_out.sem, spread_out.value(l, n + 5))
                    half = tdec[:, n * 16:n * 16 + 16, :]
                    v.tensor_tensor(half, ps[:, 4 + 2 * n:6 + 2 * n, :].rearrange("p a (i v) -> p (a i) v", v=64),
                                    cv("stack").unsqueeze(1).broadcast_to([P, 16, 64]), ALU.mult)\
                        .then_inc(spread_read.sem, 1)
                dve.wait_ge(spread_read.sem, spread_read.value(l, 6))
                own.done(v.tensor_reduce(dec[:, 0, :, :].rearrange("p h b -> p b h"), td4, AX.X, ALU.add))

                for c in range(NCH):
                    if c == 0:
                        dve.wait_ge(stored, l * 16 * STORES + 32)
                    dve.wait_ge(score1_mm.sem, score1_mm.value(l, c + 1))
                    both = cv("upper_both").unsqueeze(1).broadcast_to([P, 8, 256])
                    v.tensor_tensor(sc1.rearrange("p i j t -> p i (j t)"),
                                    ps[:, 4:8, :].rearrange("p a (i t) -> p (a i) t", i=2), both, ALU.mult)\
                        .then_inc(score1.sem, 1)
                    dve.wait_ge(score2_mm.sem, score2_mm.value(l, c + 1))
                    v.tensor_tensor(sc2.rearrange("p i j t -> p i (j t)"),
                                    ps[:, 4:8, :].rearrange("p a (i t) -> p (a i) t", i=2), both, ALU.mult)\
                        .then_inc(score2.sem, 1)
                    idents = lambda n: ident.unsqueeze(1).broadcast_to([P, n, P])
                    level = lambda name, j, n: cv(name, j * P, P).unsqueeze(1).broadcast_to([P, n, P])
                    dve.wait_ge(score2.sem, score2.value(l, c + 1))
                    own.done(v.tensor_tensor(xx[:, :, 1, :], sc2[:, :, 0, :], level("level_up", 0, 8), ALU.mult))
                    own.done(v.tensor_tensor(xx[:, :, 1, :], idents(8), xx[:, :, 1, :], ALU.subtract))
                    for j in range(LEVELS):
                        n, nd = (c * LEVELS + j) * 2, (c * (LEVELS - 1) + j - 1) * 2
                        for half in range(2):
                            hs = slice(4 * half, 4 * half + 4)
                            dve.wait_ge(q_mm.sem, q_mm.value(l, n + 1 + half))
                            v.tensor_tensor(qb[:, hs, :], ps[:, 4 + half, :].rearrange("p (i t) -> p i t", i=4),
                                            level("level_low", j, 4), ALU.mult).then_inc(q_out.sem, 1)
                        for half in range(2):
                            hs = slice(4 * half, 4 * half + 4)
                            if j == 0:
                                dve.wait_ge(q_out.sem, q_out.value(l, n + 1 + half))
                                v.tensor_tensor(xx[:, hs, 0, :], idents(4), qb[:, hs, :], ALU.subtract)\
                                    .then_inc(dx_out.sem, 1)
                                continue
                            dve.wait_ge(dx_mm.sem, dx_mm.value(l, nd + 1 + half))
                            first = 1 if j == LEVELS - 1 else 0
                            xh = xx[:, hs, first:2, :]
                            v.tensor_tensor(xh, xh, ps[:, 6:8, :].rearrange("p a (i j t) -> p (a i) j t", i=2, j=2)
                                            [:, :, first:2, :], ALU.subtract).then_inc(dx_out.sem, 1)
                    dve.wait_ge(ry_mm.sem, ry_mm.value(l, c + 1))
                    hv = ps[:, 6, :].rearrange("p (h m) -> p h m", h=4)
                    for a in range(2):
                        r = slice(64 * a, 64 * a + 64)
                        if c:
                            own.done(v.tensor_tensor(hst[r], hst[r], hv[r, :, 64 * a:64 * a + 64], ALU.add))
                        else:
                            own.done(v.tensor_copy(hst[r], hv[r, :, 64 * a:64 * a + 64]))
                    last = v.tensor_tensor(hst, hst, ends[:, :, c].unsqueeze(2).broadcast_to([P, 4, 64]), ALU.mult)
                    if c < NCH - 1:
                        own.done(last)
                        last = v.tensor_tensor(hst, hst, mids[:, :, c + 1].unsqueeze(2).broadcast_to([P, 4, 64]),
                                               ALU.mult)
                    last.then_inc(rh_out.sem, 1)

                dve.wait_ge(ryT_out.sem, ryT_out.value(l, NCH))
                v.tensor_copy(yfm[:, :, SEQ:TOK], dec[:, 0, :, :]).then_inc(stat_in.sem, 1)
                dve.wait_ge(stat_sum.sem, stat_sum.value(l, MEAN))
                v.tensor_scalar(rows[0:8, :], ps[0:8, 4, 0:TOK], 1.0 / 64, None, ALU.mult).then_inc(stat_row.sem, 1)
                dve.wait_ge(stat_wide.sem, stat_wide.value(l, MEAN))
                v.tensor_tensor(yfm, yfm, ps[:, 4:8, 0:TOK], ALU.subtract).then_inc(centred.sem, 1)
                dve.wait_ge(stat_sum.sem, stat_sum.value(l, VAR))
                v.tensor_scalar(rows[0:8, :], ps[0:8, 4, 0:TOK], 1.0 / 64, LN_EPS, ALU.mult, ALU.add)\
                    .then_inc(stat_mid.sem, 1)
                dve.wait_ge(stat_root.sem, stat_root.value(l, 2))
                v.reciprocal(rows[0:8, :], rows[0:8, :]).then_inc(stat_row.sem, 1)
                dve.wait_ge(stat_wide.sem, stat_wide.value(l, VAR))
                v.tensor_tensor(yfm, yfm, ps[:, 4:8, 0:TOK], ALU.mult).then_inc(stat_in.sem, 1)
                dve.wait_ge(stat_in.sem, stat_in.value(l, BONUS))
                own.done(v.tensor_tensor(yfm, yfm, pb("ln_w", 4), ALU.mult))
                own.done(v.tensor_tensor(yfm, yfm, pb("ln_b", 4), ALU.add))
                dve.wait_ge(stat_sum.sem, stat_sum.value(l, BONUS))
                v.tensor_copy(rows[0:8, :], ps[0:8, 4, 0:TOK]).then_inc(stat_row.sem, 1)
                dve.wait_ge(stat_wide.sem, stat_wide.value(l, BONUS))
                v.tensor_tensor(rk, zt(Z_V, 4), ps[:, 4:8, 0:TOK], ALU.mult).then_inc(bonus_read.sem, 1)
                dve.wait_ge(bonus_read.sem, l + 1)
                own.done(v.tensor_tensor(yfm, yfm, rk, ALU.add))
                own.done(v.tensor_tensor(gate, gate, yfm, ALU.mult))


                dve.wait_ge(z_ready.sem, z_ready.value(l, GLA_T - RWKV_T))
                dve.wait_ge(ggate_mm.sem, l + 1)
                v.tensor_tensor(glog, ps[:, 4:6, 0:TOK], pb("gla_b", 2), ALU.add).then_inc(ggate_x.sem, 1)
                own.done(v.memset(gsc, 0.0))
                own.done(v.tensor_scalar(zt(Z_GQ, 2), zt(Z_GQ, 2), 0.125, None, ALU.mult))
                dve.wait_ge(gsig.sem, l + 1)
                gate_gla = mix[:, MIX_GLA:MIX_GLA + 4, :]
                own.done(v.tensor_tensor(gate_gla, gate_gla, zt(Z_GG, 4), ALU.mult))
                dve.wait_ge(ggate_ln.sem, l + 1)
                own.done(v.scalar_tensor_tensor(glog, glog, 0.0, gtmp, ALU.min, ALU.subtract))
                for hp in range(2):
                    for c in range(NCH):
                        last = v.tensor_tensor_scan(gcum4[:, hp, c, :], ones, glog[:, hp, c * CH:c * CH + CH], 0.0,
                                                    ALU.mult, ALU.add)
                own.done(last)
                for j in range(LEVELS):
                    b = 1 << j
                    cum_b = gcum.rearrange("p (n m) -> p n m", m=2 * b)
                    v.tensor_tensor(part(xs, j * 512, 512).rearrange("p (n m) -> p n m", m=2 * b), cum_b,
                                    cum_b[:, :, b - 1:b].broadcast_to([P, 256 // b, 2 * b]), ALU.subtract)
                v.tensor_tensor(gkdT, gcum4, gcum4[:, :, :, CH - 1:CH].broadcast_to([P, 2, NCH, CH]), ALU.subtract)\
                    .then_inc(gdist.sem, 1)
                dve.wait_ge(gdist_exp.sem, l + 1)
                gk, gq = zt(Z_GK, 2, 0, SEQ), zt(Z_GQ, 2, 0, SEQ)
                own.done(v.tensor_tensor(kdist, dist, gk.unsqueeze(1).broadcast_to([P, LEVELS, 2, SEQ]), ALU.mult))
                own.done(v.tensor_tensor(dist, dist, gq.unsqueeze(1).broadcast_to([P, LEVELS, 2, SEQ]), ALU.mult))
                own.done(v.tensor_tensor(gqc, gqc, gq.rearrange("p h (c t) -> p h c t", c=NCH), ALU.mult))
                v.tensor_tensor(gkdT, gkdT, gk.rearrange("p h (c t) -> p h c t", c=NCH), ALU.mult)\
                    .then_inc(gops.sem, 1)
                for j in range(LEVELS + 1):
                    mask = cv("level_up", j * P, P) if j < LEVELS else ident
                    dve.wait_ge(glevel_mm.sem, glevel_mm.value(l, j + 1))
                    own.done(v.memset(pre[:, 3, 0:1], 0.0))
                    bank = 4 + 2 * (j % 2)
                    v.copy_predicated(gsc, mask.bitcast(I32).unsqueeze(1).broadcast_to([P, 8, P]),
                                      ps[:, bank:bank + 2, :].rearrange("p a (i t) -> p (a i) t", t=P))\
                        .then_inc(glevel.sem, 1)
                for c in range(NCH):
                    dve.wait_ge(gy_mm.sem, gy_mm.value(l, c + 1))
                    if c:
                        own.done(v.tensor_tensor(gst, gst, glast[:, :, c].unsqueeze(2).broadcast_to([P, 2, P]), ALU.mult))
                    hv = ps[:, 6, :].rearrange("p (h m) -> p h m", h=2)
                    for a in range(2):
                        r = slice(64 * a, 64 * a + 64)
                        if c:
                            last = v.tensor_tensor(gst[r], gst[r], hv[r, :, P * a:P * a + P], ALU.add)
                        else:
                            last = v.tensor_copy(gst[r], hv[r, :, P * a:P * a + P])
                    last.then_inc(gh_out.sem, 1)
                ghd4 = ghd.rearrange("p (b h) v -> p b h v", b=DEC)
                gtd4 = gtd.rearrange("p (b h) v -> p b h v", b=DEC)
                for n in range(4):
                    dve.wait_ge(gval_mm.sem, gval_mm.value(l, n + 1))
                    vals = ps[:, 4 + 2 * (n % 2):6 + 2 * (n % 2), :].rearrange("p b (h a v) -> p b h a v", h=2, a=2)
                    kn = z[:, Z_GK:Z_GK + 2, LEAD + SEQ + n * 2:LEAD + SEQ + n * 2 + 2]\
                        .rearrange("p h b -> p b h").unsqueeze(3).broadcast_to([P, 2, 2, P])
                    for a in range(2):
                        r = slice(64 * a, 64 * a + 64)
                        last = v.tensor_tensor(gtd4[r, n * 2:n * 2 + 2], vals[r, :, :, a, :], kn[r], ALU.mult)
                    last.then_inc(gval_read.sem, 1)
                dve.wait_ge(gstate_in.sem, l * 16 + 16)
                own.done(v.tensor_tensor(ghd4, ghd4, gdec[:, :, :].rearrange("p h b -> p b h").unsqueeze(3)
                                         .broadcast_to([P, DEC, 2, P]), ALU.mult))
                v.tensor_tensor(ghd, ghd, gtd, ALU.add).then_inc(gdec_ready.sem, 1)
                dve.wait_ge(stat_sum.sem, stat_sum.value(l, GLA_RMS))
                v.tensor_scalar(rows[0:4, :], ps[0:4, 4, 0:TOK], 1.0 / P, EPS, ALU.mult, ALU.add)\
                    .then_inc(stat_mid.sem, 1)
                dve.wait_ge(stat_root.sem, stat_root.value(l, 3))
                v.reciprocal(rows[0:4, :], rows[0:4, :]).then_inc(stat_row.sem, 1)
                dve.wait_ge(stat_wide.sem, stat_wide.value(l, GLA_RMS))
                own.done(v.tensor_scalar(gof, gof, pv("gla_norm"), None, ALU.mult))
                own.done(v.tensor_tensor(gof, gof, ps[:, 4:8, 0:TOK], ALU.mult))
                own.done(v.tensor_tensor(gate_gla, gate_gla, gof, ALU.mult))

                dve.wait_ge(z_ready.sem, z_ready.value(l, SSD_T - RWKV_T))
                dve.wait_ge(conv_in.sem, l * 16 + 16)

                def conv(first, n, zf, slot):
                    v.tensor_copy(cps[:, first:first + n, :], z[:, zf:zf + n, LEAD + SEQ - 3:LEAD + SEQ])
                    v.tensor_copy(cbuf[:, 3, first:first + n, :], zt(zf, n, SEQ, TOK)).then_inc(slot.sem, 1)
                    for i in range(4):
                        for t in range(first, first + n):
                            src = z[:, conv_z(t), i:i + SEQ]
                            w = pv("conv_w", 12 * i + t)
                            if i == 0:
                                last = v.tensor_scalar(cx[:, t, 0:SEQ], src, w, pv("conv_b", t), ALU.mult, ALU.add)
                            else:
                                last = v.scalar_tensor_tensor(cx[:, t, 0:SEQ], src, w, cx[:, t, 0:SEQ], ALU.mult, ALU.add)
                        own.done(last)

                conv(0, 8, Z_SX, conv_slot)
                dve.wait_ge(conv_dec.sem, l + 1)
                v.tensor_scalar(dtr[0:8, :], z[0:8, Z_DT, LEAD:ZW], pv("dt_bias", rows=8), None, ALU.add)\
                    .then_inc(conv_out.sem, 1)

                dve.wait_ge(conv_out.sem, l + 1)
                gate_ssd = mix[:, MIX_SSD:MIX_SSD + 4, :]
                dve.wait_ge(ssig.sem, l + 1)
                own.done(v.tensor_tensor(gate_ssd, gate_ssd, zt(Z_SG, 4), ALU.mult))
                v.tensor_tensor(cx[:, 0:8, :], cx[:, 0:8, :], stmp, ALU.mult).then_inc(sdt_x.sem, 1)
                own.done(v.tensor_scalar(lam8[:, :], pv("lam", n=4), -1.0, 0.0, ALU.mult, ALU.max))
                dve.wait_ge(lam_abs.sem, l + 1)
                own.done(v.tensor_tensor(lam8[:, :], lam8[:, :], lamt[:, :], ALU.add))
                own.done(v.tensor_scalar(lamn[:, :], lam8[:, :], -LRU_C, None, ALU.mult))
                v.tensor_scalar(lam8[:, :], lam8[:, :], LRU_C, None, ALU.mult).then_inc(lam_ready.sem, 1)
                dve.wait_ge(sdt_ln.sem, l + 1)
                own.done(v.scalar_tensor_tensor(dtr[0:8, :], dtr[0:8, :], 0.0, dcum[0:8, :], ALU.max, ALU.add))
                own.done(v.tensor_scalar(rows[0:8, :], dtr[0:8, :], acol[0:8, :], -1.0, ALU.mult, ALU.mult))
                for c in range(NCH):
                    last = v.tensor_tensor_scan(dcum[0:8, c * CH:c * CH + CH], ones[0:8, :],
                                                rows[0:8, c * CH:c * CH + CH], 0.0, ALU.mult, ALU.add)
                own.done(last)
                v.tensor_copy(dcum[0:8, SEQ:TOK], rows[0:8, SEQ:TOK]).then_inc(sdt_c.sem, 1)
                dve.wait_ge(sdt_mm.sem, l + 1)
                v.tensor_tensor(xdt, cx[:, 0:4, :], ps[:, 4:8, 0:TOK], ALU.mult).then_inc(sdt_read.sem, 1)
                dve.wait_ge(sdec_mm.sem, l + 1)
                v.tensor_copy(sdec[:, :, :], ps[:, 4, 0:4 * DEC].rearrange("p (h b) -> p h b", h=4))
                v.tensor_copy(cumT[:, :, :], ps[:, 5, 0:NCH * 8].rearrange("p (c h) -> p c h", c=NCH))\
                    .then_inc(sdec_read.sem, 1)
                dve.wait_ge(srow_mm.sem, l + 1)
                rowps = ps[:, 4:8, :].rearrange("p a (i c t) -> p (a i) c t", i=2, c=NCH)
                own.done(v.tensor_copy(lastv[:, :, :], rowps[:, :, :, CH - 1].rearrange("p h c -> p c h")))
                for h in range(8):
                    for c in range(NCH):
                        v.tensor_scalar(seg[:, h, c, :], rowps[:, h, c, :], cumT[:, c, h:h + 1], 0.0,
                                        ALU.subtract, ALU.min)
                v.tensor_tensor(wdec[:, :, :], lastv[:, :, :], cumT[:, :, :], ALU.subtract).then_inc(srow_read.sem, 1)
                dve.wait_ge(ssc_mm.sem, l + 1)
                own.done(v.tensor_tensor(ssc.rearrange("p g c t -> p (g c) t"),
                                         ps[:, 4, :].rearrange("p (i t) -> p i t", i=4),
                                         cv("upper_both", P, P).unsqueeze(1).broadcast_to([P, 4, P]), ALU.mult))
                dve.wait_ge(sexps.sem, l + 1)
                segv = seg.rearrange("p (g h) c t -> p g h (c t)", g=2)
                own.done(v.tensor_tensor(segv, segv, ssc.rearrange("p g c t -> p g (c t)").unsqueeze(2)
                                         .broadcast_to([P, 2, 4, SEQ]), ALU.mult))
                dve.wait_ge(stok.sem, l + 1)
                v.tensor_tensor(xd.rearrange("p c (h v) -> p c h v", h=8), xtok.rearrange("p c (h v) -> p c h v", h=8),
                                wdec[:, :, :].unsqueeze(3).broadcast_to([P, NCH, 8, 64]), ALU.mult)\
                    .then_inc(sops.sem, 1)
                for c in range(NCH):
                    dve.wait_ge(sy_mm.sem, sy_mm.value(l, c + 1))
                    by_head = lambda t: t.rearrange("p (h v) -> p h v", h=8)
                    if c:
                        own.done(v.tensor_tensor(by_head(yoff), by_head(ps[:, 5, :]),
                                                 ecum[:, c, :].unsqueeze(2).broadcast_to([P, 8, 64]), ALU.mult))
                        v.tensor_tensor(syt, yoff, ps[:, 4, :], ALU.add).then_inc(sy_out.sem, 1)
                        own.done(v.tensor_tensor(by_head(sst), by_head(sst),
                                                 elast[:, c, :].unsqueeze(2).broadcast_to([P, 8, 64]), ALU.mult))
                        v.tensor_tensor(sst, sst, ps[:, 6, :], ALU.add).then_inc(sh_out.sem, 1)
                    else:
                        v.tensor_copy(syt, ps[:, 4, :]).then_inc(sy_out.sem, 1)
                        v.tensor_copy(sst, ps[:, 6, :]).then_inc(sh_out.sem, 1)
                dve.wait_ge(sstate_in.sem, l * 16 + 16)
                shd4 = shd.rearrange("p (b h) n -> p b h n", b=DEC)
                own.done(v.tensor_tensor(shd4, shd4, sdec[:, :, :].rearrange("p h b -> p b h").unsqueeze(3)
                                         .broadcast_to([P, DEC, 4, P]), ALU.mult))
                std4 = std.rearrange("p (b h) n -> p b h n", b=4)
                for n in range(4):
                    b0 = (n % 2) * 4
                    dve.wait_ge(sbc_mm.sem, sbc_mm.value(l, n + 1))
                    bc = ps[:, 4 + 2 * (n % 2):6 + 2 * (n % 2), :].rearrange("p a (b g n) -> p (a b) g n", b=2, g=2)
                    for g in range(2):
                        hs = slice(2 * g, 2 * g + 2)
                        other = xdt[:, hs, SEQ + b0:SEQ + b0 + 4].rearrange("p h b -> p b h").unsqueeze(3)\
                            .broadcast_to([P, 4, 2, P]) if n < 2 else shd4[:, b0:b0 + 4, hs, :]
                        last = v.tensor_tensor(std4[:, :, hs, :], bc[:, :, g, :].unsqueeze(2).broadcast_to([P, 4, 2, P]),
                                               other, ALU.mult)
                    if n < 2:
                        own.done(last)
                        v.tensor_tensor(shd4[:, b0:b0 + 4], shd4[:, b0:b0 + 4], std4, ALU.add)\
                            .then_inc(sbc_read.sem, 1)
                        dve.wait_ge(sbc_read.sem, sbc_read.value(l, n + 1))
                    else:
                        last.then_inc(sbc_read.sem, 1)
                        dve.wait_ge(sbc_read.sem, sbc_read.value(l, n + 1))
                        own.done(v.tensor_reduce(syf[:, :, SEQ + b0:SEQ + b0 + 4].rearrange("p h b -> p b h"), std4,
                                                 AX.X, ALU.add))
                dve.wait_ge(syT_out.sem, syT_out.value(l, NCH))
                dve.wait_ge(skip_ready.sem, l + 1)
                own.done(v.tensor_tensor(syf, syf, cx[:, 0:4, :], ALU.add))
                v.tensor_tensor(syf, syf, gate_ssd, ALU.mult).then_inc(sdec_done.sem, 1)

                lgz = zt(Z_LG, 4)
                dve.wait_ge(lexp.sem, l + 1)
                own.done(v.tensor_scalar(lm, lth, 1.0, None, ALU.add))
                own.done(v.reciprocal(lm, lm))

                dve.wait_ge(stat_sum.sem, stat_sum.value(l, SSD_RMS))
                v.tensor_scalar(rows[0:1, :], ps[0:1, 4, 0:TOK], 1.0 / 512, EPS, ALU.mult, ALU.add)\
                    .then_inc(stat_mid.sem, 1)
                v.scalar_tensor_tensor(lm, lm, 2.0, lth, ALU.mult, ALU.mult).then_inc(lmul.sem, 1)
                dve.wait_ge(stat_root.sem, stat_root.value(l, 4))
                v.reciprocal(rows[0:1, :], rows[0:1, :]).then_inc(stat_row.sem, 1)
                own.done(v.tensor_tensor(syf, syf, pb("ssd_norm", 4), ALU.mult))
                dve.wait_ge(stat_wide.sem, stat_wide.value(l, SSD_RMS))
                v.tensor_tensor(gate_ssd, syf, ps[:, 4, 0:TOK].unsqueeze(1).broadcast_to([P, 4, TOK]), ALU.mult)\
                    .then_inc(ssd_mixed.sem, 1)

                dve.wait_ge(lru_in.sem, l * 16 + 16)
                dve.wait_ge(lru_pre.sem, l + 1)
                dve.wait_ge(lroot.sem, l + 1)
                own.done(v.memset(lm[:, :, 0:1], 1.0))
                own.done(v.tensor_tensor(li, li, lm, ALU.mult))
                for t in range(4):
                    v.tensor_tensor_scan(lh[:, t, 0:SEQ], la[:, t, 0:SEQ], li[:, t, 0:SEQ], 0.0, ALU.mult, ALU.add)
                own.done(v.tensor_tensor(lh[:, :, SEQ:TOK], la[:, :, SEQ:TOK], h0[:, :, :], ALU.mult))
                own.done(v.tensor_tensor(lh[:, :, SEQ:TOK], lh[:, :, SEQ:TOK], li[:, :, SEQ:TOK], ALU.add))
                v.tensor_copy(lout[:, :, :], lh[:, :, SEQ - 1:TOK]).then_inc(lru_saved.sem, 1)
                v.tensor_tensor(mix[:, MIX_LRU:MIX_LRU + 4, :], lh, lgz, ALU.mult).then_inc(mixed.sem, 1)
                dve.wait_ge(mix_hi_ready.sem, mix_hi_ready.value(l, 3))
                v.tensor_tensor(mix_lo[:, MIX_LRU:MIX_LRU + 4, :], mix[:, MIX_LRU:MIX_LRU + 4, :],
                                f32(mix_hi[:, MIX_LRU:MIX_LRU + 4, :]), ALU.subtract).then_inc(mix_split.sem, 1)
                with dve.Fori(0, DT // 4) as g:
                    for j in range(4):
                        weight_lo(l, g * 4 + j + 2, (j + 2) % 4)
                inv_rms(l, NORM_MIX_POST)
                dve.wait_ge(x_back.sem, l * 16 + 16)
                update_x(l, "mix_post", hy3, x_mid, l * DT)
                for j in range(4):
                    dve.wait_ge(h_hi_ready.sem, h_hi_ready.value(l, j + 1))
                    v.tensor_tensor(h_lo[:, 4 * j:4 * j + 4, :], hy3[:, 4 * j:4 * j + 4, :], f32(h_hi[:, 4 * j:4 * j + 4, :]),
                                    ALU.subtract).then_inc(h_split.sem, 1)
                inv_rms(l, NORM_MLP)
                dve.wait_ge(y_clear.sem, l + 1)

                def up(q):
                    with dve.Fori(0, DT // 4) as g:
                        for j in range(4):
                            m = DT + q * 2 * DT + g * 4 + j
                            dve.wait_ge(unit_done.sem, l * UNITS + ZT + m + 1)
                            v.scalar_tensor_tensor(pre[:, j, :], ps[:, j, 0:TOK], 0.0, rstd[:, :],
                                                   ALU.max, ALU.mult).then_inc(bank_free.sem, 1)
                            weight_lo(l, m + 2, (j + 2) % 4)
                            dve.wait_ge(u_hi_ready.sem, l * FT + q * DT + g * 4 + j + 1)
                            at = bass.ds(g * 4 + j, 1)
                            v.tensor_tensor(u_lo[:, at, :].rearrange("p o t -> p (o t)"), sq[:, j % 2, :],
                                            f32(u_hi[:, at, :].rearrange("p o t -> p (o t)")), ALU.subtract)\
                                .then_inc(u_split.sem, 1)

                def add_y(m, tile, j):
                    dve.wait_ge(unit_done.sem, l * UNITS + ZT + m + 1)
                    at = y3[:, bass.ds(tile, 1), :].rearrange("p o t -> p (o t)")
                    v.tensor_tensor(at, at, ps[:, j, 0:TOK], ALU.add).then_inc(bank_free.sem, 1)

                def down(q, groups):
                    with dve.Fori(0, groups) as g:
                        for j in range(4):
                            m = 2 * DT + q * 2 * DT + g * 4 + j
                            add_y(m, g * 4 + j, j)
                            weight_lo(l, m + 2, (j + 2) % 4)

                with dve.Fori(0, QUARTERS - 1) as q:
                    up(q)
                    down(q, DT // 4)
                up(QUARTERS - 1)
                down(QUARTERS - 1, DT // 4 - 1)
                for j in range(4):
                    m = SPLIT - 4 + j
                    add_y(m, DT - 4 + j, j)
                    if j < 2:
                        weight_lo(l, m + 2, j + 2)
                inv_rms(l, NORM_MLP_POST)
                update_x(l, "mlp_post", y3, x_in, (l + 1) * DT)


def _tiles(a):
    return np.swapaxes(a.reshape(a.shape[:-1] + (-1, P)), -1, -2)


def _weights(w_in, w_out, w_up, w_down):
    L = LAYERS
    gla, lru, rwkv, ssd = 0, 1552, 2576, 4368
    out = np.zeros((L, UNITS, P, DT, P), np.float32)

    def columns(first, w):
        n = w.shape[2] // P
        out[:, first:first + n] = w.reshape(L, DT, P, n, P).transpose(0, 3, 2, 1, 4)

    columns(Z_R, w_in[:, :, rwkv:rwkv + 14 * P])
    columns(Z_GQ, w_in[:, :, gla:gla + 12 * P])
    out[:, Z_GA, :, :, 0:16] = w_in[:, :, gla + 12 * P:gla + 12 * P + 16].reshape(L, DT, P, 16).transpose(0, 2, 1, 3)
    columns(Z_SG, w_in[:, :, ssd:ssd + 12 * P])
    out[:, Z_DT, :, :, 0:8] = w_in[:, :, ssd + 12 * P:ssd + 12 * P + 8].reshape(L, DT, P, 8).transpose(0, 2, 1, 3)
    columns(Z_LX, w_in[:, :, lru:lru + 8 * P])
    columns(ZT, w_out)
    mlp = out[:, ZT + DT:].reshape(L, QUARTERS, 2, DT, P, DT, P)
    mlp[:, :, 0] = w_up.reshape(L, DT, P, QUARTERS, DT, P).transpose(0, 3, 4, 2, 1, 5)
    mlp[:, :, 1] = w_down.reshape(L, QUARTERS, DT, P, DT, P).transpose(0, 1, 4, 3, 2, 5)
    return out.reshape(L * UNITS, P, DT * P)


def _params(i):
    L = LAYERS
    out = np.zeros((L, P, N_PARAM), np.float32)

    def put(name, a):
        at, n = PARAM[name]
        out[:, 0:a.shape[1], at:at + a.shape[2]] = a

    def block(w):
        full = np.zeros((L, P, 4, P), np.float32)
        full[:, 0:64, :, 0:64] = w[:, 0::2].transpose(0, 2, 1, 3)
        full[:, 64:, :, 64:] = w[:, 1::2].transpose(0, 2, 1, 3)
        return full.reshape(L, P, 512)

    for name, key in [("mix_pre", "norm_mix_pre"), ("mix_post", "norm_mix_post"), ("mlp_pre", "norm_mlp_pre"),
                      ("mlp_post", "norm_mlp_post"), ("mu", "rwkv_mu"), ("w0", "rwkv_w0"), ("a0", "rwkv_a0"),
                      ("k_k", "rwkv_k_k"), ("k_a", "rwkv_k_a"), ("ln_w", "rwkv_ln_w"), ("ln_b", "rwkv_ln_b"),
                      ("gla_b", "gla_b_gate"), ("gla_norm", "gla_norm"), ("b_a", "lru_b_a"), ("b_i", "lru_b_i"),
                      ("lam", "lru_lambda"), ("ssd_norm", "ssd_norm")]:
        put(name, _tiles(i[key]))
    put("r_k", _tiles(i["rwkv_r_k"].reshape(L, 512)))
    put("d_skip", _tiles(np.repeat(i["ssd_d"], 64, axis=1)))
    put("conv_b", np.concatenate([_tiles(i["ssd_conv_b"]), _tiles(i["lru_conv_b"])], 2))
    conv = np.concatenate([_tiles(i["ssd_conv_w"]), _tiles(i["lru_conv_w"])], 3)
    put("conv_w", conv.transpose(0, 2, 1, 3).reshape(L, P, 48))
    put("dt_bias", i["ssd_dt_bias"][:, :, None])
    put("a_log", i["ssd_a_log"][:, :, None])
    put("wa2", np.concatenate([i["rwkv_w2"], i["rwkv_a2"]], 1))
    put("g2", i["rwkv_g2"])
    put("gate2", i["gla_w_gate2"])
    put("lru_wa", block(i["lru_w_a"]))
    put("lru_wi", block(i["lru_w_i"]))
    return out


def _consts():
    out = np.zeros((P, N_CONST), np.float32)

    def put(name, a):
        at, n = CONST[name]
        out[0:a.shape[0], at:at + n] = a.reshape(a.shape[0], n)

    i = np.arange(P)
    put("ident", np.eye(P))
    put("ones", np.ones((P, P)))
    put("pairs", i[:, None] // 64 == i[None, :] // 64)
    put("stack", i[:, None] % 64 == np.arange(64)[None, :])
    h = np.arange(8)
    put("head_sum", (2 * np.arange(4)[None, :, None] + i[:, None, None] // 64) == h[None, None, :])
    put("head_row", (2 * np.arange(4)[None, :, None] + i[None, None, :] // 64) == h[:, None, None])
    put("tile_sum", np.broadcast_to(np.arange(4)[None, :, None] == np.arange(4)[None, None, :], (P, 4, 4)))
    up = i[:, None] <= i[None, :]
    put("upper_both", np.concatenate([i[:, None] < i[None, :], up], 1))
    lv = []
    for j in range(LEVELS):
        b = 1 << j
        s, t = i[:, None], i[None, :]
        lv.append((s // (2 * b) == t // (2 * b)) & (s // b % 2 == 0) & (t // b % 2 == 1))
    lv = np.stack(lv)
    put("level_up", lv.transpose(1, 0, 2))
    put("level_low", lv.transpose(2, 0, 1))
    return out


def _keyed(s):
    L, B, H, K, V = s.shape
    return s.reshape(L, B, H // 2, 2, K, V).transpose(0, 3, 4, 1, 2, 5).reshape(L, P, B * (H // 2) * V)


def kernel(**inputs):
    import concourse.bacc as bacc
    from concourse.bass_utils import run_bass_kernel_spmd

    i = {k: np.asarray(v) for k, v in inputs.items()}
    L = LAYERS
    x = np.concatenate([i["x_prompt"][0], i["x_sample"][:, 0]], 0)
    conv = np.concatenate([_tiles(i["cache_ssd_conv"]), _tiles(i["cache_lru_conv"])], 4)
    arrays = {
        "x": x.T.reshape(DT, P, TOK).transpose(1, 0, 2),
        "weights": _weights(i["w_in"], i["w_out"], i["w_up"], i["w_down"]),
        "params": _params(i),
        "consts": _consts(),
        "gla_state": _keyed(i["state_gla"]),
        "rwkv_state": _keyed(i["state_rwkv"].transpose(0, 1, 2, 4, 3)),
        "ssd_state": _keyed(i["state_ssd"]),
        "lru_state": i["state_lru"].reshape(L, DEC, 4, P).transpose(0, 3, 2, 1).reshape(L, P, 4 * DEC),
        "shift": i["cache_rwkv_shift"].reshape(L, DEC, RWKV_T, P).transpose(0, 3, 2, 1).reshape(L, P, RWKV_T * DEC),
        "conv": conv.transpose(0, 3, 2, 4, 1).reshape(L, P, 3 * 12 * DEC),
    }
    outs = {
        "y": (P, DT, TOK), "gla_p": (L, P, 256), "gla_s": (L, P, 2048), "lru": (L, P, 4, 9),
        "shift_out": (L, P, RWKV_T, 9), "rwkv_p": (L, P, 256), "rwkv_s": (L, P, 2048),
        "conv_p": (L, P, 12, 3), "conv_s": (L, P, 4, 12, DEC), "ssd_p": (L, P, 512), "ssd_s": (L, P, 4096),
    }
    nc = bacc.Bacc("TRN2", target_bir_lowering=False, num_devices=1)
    feed, aps = {}, {}
    for name, a in arrays.items():
        feed["in_" + name] = np.ascontiguousarray(a)
        aps[name] = nc.dram_tensor("in_" + name, a.shape, F32, kind="ExternalInput").ap()
    for name, shape in outs.items():
        aps[name] = nc.dram_tensor("out_" + name, shape, F32, kind="ExternalOutput").ap()
    aps["x_kept"] = nc.dram_tensor("x_kept", (P, DT, TOK), F32, kind="Internal").ap()
    build(nc, aps)
    r = run_bass_kernel_spmd(nc, [feed], core_ids=[0])
    o = {name: r.results[0]["out_" + name] for name in outs}

    def unkeyed(s, B, hp):
        s = s.reshape(L, 2, 64, B, hp, -1).transpose(0, 3, 4, 1, 2, 5)
        return np.ascontiguousarray(s.reshape(L, B, 2 * hp, 64, -1))

    y = o["y"].transpose(2, 1, 0).reshape(TOK, D_MODEL)
    lru = o["lru"].transpose(0, 3, 2, 1).reshape(L, 9, 512)
    shift = o["shift_out"].transpose(0, 3, 2, 1).reshape(L, 9, RWKV_T * P)
    conv_p = o["conv_p"].transpose(0, 3, 2, 1).reshape(L, 1, 3, 12 * P)
    conv_s = o["conv_s"].transpose(0, 4, 2, 3, 1).reshape(L, DEC, 4, 12 * P)[:, :, 1:]
    ssd_p = o["ssd_p"].reshape(L, 1, P, 8, 64).transpose(0, 1, 3, 4, 2)
    c = np.ascontiguousarray
    return (c(y[None, :SEQ]), c(y[SEQ:, None]),
            unkeyed(o["gla_p"], 1, 2), unkeyed(o["gla_s"], DEC, 2),
            c(lru[:, 0:1]), c(lru[:, 1:]),
            c(conv_p[..., 1024:]), c(conv_s[..., 1024:]),
            c(shift[:, 0:1]), c(shift[:, 1:]),
            c(unkeyed(o["rwkv_p"], 1, 4).swapaxes(3, 4)), c(unkeyed(o["rwkv_s"], DEC, 4).swapaxes(3, 4)),
            c(conv_p[..., :1024]), c(conv_s[..., :1024]),
            c(ssd_p), unkeyed(o["ssd_s"], DEC, 4))
```
